# Optimizing a Trainium2 kernel written in Bass

```python
import jax, jax.numpy as jnp
from jax import lax
import numpy as np

D_MODEL = 1024
BATCH = 1
SEQ = 1024
DEPTH = 1
DEC_BATCH = 1
DEC_SEQ = 32
PAST_LEN = 128

CHUNK = 64
Q_BLOCK = 128
RMS_EPS = 1e-6
NEG_INF = -1e30
MLA_HEADS = 8
QK_NOPE = 64
QK_ROPE = 32
QK_DIM = QK_NOPE + QK_ROPE
V_DIM = 64
Q_LORA = 256
KV_LORA = 128
ROPE_BASE = 10000.0
ATTN_SCALE = QK_DIM ** -0.5
RWKV_HEADS = 8
RWKV_HEAD = 64
RWKV_DIM = RWKV_HEADS * RWKV_HEAD
W_LORA = 64
A_LORA = 64
G_LORA = 128
LN_X_EPS = 64e-5
N_BRANCH = 2
BRANCH_DIM = 512
MLA_COLS = Q_LORA + KV_LORA + QK_ROPE
RWKV_COLS = 3 * RWKV_DIM + W_LORA + A_LORA + G_LORA
GATE_COLS = N_BRANCH * D_MODEL
IN_COLS = MLA_COLS + RWKV_COLS + GATE_COLS
N_GROUPS = 4
EXPERTS_PER_GROUP = 8
N_EXPERTS = N_GROUPS * EXPERTS_PER_GROUP
EXPERT_FF = 256
TOP_K = 2
MOE_BLOCK = 128

kernel_name = "hybrid_mla_rwkv7_hiermoe_stream_step"

def rmsnorm(x, g, eps=RMS_EPS):
    xf = x.astype(jnp.float32)
    xf = xf * lax.rsqrt(jnp.mean(xf * xf, axis=-1, keepdims=True) + eps)
    return (xf * g.astype(jnp.float32)).astype(x.dtype)

def rope(x, pos):
    half = QK_ROPE // 2
    inv = 1.0 / (ROPE_BASE ** (jnp.arange(half, dtype=jnp.float32) * (2.0 / QK_ROPE)))
    ang = pos.astype(jnp.float32)[:, None] * inv[None, :]
    ang = ang.reshape((ang.shape[0],) + (1,) * (x.ndim - 3) + (half,))
    cos, sin = jnp.cos(ang), jnp.sin(ang)
    xf = x.astype(jnp.float32)
    x1, x2 = xf[..., :half], xf[..., half:]
    return jnp.concatenate([x1 * cos - x2 * sin, x1 * sin + x2 * cos], axis=-1).astype(x.dtype)

def mla_queries(c_q, pos, q_norm_g, w_uq, q_head_norm_g):
    cq = rmsnorm(c_q, q_norm_g)
    q = jnp.einsum('blc,chd->blhd', cq, w_uq)
    q = jnp.concatenate([q[..., :QK_NOPE], rope(q[..., QK_NOPE:], pos)], axis=-1)
    return rmsnorm(q, q_head_norm_g)

def mla_keys_values(lat, kpe, w_ukv, k_head_norm_g):
    B, Lk, _ = lat.shape
    kv = jnp.einsum('blc,chd->blhd', lat, w_ukv)
    k_nope, v = kv[..., :QK_NOPE], kv[..., QK_NOPE:]
    k_rot = jnp.broadcast_to(kpe[:, :, None, :], (B, Lk, MLA_HEADS, QK_ROPE)).astype(k_nope.dtype)
    k = rmsnorm(jnp.concatenate([k_nope, k_rot], axis=-1), k_head_norm_g)
    return k, v

def chunk_causal_attention(q, k, v, q_pos, k_pos):
    s = jnp.einsum('bqhd,bkhd->bhqk', q.astype(jnp.float32), k.astype(jnp.float32)) * ATTN_SCALE
    visible = (k_pos[None, :] // CHUNK) <= (q_pos[:, None] // CHUNK)
    s = jnp.where(visible[None, None], s, NEG_INF)
    p = jax.nn.softmax(s, axis=-1)
    return jnp.einsum('bhqk,bkhd->bqhd', p, v.astype(jnp.float32)).astype(v.dtype)

def wkv7_scan(r, w, k, v, a, b, s0):
    def step(s, inp):
        r_t, w_t, k_t, v_t, a_t, b_t = inp
        sa = jnp.einsum('bhvk,bhk->bhv', s, a_t)
        s = s * w_t[:, :, None, :] + sa[..., None] * b_t[:, :, None, :] + v_t[..., None] * k_t[:, :, None, :]
        return s, jnp.einsum('bhvk,bhk->bhv', s, r_t)
    xs = tuple(jnp.moveaxis(t, 1, 0) for t in (r, w, k, v, a, b))
    s_final, ys = lax.scan(step, s0, xs)
    return jnp.moveaxis(ys, 0, 1), s_final

def rwkv7_time_mix(z, shift0, wkv0, mu, w0, w2, a0, a2, g2, k_k, k_a, r_k, lnx_g, lnx_b):
    B, L, _ = z.shape
    f32 = jnp.float32
    zf = z.astype(f32)
    prev = jnp.concatenate([shift0.astype(f32), zf[:, :-1]], axis=1)
    zm = zf + (prev - zf) * mu.astype(f32)
    r = zm[..., :RWKV_DIM]
    k = zm[..., RWKV_DIM:2 * RWKV_DIM]
    v = zm[..., 2 * RWKV_DIM:3 * RWKV_DIM]
    xw = zm[..., 3 * RWKV_DIM:3 * RWKV_DIM + W_LORA]
    xa = zm[..., 3 * RWKV_DIM + W_LORA:3 * RWKV_DIM + W_LORA + A_LORA]
    xg = zm[..., 3 * RWKV_DIM + W_LORA + A_LORA:]
    wlog = -jax.nn.softplus(-(w0.astype(f32) + jnp.tanh(xw) @ w2.astype(f32))) - 0.5
    decay = jnp.exp(-jnp.exp(wlog))
    a = jax.nn.sigmoid(a0.astype(f32) + xa @ a2.astype(f32))
    g = jax.nn.sigmoid(xg) @ g2.astype(f32)
    heads = lambda t: t.reshape(B, L, RWKV_HEADS, RWKV_HEAD)
    kk = heads(k * k_k.astype(f32))
    kk = kk * lax.rsqrt(jnp.maximum(jnp.sum(kk * kk, axis=-1, keepdims=True), 1e-24))
    k = k * (1.0 + (a - 1.0) * k_a.astype(f32))
    rh, kh, vh, ah = heads(r), heads(k), heads(v), heads(a)
    y, s_new = wkv7_scan(rh, heads(decay), kh, vh, -kk, kk * ah, wkv0.astype(f32))
    mean = jnp.mean(y, axis=-1, keepdims=True)
    var = jnp.mean(jnp.square(y - mean), axis=-1, keepdims=True)
    y = (y - mean) * lax.rsqrt(var + LN_X_EPS)
    y = y.reshape(B, L, RWKV_DIM) * lnx_g.astype(f32) + lnx_b.astype(f32)
    bonus = jnp.sum(rh * kh * r_k.astype(f32), axis=-1, keepdims=True) * vh
    out = (y + bonus.reshape(B, L, RWKV_DIM)) * g
    return out.astype(z.dtype), s_new.astype(wkv0.dtype), z[:, -1:]

def routed_expert_ffn(hf, expert_id, weight, w_gate, w_up, w_down):
    T = hf.shape[0]
    A = T * TOP_K
    flat_e = expert_id.reshape(A)
    flat_t = jnp.repeat(jnp.arange(T, dtype=jnp.int32), TOP_K)
    flat_w = weight.reshape(A).astype(hf.dtype)
    order = jnp.argsort(flat_e)
    se = flat_e[order]
    counts = jnp.zeros((N_EXPERTS,), jnp.int32).at[flat_e].add(1)
    pcounts = (counts + MOE_BLOCK - 1) // MOE_BLOCK * MOE_BLOCK
    pend = jnp.cumsum(pcounts)
    pstart = pend - pcounts
    start = jnp.cumsum(counts) - counts
    dest = pstart[se] + (jnp.arange(A, dtype=jnp.int32) - start[se])
    n_blocks = -(-A // MOE_BLOCK) + N_EXPERTS
    P = n_blocks * MOE_BLOCK
    row_tok = jnp.full((P,), T, jnp.int32).at[dest].set(flat_t[order])
    row_w = jnp.zeros((P,), hf.dtype).at[dest].set(flat_w[order])
    block_pos = jnp.arange(n_blocks, dtype=jnp.int32) * MOE_BLOCK
    block_e = jnp.minimum(jnp.searchsorted(pend, block_pos, side='right'), N_EXPERTS - 1)
    h_pad = jnp.concatenate([hf, jnp.zeros((1, hf.shape[1]), hf.dtype)], axis=0)
    xb = h_pad[row_tok].reshape(n_blocks, MOE_BLOCK, hf.shape[1])

    def run_block(args):
        xblk, e = args
        return (jax.nn.silu(xblk @ w_gate[e]) * (xblk @ w_up[e])) @ w_down[e]

    yb = lax.map(run_block, (xb, block_e)).reshape(P, hf.shape[1])
    y = jax.ops.segment_sum(yb * row_w[:, None], row_tok, num_segments=T + 1)
    return y[:T]

def hier_moe(h, w_rg, b_rg, w_re, b_re, w_eg, w_eu, w_ed):
    B, L, D = h.shape
    T = B * L
    hf = h.reshape(T, D)
    hf32 = hf.astype(jnp.float32)
    g_prob = jax.nn.softmax(hf32 @ w_rg.astype(jnp.float32) + b_rg.astype(jnp.float32), axis=-1)
    g_top, g_idx = lax.top_k(g_prob, 1)
    e_logits = jnp.einsum('td,dge->tge', hf32, w_re.astype(jnp.float32)) + b_re.astype(jnp.float32)
    e_in_group = e_logits[jnp.arange(T), g_idx[:, 0]]
    e_top, e_idx = lax.top_k(e_in_group, TOP_K)
    e_w = jax.nn.softmax(e_top, axis=-1) * g_top
    expert_id = g_idx * EXPERTS_PER_GROUP + e_idx
    return routed_expert_ffn(hf, expert_id, e_w, w_eg, w_eu, w_ed).reshape(B, L, D)

def layer_forward(x, pos, lat_past, kpe_past, wkv0, shift0,
                  norm_mix_g, w_in, q_norm_g, w_uq, kv_norm_g, w_ukv, q_head_norm_g, k_head_norm_g,
                  rwkv_mu, rwkv_w0, rwkv_w2, rwkv_a0, rwkv_a2, rwkv_g2, rwkv_k_k, rwkv_k_a, rwkv_r_k,
                  rwkv_lnx_g, rwkv_lnx_b, w_out, norm_ffn_g, w_router_group, b_router_group,
                  w_router_expert, b_router_expert, w_expert_gate, w_expert_up, w_expert_down):
    B, L, _ = x.shape
    h = rmsnorm(x, norm_mix_g)
    p = h @ w_in
    c_q = p[..., :Q_LORA]
    c_kv = p[..., Q_LORA:Q_LORA + KV_LORA]
    k_pe = p[..., Q_LORA + KV_LORA:MLA_COLS]
    z = p[..., MLA_COLS:MLA_COLS + RWKV_COLS]
    gate_logits = p[..., MLA_COLS + RWKV_COLS:]
    lat = rmsnorm(c_kv, kv_norm_g)
    kpe = rope(k_pe, pos)
    q = mla_queries(c_q, pos, q_norm_g, w_uq, q_head_norm_g)
    if lat_past is None:
        lat_all, kpe_all, k_pos = lat, kpe, pos
    else:
        lat_all = jnp.concatenate([lat_past.astype(lat.dtype), lat], axis=1)
        kpe_all = jnp.concatenate([kpe_past.astype(kpe.dtype), kpe], axis=1)
        k_pos = jnp.arange(lat_all.shape[1], dtype=jnp.int32)
    k, v = mla_keys_values(lat_all, kpe_all, w_ukv, k_head_norm_g)
    n_past = lat_all.shape[1] - L
    qb = min(Q_BLOCK, L)
    outs = []
    for s0 in range(0, L, qb):
        e0 = min(s0 + qb, L)
        kend = n_past + e0
        outs.append(chunk_causal_attention(q[:, s0:e0], k[:, :kend], v[:, :kend], pos[s0:e0], k_pos[:kend]))
    o_a = jnp.concatenate(outs, axis=1).reshape(B, L, BRANCH_DIM)
    o_b, wkv_new, shift_new = rwkv7_time_mix(z, shift0, wkv0, rwkv_mu, rwkv_w0, rwkv_w2, rwkv_a0, rwkv_a2,
                                             rwkv_g2, rwkv_k_k, rwkv_k_a, rwkv_r_k, rwkv_lnx_g, rwkv_lnx_b)
    branches = jnp.stack([o_a, o_b.astype(o_a.dtype)], axis=2)
    proj = jnp.einsum('blnc,ncd->blnd', branches, w_out)
    gates = jax.nn.sigmoid(gate_logits.astype(jnp.float32)).reshape(B, L, N_BRANCH, D_MODEL)
    x = x + jnp.sum(gates * proj.astype(jnp.float32), axis=2).astype(x.dtype)
    h2 = rmsnorm(x, norm_ffn_g)
    x = x + hier_moe(h2, w_router_group, b_router_group, w_router_expert, b_router_expert,
                     w_expert_gate, w_expert_up, w_expert_down)
    return x, lat, kpe, wkv_new, shift_new

def setup_inputs(seed: int = 0) -> dict:
    key = jax.random.key(seed)
    ks = iter(jax.random.split(key, 40))
    nrm = lambda shape, scale: jax.random.normal(next(ks), shape, jnp.float32) * scale
    gain = lambda shape: 1.0 + nrm(shape, 0.02)
    D = D_MODEL
    return {
        "x_prompt": nrm((BATCH, SEQ, D), 1.0),
        "x_sample": nrm((DEC_BATCH, DEC_SEQ, D), 1.0),
        "cache_kv_latent": nrm((DEPTH, DEC_BATCH, PAST_LEN, KV_LORA), 1.0),
        "cache_k_rope": nrm((DEPTH, DEC_BATCH, PAST_LEN, QK_ROPE), 1.0),
        "state_wkv": nrm((DEPTH, DEC_BATCH, RWKV_HEADS, RWKV_HEAD, RWKV_HEAD), 0.5),
        "state_shift": nrm((DEPTH, DEC_BATCH, 1, RWKV_COLS), 1.0),
        "norm_mix_g": gain((DEPTH, D)),
        "w_in": nrm((DEPTH, D, IN_COLS), D ** -0.5),
        "q_norm_g": gain((DEPTH, Q_LORA)),
        "w_uq": nrm((DEPTH, Q_LORA, MLA_HEADS, QK_DIM), Q_LORA ** -0.5),
        "kv_norm_g": gain((DEPTH, KV_LORA)),
        "w_ukv": nrm((DEPTH, KV_LORA, MLA_HEADS, QK_NOPE + V_DIM), KV_LORA ** -0.5),
        "q_head_norm_g": gain((DEPTH, QK_DIM)),
        "k_head_norm_g": gain((DEPTH, QK_DIM)),
        "rwkv_mu": jax.random.uniform(next(ks), (DEPTH, RWKV_COLS), jnp.float32),
        "rwkv_w0": jax.random.uniform(next(ks), (DEPTH, RWKV_DIM), jnp.float32, -5.0, 1.0),
        "rwkv_w2": nrm((DEPTH, W_LORA, RWKV_DIM), 0.5 * W_LORA ** -0.5),
        "rwkv_a0": nrm((DEPTH, RWKV_DIM), 0.1),
        "rwkv_a2": nrm((DEPTH, A_LORA, RWKV_DIM), A_LORA ** -0.5),
        "rwkv_g2": nrm((DEPTH, G_LORA, RWKV_DIM), G_LORA ** -0.5),
        "rwkv_k_k": 0.85 + nrm((DEPTH, RWKV_DIM), 0.05),
        "rwkv_k_a": 1.0 + nrm((DEPTH, RWKV_DIM), 0.05),
        "rwkv_r_k": nrm((DEPTH, RWKV_HEADS, RWKV_HEAD), 0.1),
        "rwkv_lnx_g": gain((DEPTH, RWKV_DIM)),
        "rwkv_lnx_b": nrm((DEPTH, RWKV_DIM), 0.02),
        "w_out": nrm((DEPTH, N_BRANCH, BRANCH_DIM, D), BRANCH_DIM ** -0.5),
        "norm_ffn_g": gain((DEPTH, D)),
        "w_router_group": nrm((DEPTH, D, N_GROUPS), D ** -0.5),
        "b_router_group": nrm((DEPTH, N_GROUPS), 0.01),
        "w_router_expert": nrm((DEPTH, D, N_GROUPS, EXPERTS_PER_GROUP), D ** -0.5),
        "b_router_expert": nrm((DEPTH, N_GROUPS, EXPERTS_PER_GROUP), 0.01),
        "w_expert_gate": nrm((DEPTH, N_EXPERTS, D, EXPERT_FF), D ** -0.5),
        "w_expert_up": nrm((DEPTH, N_EXPERTS, D, EXPERT_FF), D ** -0.5),
        "w_expert_down": nrm((DEPTH, N_EXPERTS, EXPERT_FF, D), EXPERT_FF ** -0.5),
    }

def reference(x_prompt, x_sample, cache_kv_latent, cache_k_rope, state_wkv, state_shift,
              norm_mix_g, w_in, q_norm_g, w_uq, kv_norm_g, w_ukv, q_head_norm_g, k_head_norm_g,
              rwkv_mu, rwkv_w0, rwkv_w2, rwkv_a0, rwkv_a2, rwkv_g2, rwkv_k_k, rwkv_k_a, rwkv_r_k,
              rwkv_lnx_g, rwkv_lnx_b, w_out, norm_ffn_g, w_router_group, b_router_group,
              w_router_expert, b_router_expert, w_expert_gate, w_expert_up, w_expert_down):
    weights = (norm_mix_g, w_in, q_norm_g, w_uq, kv_norm_g, w_ukv, q_head_norm_g, k_head_norm_g,
               rwkv_mu, rwkv_w0, rwkv_w2, rwkv_a0, rwkv_a2, rwkv_g2, rwkv_k_k, rwkv_k_a, rwkv_r_k,
               rwkv_lnx_g, rwkv_lnx_b, w_out, norm_ffn_g, w_router_group, b_router_group,
               w_router_expert, b_router_expert, w_expert_gate, w_expert_up, w_expert_down)
    bp = x_prompt.shape[0]
    pos_p = jnp.arange(x_prompt.shape[1], dtype=jnp.int32)
    pos_s = cache_kv_latent.shape[2] + jnp.arange(x_sample.shape[1], dtype=jnp.int32)
    wkv_zero = jnp.zeros((bp, RWKV_HEADS, RWKV_HEAD, RWKV_HEAD), x_prompt.dtype)
    shift_zero = jnp.zeros((bp, 1, RWKV_COLS), x_prompt.dtype)
    xp, xs = x_prompt, x_sample
    lat_p, kpe_p, wkv_p, sh_p = [], [], [], []
    lat_s, kpe_s, wkv_s, sh_s = [], [], [], []
    for l in range(DEPTH):
        lw = tuple(wt[l] for wt in weights)
        xp, a1, a2, a3, a4 = layer_forward(xp, pos_p, None, None, wkv_zero, shift_zero, *lw)
        xs, b1, b2, b3, b4 = layer_forward(xs, pos_s, cache_kv_latent[l], cache_k_rope[l],
                                           state_wkv[l], state_shift[l], *lw)
        lat_p.append(a1); kpe_p.append(a2); wkv_p.append(a3); sh_p.append(a4)
        lat_s.append(b1); kpe_s.append(b2); wkv_s.append(b3); sh_s.append(b4)
    return (xp, xs,
            jnp.stack(lat_p, 0), jnp.stack(kpe_p, 0), jnp.stack(wkv_p, 0), jnp.stack(sh_p, 0),
            jnp.stack(lat_s, 0), jnp.stack(kpe_s, 0), jnp.stack(wkv_s, 0), jnp.stack(sh_s, 0))


_drawn_inputs = setup_inputs


def setup_inputs(seed=0):
    import zlib

    import numpy as np

    out = dict(_drawn_inputs(seed))
    spreads = {}
    factors = {'q_norm_g': 8.0,
     'q_head_norm_g': 7.953,
     'k_head_norm_g': 8.0,
     'rwkv_lnx_g': 10.021,
     'rwkv_lnx_b': 9.382,
     'b_router_group': 51.238,
     'b_router_expert': 5.629,
     'norm_ffn_g': 2.685}
    for name, (base, spread) in spreads.items():
        noise = np.random.default_rng([zlib.crc32(name.encode()), seed]).standard_normal(out[name].shape)
        drawn = base * np.exp(spread * noise) if base else spread * noise
        out[name] = __import__('jax').numpy.asarray(drawn.astype(out[name].dtype))
    for name, factor in factors.items():
        out[name] = (out[name] * factor).astype(out[name].dtype)
    return out
```

```python
import math
from contextlib import ExitStack

import concourse.bass as bass
from concourse import mybir

F32 = mybir.dt.float32
I32 = mybir.dt.int32
U32 = mybir.dt.uint32
ALU = mybir.AluOpType
ACT = mybir.ActivationFunctionType
AX = mybir.AxisListType.X

P = 128
D = 1024
DC = D // P
SEQ, DEC, PAST = 1024, 32, 128
NPT = SEQ // P
NT = NPT + 1
PAST_TILE = NT
EPS = 1e-6
H, NOPE, ROPE, VD = 8, 64, 32, 64
HALF = ROPE // 2
QK = NOPE + ROPE
QL, KL = 256, 128
MLA = QL + KL + ROPE
NEG = -1e30
HB = H // 2
RD, RH = 512, 64
ZC = 1792
ZT = ZC // P
W_LORA = 64
PAIRS = RD // P
KAPPA = 0.6065306597126334
CENTRE = 38.0
GN_EPS = 64e-5
NG, EPG, NE, FF = 4, 8, 32, 256
RT = NG + NE
CAP = P
OVERFLOW = 2 * (SEQ + DEC) // CAP
SLOTS = (NE + OVERFLOW) * CAP
DUMMY = 2 * P
BIG = 3.0e38


POOL_QUEUE = ("past_in", "h_stored", "lat_stored", "v_stored", "qk_stored", "ob_stored", "state_in")


class InOrder:

    def __init__(self, eng, sem):
        self.eng, self.sem, self.n = eng, sem, 0

    def __call__(self, ins):
        self.n += 1
        ins.then_inc(self.sem, 1)
        self.eng.wait_ge(self.sem, self.n)

    def lap(self):
        self.eng.sem_clear(self.sem)
        self.n = 0


def at(x, t):
    s = x[bass.ds(t, 1)]
    names = "bcdef"[:len(s.shape) - 2]
    return s.rearrange("o a " + " ".join(names) + " -> (o a) " + " ".join(names))


def goes_on(pool, sem):
    pool.sem_inc(sem, 1)


def give_back(nc, sems):
    with nc.Block() as block:
        @block.sync
        def _(sp):
            for s in sems:
                sp.sem_clear(s)


def spread(ap, shape):
    return ap.broadcast_to(shape)


def tiles(eng, body, first, last):
    with eng.Fori(0, first) as t:
        body(t, False)
    for t in range(first, last):
        body(t, True)


def latents(nc, io):
    with ExitStack() as c:
        sb = lambda n, s: c.enter_context(nc.sbuf_tensor("a_" + n, s, F32))
        sems = []

        def sem(n):
            if n in POOL_QUEUE:
                return io["hold"].enter_context(nc.semaphore("a_" + n))
            sems.append(c.enter_context(nc.semaphore("a_" + n)))
            return sems[-1]

        banks = [c.enter_context(nc.psum_tensor(f"a_ps{i}", [P, 512], F32)) for i in range(8)]
        w = sb("w", [P, DC, MLA])
        wq = sb("wq", [P, 2, H * QK])
        wkv = sb("wkv", [P, H * P])
        ident = sb("ident", [P, P])
        ones = sb("ones", [P, P])
        g_mix = sb("g_mix", [P, DC])
        g_lat = sb("g_lat", [P, QL + KL])
        g_head = sb("g_head", [P, 2, QK])
        xT = sb("xT", [P, DC, P])
        sq = sb("sq", [P, DC, P])
        hT = sb("hT", [P, DC, P])
        rb = sb("rb", [P, P])
        trig = sb("trig", [P, ROPE])
        p1 = sb("p1", [P, MLA])
        p1sq = sb("p1sq", [P, QL])
        ms = sb("ms", [P, 2])
        cn = sb("cn", [P, QL + KL])
        kpe = sb("kpe", [P, ROPE])
        rt = sb("rt", [P, 4, H, HALF])
        rk = sb("rk", [P, 4, HALF])
        cT = sb("cT", [P, 3, P])
        qk = sb("qk", [P, 2 * H, QK])
        qksq = sb("qksq", [P, 2 * H, QK])
        hms = sb("hms", [P, 2 * H])
        v = sb("v", [P, H, VD])
        qkT = sb("qkT", [QK, 2 * H, P])
        consts_in, x_in, trig_in, past_in = sem("consts_in"), sem("x_in"), sem("trig_in"), sem("past_in")
        ones_set, dve_step, act_step = sem("ones_set"), sem("dve_step"), sem("act_step")
        sq_ready, ssq_done, ms_ready, rms_root, xg_done, h_ready = (sem(n) for n in (
            "sq_ready", "ssq_done", "ms_ready", "rms_root", "xg_done", "h_ready"))
        p1_done, p1_copied, lat_ss, lat_ms, lat_root, c_ready = (sem(n) for n in (
            "p1_done", "p1_copied", "lat_ss", "lat_ms", "lat_root", "c_ready"))
        cT_done, cT_copied, qkv_done, qkv_copied, head_ms, head_root, qk_ready = (sem(n) for n in (
            "cT_done", "cT_copied", "qkv_done", "qkv_copied", "head_ms", "head_root", "qk_ready"))
        qkT_done, qkT_copied = sem("qkT_done"), sem("qkT_copied")
        h_stored, lat_stored, v_stored, qk_stored = sem("h_stored"), sem("lat_stored"), sem("v_stored"), sem("qk_stored")
        NTILE = NT + 1
        pool_on = sem("pool_on")
        c.callback(give_back, nc, sems)
        block = c.enter_context(nc.Block())

        @block.sync
        def _(sp):
            for dst, src in ((w[:], io["w_mla"]), (wq[:], io["w_uq"]), (wkv[:], io["w_ukv"]),
                             (ident[:], io["ident"]), (g_mix[:], io["norm_mix_g"]),
                             (g_lat[:, 0:QL], io["q_norm_g"].partition_broadcast(P)),
                             (g_lat[:, QL:], io["kv_norm_g"].partition_broadcast(P)),
                             (g_head[:, 0, :], io["q_head_norm_g"].partition_broadcast(P)),
                             (g_head[:, 1, :], io["k_head_norm_g"].partition_broadcast(P))):
                sp.dma_start(dst, src).then_inc(consts_in, 16)

            def loads(t, _):
                sp.wait_ge(xg_done, t)
                sp.dma_start(xT[:], at(io["xT"], t)).then_inc(x_in, 16)
                sp.wait_ge(qk_ready, t)
                sp.dma_start(trig[:], at(io["trig"], t)).then_inc(trig_in, 16)

            with sp.Fori(0, NT) as t:
                loads(t, False)
            loads(NT, True)

        @block.gpsimd
        def _(pool):
            pool.memset(ones[:], 1.0).then_inc(ones_set, 1)

            def stores(t, last):
                pool.wait_ge(h_ready, t + 1)
                goes_on(pool, pool_on)
                pool.dma_start(at(io["hT_d"], t), hT[:]).then_inc(h_stored, 16)
                if last and t == PAST_TILE:
                    pool.wait_ge(cT_done, t)
                    pool.wait_ge(lat_stored, 32 * t)
                    pool.wait_ge(qk_ready, t)
                    goes_on(pool, pool_on)
                    pool.dma_start(cn[:, QL:], io["past_lat"]).then_inc(past_in, 16)
                    pool.dma_start(kpe[:], io["past_kpe"]).then_inc(past_in, 16)
                else:
                    pool.wait_ge(c_ready, t + 1)
                    goes_on(pool, pool_on)
                    pool.dma_start(at(io["lat"], t), cn[:, QL:]).then_inc(lat_stored, 16)
                    pool.dma_start(at(io["kpe"], t), kpe[:]).then_inc(lat_stored, 16)
                pool.wait_ge(qkv_copied, t + 1)
                goes_on(pool, pool_on)
                pool.dma_start(at(io["v_d"], t), v[:]).then_inc(v_stored, 16)
                pool.wait_ge(qkT_copied, 4 * (t + 1))
                goes_on(pool, pool_on)
                pool.dma_start(at(io["qT_d"], t), qkT[:, 0:H, :]).then_inc(qk_stored, 16)
                pool.dma_start(at(io["kT_d"], t), qkT[:, H:, :]).then_inc(qk_stored, 16)

            tiles(pool, stores, NPT, NTILE)
            pool.wait_ge(h_stored, 16 * NTILE)
            pool.wait_ge(lat_stored, 32 * NT)
            pool.wait_ge(v_stored, 16 * NTILE)
            pool.wait_ge(qk_stored, 32 * NTILE)

        @block.vector
        def _(dve):
            step = InOrder(dve, dve_step)
            dve.wait_ge(consts_in, 16 * 9)
            dve.wait_ge(ones_set, 1)
            step(dve.tensor_scalar(g_head[:, 0, :], g_head[:, 0, :], QK ** -0.5, None, ALU.mult))
            step.lap()

            def body(t, last):
                past = last and t == PAST_TILE
                dve.wait_ge(x_in, 16 * (t + 1))
                dve.wait_ge(ssq_done, t)
                dve.tensor_tensor(sq[:], xT[:], xT[:], ALU.mult).then_inc(sq_ready, 1)
                dve.wait_ge(p1_done, t)
                dve.wait_ge(h_stored, 16 * t)
                dve.tensor_tensor(hT[:], xT[:], spread(g_mix[:].unsqueeze(2), [P, DC, P]),
                                  ALU.mult).then_inc(xg_done, 1)
                dve.wait_ge(ssq_done, t + 1)
                dve.tensor_scalar(rb[:], banks[0][:, 0:P], 1.0 / D, EPS, ALU.mult, ALU.add).then_inc(ms_ready, 1)
                dve.wait_ge(rms_root, t + 1)
                step(dve.reciprocal(rb[:], rb[:]))
                dve.wait_ge(xg_done, t + 1)
                dve.tensor_tensor(hT[:], hT[:], spread(rb[:].unsqueeze(1), [P, DC, P]),
                                  ALU.mult).then_inc(h_ready, 1)
                dve.wait_ge(lat_ss, 2 * (t + 1))
                step(dve.tensor_scalar(ms[:, 0:1], ms[:, 0:1], 1.0 / QL, EPS, ALU.mult, ALU.add))
                dve.tensor_scalar(ms[:, 1:2], ms[:, 1:2], 1.0 / KL, EPS, ALU.mult, ALU.add).then_inc(lat_ms, 1)
                dve.wait_ge(lat_root, t + 1)
                step(dve.reciprocal(ms[:], ms[:]))
                dve.wait_ge(cT_done, t)
                dve.wait_ge(trig_in, 16 * (t + 1))
                cos, sin = trig[:, 0:HALF], trig[:, HALF:]
                if past:
                    step(dve.scalar_tensor_tensor(cn[:, 0:QL], p1[:, 0:QL], ms[:, 0:1], g_lat[:, 0:QL], ALU.mult, ALU.mult))
                    dve.wait_ge(past_in, 32)
                    step(dve.tensor_copy(rk[:, 0, :], cos))
                else:
                    dve.wait_ge(lat_stored, 32 * t)
                    dve.scalar_tensor_tensor(cn[:, 0:QL], p1[:, 0:QL], ms[:, 0:1], g_lat[:, 0:QL], ALU.mult, ALU.mult)
                    step(dve.scalar_tensor_tensor(cn[:, QL:], p1[:, QL:QL + KL], ms[:, 1:2], g_lat[:, QL:], ALU.mult, ALU.mult))
                    x1, x2 = p1[:, QL + KL:QL + KL + HALF], p1[:, QL + KL + HALF:]
                    for n, (a, b) in enumerate(((x1, cos), (x2, sin), (x1, sin), (x2, cos))):
                        step(dve.tensor_tensor(rk[:, n, :], a, b, ALU.mult))
                    step(dve.tensor_tensor(kpe[:, 0:HALF], rk[:, 0, :], rk[:, 1, :], ALU.subtract))
                    step(dve.tensor_tensor(kpe[:, HALF:], rk[:, 2, :], rk[:, 3, :], ALU.add))
                dve.tensor_copy(rk[:, 0, :], cos).then_inc(c_ready, 1)
                dve.wait_ge(qkv_copied, t + 1)
                step(dve.tensor_copy(qk[:, H:, NOPE:], spread(kpe[:].unsqueeze(1), [P, H, ROPE])))
                cos8, sin8 = (spread(a.unsqueeze(1), [P, H, HALF]) for a in (cos, sin))
                x1, x2 = qk[:, 0:H, NOPE:NOPE + HALF], qk[:, 0:H, NOPE + HALF:]
                for n, (a, b) in enumerate(((x1, cos8), (x2, sin8), (x1, sin8), (x2, cos8))):
                    step(dve.tensor_tensor(rt[:, n], a, b, ALU.mult))
                step(dve.tensor_tensor(x1, rt[:, 0], rt[:, 1], ALU.subtract))
                step(dve.tensor_tensor(x2, rt[:, 2], rt[:, 3], ALU.add))
                step(dve.tensor_tensor(qksq[:], qk[:], qk[:], ALU.mult))
                step(dve.tensor_reduce(hms[:], qksq[:], AX, ALU.add))
                dve.tensor_scalar(hms[:], hms[:], 1.0 / QK, EPS, ALU.mult, ALU.add).then_inc(head_ms, 1)
                dve.wait_ge(head_root, t + 1)
                step(dve.reciprocal(hms[:], hms[:]))
                step(dve.tensor_tensor(qksq[:], qk[:], spread(hms[:].unsqueeze(2), [P, 2 * H, QK]), ALU.mult))
                step(dve.tensor_tensor(qk[:, 0:H], qksq[:, 0:H], spread(g_head[:, 0:1], [P, H, QK]), ALU.mult))
                step.lap()
                dve.tensor_tensor(qk[:, H:], qksq[:, H:], spread(g_head[:, 1:2], [P, H, QK]),
                                  ALU.mult).then_inc(qk_ready, 1)

            tiles(dve, body, NPT, NTILE)

        @block.scalar
        def _(act):
            step = InOrder(act, act_step)

            def body(t, _):
                act.wait_ge(ms_ready, t + 1)
                act.activation(rb[:], rb[:], ACT.Sqrt).then_inc(rms_root, 1)
                act.wait_ge(p1_done, t + 1)
                act.wait_ge(c_ready, t)
                act.activation(p1[:], banks[1][:, 0:MLA], ACT.Copy).then_inc(p1_copied, 1)
                act.wait_ge(p1_copied, t + 1)
                act.wait_ge(lat_ss, 2 * t)
                act.activation(p1sq[:], p1[:, 0:QL], ACT.Square, accum_out=ms[:, 0:1]).then_inc(lat_ss, 1)
                act.wait_ge(lat_ss, 2 * t + 1)
                act.activation(p1sq[:, 0:KL], p1[:, QL:QL + KL], ACT.Square, accum_out=ms[:, 1:2]).then_inc(lat_ss, 1)
                act.wait_ge(lat_ms, t + 1)
                act.activation(ms[:], ms[:], ACT.Sqrt).then_inc(lat_root, 1)
                act.wait_ge(cT_done, t + 1)
                act.activation(cT[:], banks[2][:, 0:3 * P], ACT.Copy).then_inc(cT_copied, 1)
                act.wait_ge(qkv_done, t + 1)
                act.wait_ge(qkT_done, 4 * t)
                act.wait_ge(v_stored, 16 * t)
                for n in range(2):
                    heads = slice(HB * n, HB * n + HB)
                    act.activation(qk[:, heads, :], banks[3 + n][:, 0:HB * QK], ACT.Copy)
                    kv = banks[5 + n][:].rearrange("p (h d) -> p h d", h=HB)
                    act.activation(qk[:, H + HB * n:H + HB * n + HB, 0:NOPE], kv[:, :, 0:NOPE], ACT.Copy)
                    step(act.activation(v[:, heads, :], kv[:, :, NOPE:], ACT.Copy))
                act.sem_inc(qkv_copied, 1)
                act.wait_ge(head_ms, t + 1)
                act.activation(hms[:], hms[:], ACT.Sqrt).then_inc(head_root, 1)
                act.wait_ge(qk_stored, 32 * t)
                for n, b in enumerate((7, 2, 3, 4)):
                    act.wait_ge(qkT_done, 4 * t + n + 1)
                    act.activation(qkT[:, 4 * n:4 * n + 4, :], banks[b][0:QK, :], ACT.Copy).then_inc(qkT_copied, 1)
                step.lap()

            tiles(act, body, NPT, NTILE)

        @block.tensor
        def _(pe):
            pe.wait_ge(consts_in, 16 * 9)
            pe.wait_ge(ones_set, 1)

            def body(t, _):
                pe.wait_ge(sq_ready, t + 1)
                pe.wait_ge(ms_ready, t)
                for k in range(DC):
                    mm = pe.matmul(banks[0][:, 0:P], ones[:], sq[:, k, :], start=(k == 0), stop=(k == DC - 1))
                mm.then_inc(ssq_done, 1)
                pe.wait_ge(h_ready, t + 1)
                pe.wait_ge(p1_copied, t)
                for k in range(DC):
                    mm = pe.matmul(banks[1][:, 0:MLA], hT[:, k, :], w[:, k, :], start=(k == 0), stop=(k == DC - 1))
                mm.then_inc(p1_done, 1)
                pe.wait_ge(c_ready, t + 1)
                pe.wait_ge(qkT_copied, 4 * t)
                for n in range(3):
                    mm = pe.transpose(banks[2][:, n * P:(n + 1) * P], cn[:, n * P:(n + 1) * P], ident[:])
                mm.then_inc(cT_done, 1)
                pe.wait_ge(cT_copied, t + 1)
                pe.wait_ge(qkv_copied, t)
                for n in range(2):
                    for k in range(2):
                        pe.matmul(banks[3 + n][:, 0:HB * QK], cT[:, k, :], wq[:, k, n * HB * QK:(n + 1) * HB * QK],
                                  start=(k == 0), stop=(k == 1))
                    mm = pe.matmul(banks[5 + n][:], cT[:, 2, :], wkv[:, n * 512:(n + 1) * 512], start=True, stop=True)
                mm.then_inc(qkv_done, 1)
                pe.wait_ge(qk_ready, t + 1)
                for n, b in enumerate((7, 2, 3, 4)):
                    for j in range(4):
                        mm = pe.transpose(banks[b][0:QK, j * P:(j + 1) * P], qk[:, 4 * n + j, :], ident[:])
                    mm.then_inc(qkT_done, 1)

            tiles(pe, body, NPT, NTILE)


def mixing(nc, io):
    LEVELS = (2, 4, 8, 16, 32, 64)
    with ExitStack() as c:
        sb = lambda n, s: c.enter_context(nc.sbuf_tensor("b_" + n, s, F32))
        sems = []

        def sem(n):
            if n in POOL_QUEUE:
                return io["hold"].enter_context(nc.semaphore("b_" + n))
            sems.append(c.enter_context(nc.semaphore("b_" + n)))
            return sems[-1]

        banks = [c.enter_context(nc.psum_tensor(f"b_ps{i}", [P, 512], F32)) for i in range(8)]
        wz = sb("wz", [P, DC, ZC])
        wa2 = sb("wa2", [P, RD])
        g2 = sb("g2", [P, RD])
        ident = sb("ident", [P, P])
        vecs = sb("vecs", [P, ZT + 5 * PAIRS])
        mu = vecs[:, 0:ZT]
        w0, a0, k_k, k_a, r_k = (vecs[:, ZT + PAIRS * n:ZT + PAIRS * (n + 1)] for n in range(5))
        ln = sb("ln", [P, 2, RD])
        same_head = sb("same_head", [P, P])
        causal = sb("causal", [P, 2 * P])
        first = sb("first", [P, 2, P])
        merge_mask = sb("merge_mask", [P, len(LEVELS), P // 2])
        hT = sb("hT", [P, DC, P])
        z = sb("z", [P, ZT, P + 1])
        zlast = sb("zlast", [P, ZT])
        zm = sb("zm", [P, ZT, P])
        la = sb("la", [P, P])
        sg = sb("sg", [P, P])
        kk = sb("kk", [P, PAIRS, P])
        kn = sb("kn", [P, PAIRS, P])
        sig = sb("sig", [P, PAIRS, P])
        av = sb("av", [P, PAIRS, P])
        cs = sb("cs", [P, PAIRS, P])
        csm = sb("csm", [P, PAIRS, P])
        one = sb("one", [P, P])
        bias = sb("bias", [P, 2])
        eW = sb("eW", [P, PAIRS, P])
        wc = sb("wc", [P, PAIRS])
        k2 = sb("k2", [P, PAIRS, P])
        art = sb("art", [P, PAIRS, 2 * P])
        bt = sb("bt", [P, PAIRS, P])
        kt = sb("kt", [P, PAIRS, P])
        rkk = kn
        tok = sb("tok", [P, 3, RD])
        bon = sb("bon", [P, H])
        gs = sb("gs", [P, RD])
        M = sb("M", [P, H, 2, 2 * P])
        T = sb("T", [P, H, P])
        U = sb("U", [P, H, P])
        L = [sb(f"L{n}", [P, H, P]) for n in range(len(LEVELS))]
        X = sb("X", [P, RD])
        W = sb("W", [P, RD])
        S = sb("S", [P, PAIRS, P])
        y = sb("y", [P, H, RH])
        st = sb("st", [P, 2, H])
        sout = csm
        (consts_in, h_in, set_done, carry_set, z_done, z_copied, zm_ready, lora_in, kk_sq, lora_done, gate_copied,
         w_sum, w_sig, a_sum, a_sig, nn_done, nn_ready, nn_root, cs_ready, e_ready, feats_ready, tok_done, tok_copied,
         gram_done, gram_copied, T_ready, low_done, low_copied, merge_done, merged, x_done, x_copied, w_done, w_copied,
         y_done, y_copied, d_done, s_ready, v_ready, v_root, out_ready, ob_stored, dve_step, act_step, state_out,
         state_in, e_used) = (
            sem(n) for n in (
                "consts_in h_in set_done carry_set z_done z_copied zm_ready lora_in kk_sq lora_done gate_copied "
                "w_sum w_sig a_sum a_sig nn_done nn_ready nn_root cs_ready e_ready feats_ready tok_done tok_copied "
                "gram_done gram_copied T_ready low_done low_copied merge_done merged x_done x_copied w_done w_copied "
                "y_done y_copied d_done s_ready v_ready v_root out_ready ob_stored dve_step act_step state_out "
                "state_in e_used").split())
        NL = len(LEVELS)
        pool_on = sem("pool_on")
        c.callback(give_back, nc, sems)
        block = c.enter_context(nc.Block())

        @block.sync
        def _(sp):
            loads = ((wz[:], io["w_z"]), (wa2[:], io["wa2"]), (g2[:], io["g2"]), (ident[:], io["ident"]),
                     (vecs[:], io["vecs"]), (ln[:, 0, :], io["rwkv_lnx_g"].partition_broadcast(P)),
                     (ln[:, 1, :], io["rwkv_lnx_b"].partition_broadcast(P)), (same_head[:], io["same_head"]),
                     (causal[:], io["causal"]), (first[:], io["first"]), (merge_mask[:], io["merge_mask"]))
            for dst, src in loads:
                sp.dma_start(dst, src).then_inc(consts_in, 16)

            def body(t, _):
                sp.wait_ge(z_done, t)
                sp.dma_start(hT[:], at(io["hT_d"], t)).then_inc(h_in, 16)

            tiles(sp, body, NPT, NT)

        @block.gpsimd
        def _(pool):
            for n in range(NL):
                pool.memset(L[n][:], 0.0)
            pool.memset(one[:], 1.0)
            pool.memset(bias[:, 0:1], CENTRE)
            pool.memset(bias[:, 1:2], -CENTRE)
            pool.memset(z[:, :, P:], 0.0)
            pool.memset(S[:], 0.0).then_inc(set_done, 1)

            def body(t, last):
                if last:
                    pool.wait_ge(state_out, 1)
                    goes_on(pool, pool_on)
                    pool.dma_start(io["shift"][0], zlast[:]).then_inc(ob_stored, 16)
                    pool.dma_start(io["wkv"][0], sout[:]).then_inc(ob_stored, 16)
                    pool.wait_ge(ob_stored, 16 * NPT + 32)
                    goes_on(pool, pool_on)
                    pool.dma_start(zlast[:], io["shift0"]).then_inc(state_in, 16)
                    pool.dma_start(S[:], io["wkv0"]).then_inc(state_in, 16)
                pool.wait_ge(out_ready, t + 1)
                goes_on(pool, pool_on)
                pool.dma_start(at(io["ob_d"], t), y[:]).then_inc(ob_stored, 16)

            tiles(pool, body, NPT, NT)
            pool.wait_ge(state_out, 2)
            goes_on(pool, pool_on)
            pool.dma_start(io["shift"][1], zlast[:]).then_inc(ob_stored, 16)
            pool.dma_start(io["wkv"][1], sout[:]).then_inc(ob_stored, 16)
            pool.wait_ge(ob_stored, 16 * NT + 64)

        @block.vector
        def _(dve):
            step = InOrder(dve, dve_step)
            dve.wait_ge(consts_in, 16 * 11)
            dve.wait_ge(set_done, 1)
            col = lambda a, n: spread(a.unsqueeze(2), [P, n, P])

            def body(t, last):
                nv = DEC if last else P
                if last:
                    dve.wait_ge(s_ready, t)
                    step(dve.tensor_copy(zlast[:], z[:, :, P]))
                    dve.tensor_scalar(sout[:], S[:], float(math.exp(CENTRE)), None, ALU.mult).then_inc(state_out, 1)
                    dve.wait_ge(state_in, 32)
                    step(dve.tensor_scalar(S[:], S[:], float(math.exp(-CENTRE)), None, ALU.mult))
                    dve.tensor_copy(z[:, :, 0], zlast[:]).then_inc(carry_set, 1)
                else:
                    dve.tensor_copy(z[:, :, 0:1], z[:, :, P:]).then_inc(carry_set, 1)
                dve.wait_ge(z_copied, 4 * (t + 1))
                here = z[:, :, 1:]
                step(dve.tensor_tensor(zm[:], z[:, :, 0:P], here, ALU.subtract))
                step(dve.tensor_tensor(zm[:], zm[:], col(mu, ZT), ALU.mult))
                dve.tensor_tensor(zm[:], zm[:], here, ALU.add).then_inc(zm_ready, 1)
                dve.wait_ge(zm_ready, t + 1)
                r, k = zm[:, 0:PAIRS], zm[:, PAIRS:2 * PAIRS]
                step(dve.tensor_tensor(kk[:], k, col(k_k, PAIRS), ALU.mult))
                dve.tensor_tensor(kn[:], kk[:], kk[:], ALU.mult).then_inc(kk_sq, 1)
                dve.wait_ge(lora_done, t + 1)
                dve.tensor_tensor(sig[:], banks[4][:].rearrange("p (a b) -> p a b", a=PAIRS), col(w0, PAIRS),
                                  ALU.add).then_inc(w_sum, 1)
                dve.tensor_tensor(av[:], banks[5][:].rearrange("p (a b) -> p a b", a=PAIRS), col(a0, PAIRS),
                                  ALU.add).then_inc(a_sum, 1)
                dve.wait_ge(nn_done, t + 1)
                dve.tensor_scalar(kn[:], banks[7][:].rearrange("p (a b) -> p a b", a=PAIRS), 1e-24, None,
                                  ALU.max).then_inc(nn_ready, 1)
                dve.wait_ge(w_sig, t + 1)
                for p in range(PAIRS):
                    step(dve.tensor_tensor_scan(cs[:, p, :], one[:], sig[:, p, :], 0.0, ALU.mult, ALU.add))
                dve.tensor_tensor(csm[:], cs[:], sig[:], ALU.subtract).then_inc(cs_ready, 1)
                dve.wait_ge(nn_root, t + 1)
                step(dve.reciprocal(kn[:], kn[:]))
                step(dve.tensor_tensor(kk[:], kk[:], kn[:], ALU.mult))
                dve.wait_ge(a_sig, t + 1)
                step(dve.scalar_tensor_tensor(k2[:], av[:], 1.0, col(k_a, PAIRS), ALU.subtract, ALU.mult))
                step(dve.scalar_tensor_tensor(k2[:], k2[:], 1.0, k, ALU.add, ALU.mult))
                dve.wait_ge(e_ready, 3 * t + 1)
                step(dve.scalar_tensor_tensor(art[:, :, 0:P], kk[:], -1.0, eW[:], ALU.mult, ALU.mult))
                dve.sem_inc(e_used, 1)
                step(dve.tensor_tensor(kk[:], kk[:], av[:], ALU.mult))
                dve.wait_ge(e_ready, 3 * t + 2)
                step(dve.tensor_tensor(art[:, :, P:], r, eW[:], ALU.mult))
                dve.sem_inc(e_used, 1)
                step(dve.tensor_tensor(rkk[:], r, k2[:], ALU.mult))
                step(dve.tensor_tensor(rkk[:], rkk[:], col(r_k, PAIRS), ALU.mult))
                dve.wait_ge(e_ready, 3 * t + 3)
                dve.tensor_tensor(bt[:], kk[:], eW[:], ALU.mult)
                step(dve.tensor_tensor(kt[:], k2[:], eW[:], ALU.mult))
                dve.sem_inc(e_used, 1)
                dve.sem_inc(feats_ready, 1)
                for p in range(PAIRS):
                    dve.wait_ge(gram_done, PAIRS * t + p + 1)
                    for j in range(2):
                        bank = banks[(4, 0)[p % 2] + j]
                        step(dve.tensor_tensor(M[:, 2 * p + j], bank[:].rearrange("p (a b) -> p a b", a=2),
                                               spread(causal[:].unsqueeze(1), [P, 2, 2 * P]), ALU.mult))
                    dve.sem_inc(gram_copied, 1)
                for j in range(2):
                    step(dve.tensor_tensor(T[:, j:H:2, :], banks[6 + j][:].rearrange("p (a b) -> p a b", a=PAIRS),
                                           spread(first[:, 0:1, :], [P, PAIRS, P]), ALU.mult))
                step(dve.tensor_tensor(U[:], M[:, :, 0, 0:P], spread(first[:, 1:2, :], [P, H, P]), ALU.mult))
                step(dve.tensor_tensor(T[:], T[:], spread(ident[:].unsqueeze(1), [P, H, P]), ALU.add))
                step(dve.tensor_tensor(U[:], U[:], spread(ident[:].unsqueeze(1), [P, H, P]), ALU.add))
                dve.sem_inc(T_ready, 1)
                for n, b in enumerate(LEVELS):
                    halves = lambda a: a[:].rearrange("p h (j e i) -> p h j e i", e=2, i=b)
                    flat = lambda i: banks[i][:].rearrange("p (h j i) -> p h j i", h=H, i=b)
                    base = 3 * (n % 2)
                    dve.wait_ge(low_done, NL * t + n + 1)
                    mask = merge_mask[:, n, :].rearrange("p (j i) -> p j i", i=b).unsqueeze(1)
                    dve.tensor_tensor(halves(L[n])[:, :, :, 0, :], flat(base), spread(mask, [P, H, P // (2 * b), b]),
                                      ALU.mult).then_inc(low_copied, 1)
                    dve.wait_ge(merge_done, NL * t + n + 1)
                    if n < NL - 1:
                        step(dve.tensor_tensor(halves(T)[:, :, :, 0, :], halves(T)[:, :, :, 0, :], flat(base + 1), ALU.add))
                    step(dve.tensor_tensor(halves(U)[:, :, :, 1, :], halves(U)[:, :, :, 1, :], flat(base + 2), ALU.add))
                    dve.sem_inc(merged, 1)
                dve.wait_ge(d_done, t + 1)
                step(dve.tensor_tensor(k2[:], banks[1][:].rearrange("p (a b) -> p a b", a=PAIRS),
                                       spread(same_head[:].unsqueeze(1), [P, PAIRS, P]), ALU.mult))
                step(dve.tensor_tensor(k2[:], k2[:], S[:], ALU.add))
                dve.tensor_tensor(S[:], k2[:], col(wc[:], PAIRS), ALU.mult).then_inc(s_ready, 1)
                dve.wait_ge(y_copied, t + 1)
                heads = lambda a: spread(a.unsqueeze(2), [P, H, RH])
                xh = X[:].rearrange("p (h d) -> p h d", h=H)
                step(dve.tensor_reduce(st[:, 0], y[:], AX, ALU.add))
                step(dve.tensor_scalar(st[:, 0], st[:, 0], 1.0 / RH, None, ALU.mult))
                step(dve.tensor_tensor(y[:], y[:], heads(st[:, 0]), ALU.subtract))
                step(dve.tensor_tensor(xh, y[:], y[:], ALU.mult))
                step(dve.tensor_reduce(st[:, 1], xh, AX, ALU.add))
                dve.tensor_scalar(st[:, 1], st[:, 1], 1.0 / RH, GN_EPS, ALU.mult, ALU.add).then_inc(v_ready, 1)
                vt = tok[:, 2, :].rearrange("p (h d) -> p h d", h=H)
                step(dve.tensor_tensor(xh, vt, heads(bon[:]), ALU.mult))
                step(dve.tensor_tensor(X[:], X[:], ln[:, 1, :], ALU.add))
                dve.wait_ge(v_root, t + 1)
                step(dve.reciprocal(st[:, 1], st[:, 1]))
                step(dve.tensor_tensor(y[:], y[:], heads(st[:, 1]), ALU.mult))
                yf = y[:].rearrange("p h d -> p (h d)")
                step(dve.tensor_tensor(yf, yf, ln[:, 0, :], ALU.mult))
                step(dve.tensor_tensor(yf, yf, X[:], ALU.add))
                step.lap()
                dve.tensor_tensor(yf, yf, gs[:], ALU.mult).then_inc(out_ready, 1)

            tiles(dve, body, NPT, NT)
            dve.wait_ge(s_ready, NT)
            step(dve.tensor_copy(zlast[:], z[:, :, DEC]))
            dve.tensor_scalar(sout[:], S[:], float(math.exp(CENTRE)), None, ALU.mult).then_inc(state_out, 1)

        @block.scalar
        def _(act):
            step = InOrder(act, act_step)
            act.wait_ge(set_done, 1)

            def body(t, last):
                nv = DEC if last else P
                act.wait_ge(carry_set, t + 1)
                for n in range(4):
                    k = min(4, ZT - 4 * n)
                    act.wait_ge(z_done, t + 1)
                    act.activation(z[:, 4 * n:4 * n + k, 1:], banks[n][:, 0:k * P].rearrange("p (a b) -> p a b", a=k),
                                   ACT.Copy).then_inc(z_copied, 1)
                act.wait_ge(zm_ready, t + 1)
                act.activation(la[0:W_LORA, :], zm[0:W_LORA, 12, :], ACT.Tanh)
                step(act.activation(sg[:], zm[:, 13, :], ACT.Sigmoid))
                act.sem_inc(lora_in, 1)
                act.wait_ge(w_sum, t + 1)
                act.activation(sig[:], sig[:], ACT.Sigmoid).then_inc(w_sig, 1)
                act.wait_ge(a_sum, t + 1)
                act.activation(av[:], av[:], ACT.Sigmoid).then_inc(a_sig, 1)
                act.wait_ge(out_ready, t)
                act.activation(gs[:], banks[6][:], ACT.Copy).then_inc(gate_copied, 1)
                act.wait_ge(nn_ready, t + 1)
                act.activation(kn[:], kn[:], ACT.Sqrt).then_inc(nn_root, 1)
                act.wait_ge(cs_ready, t + 1)
                step(act.activation(wc[:], cs[:, :, nv - 1], ACT.Exp, scale=-KAPPA))
                act.activation(eW[:], csm[:], ACT.Exp, bias=bias[:, 0:1], scale=-KAPPA).then_inc(e_ready, 1)
                act.wait_ge(e_used, 3 * t + 1)
                act.activation(eW[:], cs[:], ACT.Exp, bias=bias[:, 0:1], scale=-KAPPA).then_inc(e_ready, 1)
                act.wait_ge(e_used, 3 * t + 2)
                act.activation(eW[:], cs[:], ACT.Exp, bias=bias[:, 1:2], scale=KAPPA).then_inc(e_ready, 1)
                act.wait_ge(tok_done, t + 1)
                for n in range(3):
                    act.activation(tok[:, n, :], banks[n][:], ACT.Copy)
                step(act.activation(bon[:], banks[3][:, 0:H], ACT.Copy))
                act.sem_inc(tok_copied, 1)
                act.wait_ge(x_done, t + 1)
                act.activation(X[:], banks[6][:], ACT.Copy).then_inc(x_copied, 1)
                act.wait_ge(w_done, t + 1)
                act.activation(W[:], banks[7][:], ACT.Copy).then_inc(w_copied, 1)
                act.wait_ge(y_done, t + 1)
                act.wait_ge(ob_stored, 16 * t)
                act.activation(y[:], banks[0][:].rearrange("p (h d) -> p h d", h=H), ACT.Copy).then_inc(y_copied, 1)
                step.lap()
                act.wait_ge(v_ready, t + 1)
                act.activation(st[:, 1], st[:, 1], ACT.Sqrt).then_inc(v_root, 1)

            tiles(act, body, NPT, NT)

        @block.tensor
        def _(pe):
            pe.wait_ge(consts_in, 16 * 11)
            pe.wait_ge(set_done, 1)

            def body(t, last):
                nv = DEC if last else P
                pe.wait_ge(h_in, 16 * (t + 1))
                pe.wait_ge(s_ready, t)
                pe.wait_ge(y_copied, t)
                for n in range(ZT):
                    for k in range(DC):
                        mm = pe.matmul(banks[n // 4][:, n % 4 * P:(n % 4 + 1) * P], wz[:, k, n * P:(n + 1) * P], hT[:, k, :],
                                       start=(k == 0), stop=(k == DC - 1))
                mm.then_inc(z_done, 1)
                pe.wait_ge(kk_sq, t + 1)
                for p in range(PAIRS):
                    mm = pe.matmul(banks[7][:, p * P:(p + 1) * P], same_head[:], kn[:, p, :], start=True, stop=True)
                mm.then_inc(nn_done, 1)
                pe.wait_ge(lora_in, t + 1)
                for p in range(PAIRS):
                    cols = slice(p * P, (p + 1) * P)
                    pe.matmul(banks[4][:, cols], wa2[0:W_LORA, cols], la[0:W_LORA, :], start=True, stop=True)
                    pe.matmul(banks[5][:, cols], wa2[W_LORA:, cols], zm[W_LORA:, 12, :], start=True, stop=True)
                pe.matmul(banks[6][:], sg[:], g2[:], start=True, stop=True).then_inc(lora_done, 1)
                pe.wait_ge(feats_ready, t + 1)
                for p in range(PAIRS):
                    cols = slice(p * P, (p + 1) * P)
                    pe.transpose(banks[0][:, cols], kt[:, p, :], ident[:])
                    pe.transpose(banks[1][:, cols], bt[:, p, :], ident[:])
                    pe.transpose(banks[2][:, cols], zm[:, 2 * PAIRS + p, :], ident[:])
                    mm = pe.matmul(banks[3][:, 2 * p:2 * p + 2], rkk[:, p, :], same_head[:, 0:P:RH], start=True, stop=True)
                mm.then_inc(tok_done, 1)
                pe.wait_ge(tok_copied, t + 1)
                pe.wait_ge(gate_copied, t + 1)
                for p in range(PAIRS):
                    if p >= 2:
                        pe.wait_ge(gram_copied, PAIRS * t + p - 1)
                    for j in range(2):
                        bank = banks[(4, 0)[p % 2] + j]
                        f = slice(RH * j, RH * j + RH)
                        pe.matmul(bank[:, 0:2 * P], bt[f, p, :], art[f, p, :], start=True, stop=True)
                        pe.matmul(bank[:, 2 * P:], kt[f, p, :], art[f, p, :], start=True, stop=True)
                        mm = pe.matmul(banks[6 + j][:, p * P:(p + 1) * P], art[f, p, 0:P], bt[f, p, :], start=True, stop=True)
                    mm.then_inc(gram_done, 1)
                pe.wait_ge(T_ready, t + 1)
                for n, b in enumerate(LEVELS):
                    halves = lambda a, h: a[:, h, :].rearrange("p (j e i) -> p j e i", e=2, i=b)
                    base = 3 * (n % 2)
                    if n > 0:
                        pe.wait_ge(merged, NL * t + n)
                    for h in range(H):
                        mm = pe.matmul(banks[base][:, h * RH:(h + 1) * RH], M[:, h, 0, 0:P], halves(T, h)[:, :, 0, :],
                                       start=True, stop=True)
                    mm.then_inc(low_done, 1)
                    pe.wait_ge(low_copied, NL * t + n + 1)
                    for h in range(H):
                        cols = slice(h * RH, (h + 1) * RH)
                        if n < NL - 1:
                            pe.matmul(banks[base + 1][:, cols], U[:, h, :], halves(L[n], h)[:, :, 0, :], start=True, stop=True)
                        mm = pe.matmul(banks[base + 2][:, cols], L[n][:, h, :], halves(U, h)[:, :, 1, :], start=True, stop=True)
                    mm.then_inc(merge_done, 1)
                for p in range(PAIRS):
                    pe.matmul(banks[6][:, p * P:(p + 1) * P], art[:, p, 0:P], S[:, p, :], start=True, stop=False)
                    for h in (2 * p, 2 * p + 1):
                        cols = slice(h * RH, (h + 1) * RH)
                        mm = pe.matmul(banks[6][:, cols], M[:, h, 1, 0:P], tok[:, 2, cols], start=False, stop=(h % 2 == 1))
                mm.then_inc(x_done, 1)
                pe.wait_ge(merged, NL * (t + 1))
                pe.wait_ge(x_copied, t + 1)
                for h in range(H):
                    cols = slice(h * RH, (h + 1) * RH)
                    mm = pe.matmul(banks[7][:, cols], U[:, h, :], X[:, cols], start=True, stop=True)
                mm.then_inc(w_done, 1)
                pe.wait_ge(w_copied, t + 1)
                for p in range(PAIRS):
                    pe.matmul(banks[0][:, p * P:(p + 1) * P], art[:, p, P:], S[:, p, :], start=True, stop=False)
                    for h in (2 * p, 2 * p + 1):
                        cols = slice(h * RH, (h + 1) * RH)
                        pe.matmul(banks[0][:, cols], M[:, h, 0, P:], W[:, cols], start=False, stop=False)
                        mm = pe.matmul(banks[0][:, cols], M[:, h, 1, P:], tok[:, 2, cols], start=False, stop=(h % 2 == 1))
                mm.then_inc(y_done, 1)
                for p in range(PAIRS):
                    cols = slice(p * P, (p + 1) * P)
                    pe.matmul(banks[1][:, cols], tok[0:nv, 1, cols], W[0:nv, cols], start=True, stop=False)
                    mm = pe.matmul(banks[1][:, cols], tok[0:nv, 0, cols], tok[0:nv, 2, cols], start=False, stop=True)
                mm.then_inc(d_done, 1)

            tiles(pe, body, NPT, NT)


def attention(nc, io):
    STEPS = NT
    with ExitStack() as c:
        sb = lambda n, s: c.enter_context(nc.sbuf_tensor("c_" + n, s, F32))
        sem = lambda n: c.enter_context(nc.semaphore("c_" + n))
        ps = lambda n, s: c.enter_context(nc.psum_tensor("c_" + n, s, F32))
        score = [ps(f"score{i}", [P, 2, 512]) for i in range(2)]
        turned = [ps(f"turned{i}", [P, 512]) for i in range(2)]
        acc = ps("acc", [P, 512])
        ident = sb("ident", [P, P])
        qT = [sb(f"qT{j}", [QK, NT, P]) for j in range(2)]
        kT = [sb(f"kT{j}", [QK, NT + 1, P]) for j in range(2)]
        v = [sb(f"v{j}", [P, NT + 1, VD]) for j in range(2)]
        probs = [sb(f"probs{i}", [P, NPT * P]) for i in range(2)]
        probsT = sb("probsT", [P, NPT, P])
        top = sb("top", [P, 2])
        total = sb("total", [P, 2])
        inv = sb("inv", [P, 1])
        out = [sb(f"out{j}", [P, NT, VD]) for j in range(2)]
        (const_in, head_in, score_done, score_free, top_ready, exp_done, turn_done, turn_dve, turn_act, probs_free, pv_done,
         acc_copied, head_used, out_stored, dve_step, total_free) = (sem(n) for n in (
             "const_in head_in score_done score_free top_ready exp_done turn_done turn_dve turn_act probs_free pv_done "
             "acc_copied head_used out_stored dve_step total_free").split())
        pool_on = sem("pool_on")
        nothing = sb("nothing", [P, D])
        nothing_set, overflow_filled = sem("nothing_set"), sem("overflow_filled")
        head_in = [head_in, sem("head_in_odd")]
        block = c.enter_context(nc.Block())
        keys = [[(k, P) for k in range(i + 1)] for i in range(NPT)] + [[(PAST_TILE, P), (NPT, DEC)]]
        width = [sum(n for _, n in ks) for ks in keys]

        @block.sync
        def _(sp):
            sp.dma_start(ident[:], io["ident"]).then_inc(const_in, 16)
            with sp.Fori(0, H // 2) as u:
                for j in range(2):
                    h = u * 2 + j
                    sp.wait_ge(head_used, u)
                    sp.dma_start(qT[j][:], io["qT_d"][0:NT, :, bass.ds(h, 1), :].rearrange("t d o n -> d t (o n)")).then_inc(head_in[j], 16)
                    sp.dma_start(kT[j][:], io["kT_d"][:, :, bass.ds(h, 1), :].rearrange("t d o n -> d t (o n)")).then_inc(head_in[j], 16)
                    sp.dma_start(v[j][:], io["v_d"][:, :, bass.ds(h, 1), :].rearrange("t p o n -> p t (o n)")).then_inc(head_in[j], 16)
            sp.wait_ge(nothing_set, 1)
            with sp.Fori(0, OVERFLOW) as n:
                sp.dma_start(at(io["y_d"], n + NE), nothing[:]).then_inc(overflow_filled, 16)
            sp.wait_ge(overflow_filled, 16 * OVERFLOW)

        @block.gpsimd
        def _(pool):
            pool.memset(nothing[:], 0.0).then_inc(nothing_set, 1)
            with pool.Fori(0, H // 2) as u:
                for j in range(2):
                    pool.wait_ge(acc_copied, 2 * STEPS * u + STEPS * (j + 1))
                    goes_on(pool, pool_on)
                    pool.dma_start(io["oa_d"][:, :, bass.ds(u * 2 + j, 1), :].rearrange("t p o n -> p t (o n)"), out[j][:]).then_inc(out_stored, 16)
            pool.wait_ge(out_stored, 16 * H)

        @block.vector
        def _(dve):
            step = InOrder(dve, dve_step)
            with dve.Fori(0, H // 2) as u:
                for j in range(2):
                    dve.wait_ge(out_stored, 32 * u)
                    g = lambda s: 2 * STEPS * u + STEPS * j + s

                    def maxima(s):
                        b = (j * STEPS + s) % 2
                        sc = score[b][:].rearrange("p a n -> p (a n)")
                        dve.wait_ge(score_done, g(s) + 1)
                        if s < NPT:
                            step(dve.memset(sc[0:64, width[s] - 64:width[s]], NEG))
                        dve.tensor_reduce(top[:, b:b + 1], sc[:, 0:width[s]], AX, ALU.max, negate=True).then_inc(top_ready, 1)

                    maxima(0)
                    for s in range(STEPS):
                        if s + 1 < STEPS:
                            maxima(s + 1)
                        n = min(4, len(keys[s]))
                        dve.wait_ge(turn_done, 2 * g(s) + 1)
                        dve.wait_ge(pv_done, g(s))
                        if s < NPT:
                            dve.tensor_copy(probsT[:, 0:n, :], turned[0][:, 0:n * P].rearrange("p (a b) -> p a b", b=P)).then_inc(turn_dve, 1)
                        else:
                            step(dve.tensor_copy(probsT[:, 0, :], turned[0][:, 0:P]))
                            dve.tensor_copy(probsT[0:DEC, 1, :], turned[0][0:DEC, P:2 * P]).then_inc(turn_dve, 1)
                        b = (j * STEPS + s) % 2
                        dve.wait_ge(exp_done, g(s) + 1)
                        dve.wait_ge(acc_copied, g(s))
                        step(dve.reciprocal(inv[:], total[:, b:b + 1]))
                        dve.sem_inc(total_free, 1)
                        dve.wait_ge(pv_done, g(s) + 1)
                        dve.tensor_scalar(out[j][:, s, :], acc[:, 0:VD], inv[:, 0:1], None, ALU.mult).then_inc(acc_copied, 1)
                    step.lap()

        @block.scalar
        def _(act):
            act.sem_inc(score_free, 2)
            act.sem_inc(probs_free, 1)
            act.sem_inc(total_free, 1)
            with act.Fori(0, H // 2) as u:
                for j in range(2):
                    g = lambda s: 2 * STEPS * u + STEPS * j + s

                    def exps(s):
                        b = (j * STEPS + s) % 2
                        act.wait_ge(top_ready, g(s) + 1)
                        act.wait_ge(probs_free, g(s))
                        act.wait_ge(total_free, g(s))
                        act.activation(probs[b][:, 0:width[s]], score[b][:].rearrange("p a n -> p (a n)")[:, 0:width[s]],
                                       ACT.Exp, bias=top[:, b:b + 1], accum_out=total[:, b:b + 1]).then_inc(exp_done, 1)
                        act.wait_ge(exp_done, g(s) + 1)
                        act.sem_inc(score_free, 1)

                    for s in range(STEPS):
                        exps(s)
                        n = len(keys[s])
                        if n > 4:
                            act.wait_ge(turn_done, 2 * g(s) + 2)
                            act.wait_ge(pv_done, g(s))
                            act.activation(probsT[:, 4:n, :], turned[1][:, 0:(n - 4) * P], ACT.Copy).then_inc(turn_act, 1)
                        else:
                            act.sem_inc(turn_act, 1)

        @block.tensor
        def _(pe):
            pe.wait_ge(const_in, 16)
            with pe.Fori(0, H // 2) as u:
                for j in range(2):
                    g = lambda s: 2 * STEPS * u + STEPS * j + s
                    pe.wait_ge(head_in[j], 48 * (u + 1))

                    def scores(s):
                        b = (j * STEPS + s) % 2
                        pe.wait_ge(score_free, g(s) + 1)
                        if s < NPT:
                            for n in range(0, width[s], 512):
                                m = min(512, width[s] - n)
                                mm = pe.matmul(score[b][:, n // 512, 0:m], qT[j][:, s, :], kT[j][:, n // P:(n + m) // P, :],
                                               start=True, stop=True)
                        else:
                            pe.matmul(score[b][:, 0, 0:P], qT[j][:, s, :], kT[j][:, PAST_TILE, :], start=True, stop=True)
                            mm = pe.matmul(score[b][:, 0, P:P + DEC], qT[j][:, s, :], kT[j][:, NPT, 0:DEC], start=True, stop=True)
                        mm.then_inc(score_done, 1)

                    scores(0)
                    for s in range(STEPS):
                        if s + 1 < STEPS:
                            scores(s + 1)
                        b = (j * STEPS + s) % 2
                        pe.wait_ge(exp_done, g(s) + 1)
                        for n, (_, m) in enumerate(keys[s]):
                            mm = pe.transpose(turned[n // 4][0:m, n % 4 * P:(n % 4 + 1) * P], probs[b][:, n * P:n * P + m], ident[:])
                            if n == 3 and len(keys[s]) > 4:
                                mm.then_inc(turn_done, 1)
                        mm.then_inc(turn_done, 1 if len(keys[s]) > 4 else 2)
                        pe.wait_ge(turn_dve, g(s) + 1)
                        pe.wait_ge(turn_act, g(s) + 1)
                        pe.sem_inc(probs_free, 1)
                        pe.wait_ge(acc_copied, g(s))
                        for n, (k, m) in enumerate(keys[s]):
                            mm = pe.matmul(acc[:, 0:VD], probsT[0:m, n, :], v[j][0:m, k, :], start=(n == 0), stop=(n == len(keys[s]) - 1))
                        mm.then_inc(pv_done, 1)
                pe.wait_ge(pv_done, 2 * STEPS * (u + 1))
                pe.sem_inc(head_used, 1)


def merge(nc, io, keep):
    with ExitStack() as c:
        sb = lambda n, s, d=F32: c.enter_context(nc.sbuf_tensor("d_" + n, s, d))
        sem = lambda n: c.enter_context(nc.semaphore("d_" + n))
        banks = [c.enter_context(nc.psum_tensor(f"d_ps{i}", [P, 512], F32)) for i in range(8)]
        wg = sb("wg", [P, DC, 2 * D])
        wo = sb("wo", [P, 2 * HB, D])
        wr = sb("wr", [P, DC, RT])
        br = sb("br", [P, RT])
        ident = sb("ident", [P, P])
        before = sb("before", [P, P])
        ones = sb("ones", [P, P])
        g_ffn = sb("g_ffn", [P, D])
        count_up = sb("count_up", [P, NE])
        real = sb("real", [P, 1])
        hT = sb("hT", [P, DC, P])
        o = sb("o", [P, 2, H * VD])
        x = sb("x", [P, D])
        oT = sb("oT", [P, 2 * HB, P])
        gate = sb("gate", [P, 2, 512])
        mixed = sb("mixed", [P, 512])
        junk = sb("junk", [P, D])
        ms = sb("ms", [P, 1])
        h2 = sb("h2", [P, D])
        h2T = sb("h2T", [P, DC, P])
        lg = sb("lg", [P, RT])
        gpad = sb("gpad", [P, 8])
        gtop = sb("gtop", [P, 8])
        gidx = sb("gidx", [P, 8], U32)
        etop = sb("etop", [P, 8])
        eidx = sb("eidx", [P, 8], U32)
        small = sb("small", [P, 8])
        gexp = sb("gexp", [P, NG])
        pen = sb("pen", [P, NG])
        el = sb("el", [P, NE])
        rec = sb("rec", [P, 2 * NE + 6])
        both = sb("both", [P, NE])
        pos = sb("pos", [P, NE])
        prod = sb("prod", [P, 2, NE])
        run, route = keep["run"], keep["route"]
        pool_on = sem("pool_on")
        (consts_in, set_done, h_in, o_in, x_in, oT_done, oT_copied, gates_done, gate_used, proj_done, mixed_done, x_done, x_sq,
         ms_ready, rms_root, h2_ready, h2T_done, h2T_copied, lg_done, neg_top, g_sum, d_ready, d_sig, both_ready, count_done,
         counted, x_stored, h2_stored, dve_step, act_step) = (sem(n) for n in (
             "consts_in set_done h_in o_in x_in oT_done oT_copied gates_done gate_used proj_done mixed_done x_done x_sq "
             "ms_ready rms_root h2_ready h2T_done h2T_copied lg_done neg_top g_sum d_ready d_sig both_ready count_done "
             "counted x_stored h2_stored dve_step act_step").split())
        block = c.enter_context(nc.Block())

        @block.sync
        def _(sp):
            for dst, src in ((wg[:], io["w_gates"]), (wo[:], io["w_out"]), (wr[:], io["w_router"]),
                             (br[:], io["b_router"].partition_broadcast(P)), (ident[:], io["ident"]),
                             (before[:], io["causal"][:, 0:P]), (g_ffn[:], io["norm_ffn_g"].partition_broadcast(P)),
                             (count_up[:], io["count_up"].partition_broadcast(P)), (real[:], io["real"])):
                sp.dma_start(dst, src).then_inc(consts_in, 16)

            def body(t, _):
                sp.wait_ge(oT_done, t)
                sp.dma_start(o[:, 0, :], at(io["oa_d"], t).rearrange("p h d -> p (h d)")).then_inc(o_in, 16)
                sp.dma_start(o[:, 1, :], at(io["ob_d"], t).rearrange("p h d -> p (h d)")).then_inc(o_in, 16)
                sp.wait_ge(gates_done, 2 * t)
                sp.dma_start(hT[:], at(io["hT_d"], t)).then_inc(h_in, 16)
                sp.wait_ge(x_stored, 16 * t)
                sp.wait_ge(h2_ready, t)
                sp.dma_start(x[:], at(io["x"], t)).then_inc(x_in, 16)

            tiles(sp, body, NPT, NT)

        @block.gpsimd
        def _(pool):
            pool.memset(ones[:], 1.0)
            pool.memset(gpad[:], -BIG)
            pool.memset(run[:], 0.0).then_inc(set_done, 1)

            def body(t, _):
                pool.wait_ge(x_done, t + 1)
                goes_on(pool, pool_on)
                pool.dma_start(at(io["x2_d"], t), x[:]).then_inc(x_stored, 16)
                pool.wait_ge(h2_ready, t + 1)
                goes_on(pool, pool_on)
                pool.dma_start(at(io["h2_d"], t), h2[:]).then_inc(h2_stored, 16)

            tiles(pool, body, NPT, NT)
            pool.wait_ge(x_stored, 16 * NT)
            pool.wait_ge(h2_stored, 16 * NT)

        @block.vector
        def _(dve):
            step = InOrder(dve, dve_step)
            dve.wait_ge(consts_in, 16 * 9)
            dve.wait_ge(set_done, 1)

            def body(t, last):
                dve.wait_ge(oT_done, t + 1)
                dve.tensor_copy(oT[:, HB:, :], banks[1][:].rearrange("p (a b) -> p a b", b=P)).then_inc(oT_copied, 1)
                dve.wait_ge(x_in, 16 * (t + 1))
                for n in range(2):
                    cols = slice(512 * n, 512 * n + 512)
                    dve.wait_ge(gate_used, 2 * t + n + 1)
                    dve.wait_ge(proj_done, 2 * t + n + 1)
                    for b in range(2):
                        step(dve.tensor_tensor(mixed[:], gate[:, b, :], banks[(4, 0)[n] + b][:], ALU.mult))
                        if b == 1:
                            dve.sem_inc(mixed_done, 1)
                        ins = dve.tensor_tensor(x[:, cols], x[:, cols], mixed[:], ALU.add)
                        if n == 1 and b == 1:
                            ins.then_inc(x_done, 1)
                        else:
                            step(ins)
                dve.wait_ge(x_sq, t + 1)
                dve.tensor_scalar(ms[:], ms[:], 1.0 / D, EPS, ALU.mult, ALU.add).then_inc(ms_ready, 1)
                dve.wait_ge(rms_root, t + 1)
                step(dve.reciprocal(ms[:], ms[:]))
                dve.wait_ge(h2_stored, 16 * t)
                dve.wait_ge(h2T_done, t)
                dve.scalar_tensor_tensor(h2[:], x[:], ms[:, 0:1], g_ffn[:], ALU.mult, ALU.mult).then_inc(h2_ready, 1)
                dve.wait_ge(h2T_done, t + 1)
                dve.tensor_copy(h2T[:, 4:, :], banks[3][:].rearrange("p (a b) -> p a b", b=P)).then_inc(h2T_copied, 1)
                dve.wait_ge(lg_done, t + 1)
                step(dve.tensor_tensor(lg[:], banks[4][:, 0:RT], br[:], ALU.add))
                step(dve.tensor_copy(gpad[:, 0:NG], lg[:, 0:NG]))
                step(dve.max(gtop[:], gpad[:]))
                dve.tensor_scalar(small[:, 0:1], gtop[:, 0:1], -1.0, None, ALU.mult).then_inc(neg_top, 1)
                step(dve.max_index(gidx[:], gtop[:], gpad[:]))
                step(dve.tensor_copy(small[:, 2:3], gidx[:, 0:1]))
                step(dve.tensor_scalar(pen[:], count_up[:, 0:NG], small[:, 2:3], None, ALU.is_equal))
                step(dve.tensor_scalar(pen[:], pen[:], BIG, -BIG, ALU.mult, ALU.add))
                step(dve.tensor_tensor(el[:].rearrange("p (g e) -> p g e", g=NG), lg[:, NG:].rearrange("p (g e) -> p g e", g=NG),
                                       spread(pen[:].unsqueeze(2), [P, NG, EPG]), ALU.add))
                step(dve.max(etop[:], el[:]))
                step(dve.max_index(eidx[:], etop[:], el[:]))
                step(dve.tensor_tensor(small[:, 4:5], etop[:, 0:1], etop[:, 1:2], ALU.subtract))
                dve.tensor_scalar(small[:, 5:6], small[:, 4:5], -1.0, None, ALU.mult).then_inc(d_ready, 1)
                step(dve.tensor_copy(rec[:, 2 * NE:2 * NE + 2], eidx[:, 0:2]))
                hot = rec[:, 0:2 * NE].rearrange("p (k e) -> p k e", k=2)
                for k in range(2):
                    step(dve.tensor_scalar(hot[:, k, :], count_up[:], rec[:, 2 * NE + k:2 * NE + k + 1], None, ALU.is_equal))
                    if last:
                        step(dve.tensor_scalar(hot[:, k, :], hot[:, k, :], real[:, 0:1], None, ALU.mult))
                dve.tensor_tensor(both[:], hot[:, 0, :], hot[:, 1, :], ALU.add).then_inc(both_ready, 1)
                dve.wait_ge(g_sum, t + 1)
                step(dve.reciprocal(small[:, 3:4], small[:, 1:2]))
                dve.wait_ge(d_sig, t + 1)
                step(dve.tensor_scalar(rec[:, 2 * NE + 4:], small[:, 6:8], small[:, 3:4], None, ALU.mult))
                dve.wait_ge(count_done, t + 1)
                step(dve.tensor_tensor(pos[:], banks[5][:, 0:NE], run[:], ALU.add))
                dve.tensor_tensor(run[:], banks[6][:, 0:NE], run[:], ALU.add).then_inc(counted, 1)
                step(dve.tensor_tensor(prod[:], hot, spread(pos[:].unsqueeze(1), [P, 2, NE]), ALU.mult))
                step(dve.tensor_reduce(rec[:, 2 * NE + 2:2 * NE + 4], prod[:], AX, ALU.add))
                dve.wait_ge(counted, t + 1)
                step(dve.tensor_copy(route[:, bass.ds(t, 1), :].rearrange("p o n -> p (o n)"), rec[:]))
                step.lap()

            tiles(dve, body, NPT, NT)

        @block.scalar
        def _(act):
            step = InOrder(act, act_step)

            def body(t, _):
                act.wait_ge(oT_done, t + 1)
                act.activation(oT[:, 0:HB, :], banks[0][:].rearrange("p (a b) -> p a b", b=P), ACT.Copy).then_inc(oT_copied, 1)
                for n in range(2):
                    act.wait_ge(gates_done, 2 * t + n + 1)
                    act.wait_ge(mixed_done, 2 * t + n)
                    for b in range(2):
                        ins = act.activation(gate[:, b, :], banks[(2, 6)[n] + b][:], ACT.Sigmoid)
                    ins.then_inc(gate_used, 1)
                act.wait_ge(x_done, t + 1)
                act.wait_ge(x_sq, t)
                act.activation(junk[:], x[:], ACT.Square, accum_out=ms[:]).then_inc(x_sq, 1)
                act.wait_ge(ms_ready, t + 1)
                act.activation(ms[:], ms[:], ACT.Sqrt).then_inc(rms_root, 1)
                act.wait_ge(h2T_done, t + 1)
                act.activation(h2T[:, 0:4, :], banks[2][:].rearrange("p (a b) -> p a b", b=P), ACT.Copy).then_inc(h2T_copied, 1)
                act.wait_ge(neg_top, t + 1)
                act.wait_ge(g_sum, t)
                act.activation(gexp[:], lg[:, 0:NG], ACT.Exp, bias=small[:, 0:1], accum_out=small[:, 1:2]).then_inc(g_sum, 1)
                act.wait_ge(d_ready, t + 1)
                act.activation(small[:, 6:8], small[:, 4:6], ACT.Sigmoid).then_inc(d_sig, 1)

            tiles(act, body, NPT, NT)

        @block.tensor
        def _(pe):
            pe.wait_ge(consts_in, 16 * 9)
            pe.wait_ge(set_done, 1)

            def body(t, _):
                pe.wait_ge(o_in, 32 * (t + 1))
                pe.wait_ge(mixed_done, 2 * t)
                for b in range(2):
                    for k in range(HB):
                        mm = pe.transpose(banks[b][:, k * P:(k + 1) * P], o[:, b, k * P:(k + 1) * P], ident[:])
                mm.then_inc(oT_done, 1)
                pe.wait_ge(h_in, 16 * (t + 1))
                pe.wait_ge(h2T_copied, 2 * t)
                pe.wait_ge(counted, t)
                for n in range(2):
                    for b in range(2):
                        for k in range(DC):
                            mm = pe.matmul(banks[(2, 6)[n] + b][:], hT[:, k, :], wg[:, k, b * D + n * 512:b * D + n * 512 + 512],
                                           start=(k == 0), stop=(k == DC - 1))
                    mm.then_inc(gates_done, 1)
                    pe.wait_ge(oT_copied, 2 * (t + 1))
                    for b in range(2):
                        for k in range(HB):
                            mm = pe.matmul(banks[(4, 0)[n] + b][:], oT[:, HB * b + k, :], wo[:, HB * b + k, n * 512:n * 512 + 512],
                                           start=(k == 0), stop=(k == HB - 1))
                    mm.then_inc(proj_done, 1)
                pe.wait_ge(h2_ready, t + 1)
                for k in range(DC):
                    mm = pe.transpose(banks[2 + k // 4][:, k % 4 * P:(k % 4 + 1) * P], h2[:, k * P:(k + 1) * P], ident[:])
                mm.then_inc(h2T_done, 1)
                pe.wait_ge(h2T_copied, 2 * (t + 1))
                for k in range(DC):
                    mm = pe.matmul(banks[4][:, 0:RT], h2T[:, k, :], wr[:, k, :], start=(k == 0), stop=(k == DC - 1))
                mm.then_inc(lg_done, 1)
                pe.wait_ge(both_ready, t + 1)
                pe.matmul(banks[5][:, 0:NE], before[:], both[:], start=True, stop=True)
                pe.matmul(banks[6][:, 0:NE], ones[:], both[:], start=True, stop=True).then_inc(count_done, 1)

            tiles(pe, body, NPT, NT)


def slots(nc, io, keep):
    BLOCKS = NE + OVERFLOW + 2
    NBMAX = -(-(SEQ + DEC) // CAP)
    with ExitStack() as c:
        sb = lambda n, s, d=F32: c.enter_context(nc.sbuf_tensor("e_" + n, s, d))
        sem = lambda n: c.enter_context(nc.semaphore("e_" + n))
        more = sb("more", [P, NE])
        gt = sb("gt", [P, NE])
        upto = sb("upto", [P, NE])
        one = sb("one", [P, NE])
        base = sb("base", [P, NE])
        count_up = sb("count_up", [P, NE])
        owned = sb("owned", [P, OVERFLOW, NE])
        q = sb("q", [P, NT, 2])
        ge = sb("ge", [P, NT, 2])
        hb = sb("hb", [P, NT, 2, NE])
        bb = sb("bb", [P, NT, 2])
        over = sb("over", [P, NT, 2])
        place = sb("place", [P, NT, 2])
        fixed = sb("fixed", [P, 2, NT, 2])
        zeros = sb("zeros", [P, BLOCKS], I32)
        token = sb("token", [P, NT], I32)
        table = [[sb(f"table{t}_{k}", [P, 1], I32) for k in range(2)] for t in range(NT)]
        tf = sb("tf", [P, NT, 2])
        run, route, row_of, plan = keep["run"], keep["route"], keep["row_of"], keep["plan"]
        planf = sb("planf", [P, OVERFLOW + 1])
        consts_in, set_done, dve_step, table_set, scattered, ready = (
            sem(n) for n in ("consts_in", "set_done", "dve_step", "table_set", "scattered", "ready"))
        block = c.enter_context(nc.Block())

        @block.sync
        def _(sp):
            sp.dma_start(count_up[:], io["count_up"].partition_broadcast(P)).then_inc(consts_in, 16)
            sp.dma_start(fixed[:], io["fixed"]).then_inc(consts_in, 16)
            sp.dma_start(token[:], io["token"]).then_inc(consts_in, 16)

        @block.gpsimd
        def _(pool):
            pool.memset(one[:], 1.0).then_inc(set_done, 1)
            pool.memset(zeros[:], 0).then_inc(set_done, 1)
            pool.wait_ge(set_done, 2)
            pool.dma_start(io["table_d"].rearrange("(p n) o -> p (n o)", p=P), zeros[:]).then_inc(table_set, 16)
            pool.wait_ge(table_set, 16)
            pool.wait_ge(consts_in, 48)
            pool.wait_ge(ready, 1)
            for t in range(NT):
                for k in range(2):
                    pool.indirect_dma_start(io["table_d"], bass.IndirectOffsetOnAxis(ap=table[t][k][:, 0:1], axis=0),
                                            token[:, t:t + 1], None).then_inc(scattered, 16)
            pool.wait_ge(scattered, 32 * NT)

        @block.vector
        def _(dve):
            step = InOrder(dve, dve_step)
            dve.wait_ge(consts_in, 48)
            dve.wait_ge(set_done, 2)
            step(dve.tensor_scalar(more[:], run[:], float(CAP), None, ALU.is_gt))
            for n in range(2, NBMAX):
                step(dve.tensor_scalar(gt[:], run[:], float(CAP * n), None, ALU.is_gt))
                step(dve.tensor_tensor(more[:], more[:], gt[:], ALU.add))
            step(dve.tensor_tensor_scan(upto[:], one[:], more[:], 0.0, ALU.mult, ALU.add))
            step(dve.tensor_tensor(base[:], upto[:], more[:], ALU.subtract))
            for n in range(OVERFLOW):
                step(dve.tensor_scalar(owned[:, n, :], upto[:], float(n), None, ALU.is_le))
            step(dve.tensor_reduce(planf[:, 0:OVERFLOW], owned[:], AX, ALU.add))
            step(dve.tensor_scalar(planf[:, 0:OVERFLOW], planf[:, 0:OVERFLOW], float(NE - 1), None, ALU.min))
            step(dve.tensor_copy(planf[:, OVERFLOW:], upto[:, NE - 1:]))
            step(dve.tensor_copy(plan[:], planf[:]))
            pos, ex = route[:, :, 2 * NE + 2:2 * NE + 4], route[:, :, 2 * NE:2 * NE + 2]
            step(dve.tensor_scalar(q[:], pos, float(CAP), None, ALU.is_ge))
            for n in range(2, NBMAX):
                step(dve.tensor_scalar(ge[:], pos, float(CAP * n), None, ALU.is_ge))
                step(dve.tensor_tensor(q[:], q[:], ge[:], ALU.add))
            step(dve.scalar_tensor_tensor(place[:], q[:], -float(CAP), pos, ALU.mult, ALU.add))
            for k in range(2):
                step(dve.tensor_tensor(hb[:, :, k, :], route[:, :, NE * k:NE * k + NE],
                                       spread(base[:].unsqueeze(1), [P, NT, NE]), ALU.mult))
                step(dve.tensor_reduce(bb[:, :, k], hb[:, :, k, :], AX, ALU.add))
            step(dve.tensor_scalar(over[:], q[:], 1.0, None, ALU.min))
            step(dve.scalar_tensor_tensor(bb[:], q[:], float(NE - 1), bb[:], ALU.add, ALU.add))
            step(dve.tensor_tensor(bb[:], bb[:], ex, ALU.subtract))
            step(dve.tensor_tensor(bb[:], bb[:], over[:], ALU.mult))
            step(dve.tensor_tensor(bb[:], bb[:], ex, ALU.add))
            step(dve.scalar_tensor_tensor(tf[:], place[:], float(BLOCKS), bb[:], ALU.mult, ALU.add))
            step(dve.tensor_tensor(tf[:], tf[:], fixed[:, 0], ALU.mult))
            step(dve.tensor_tensor(tf[:], tf[:], fixed[:, 1], ALU.add))
            for t in range(NT):
                for k in range(2):
                    step(dve.tensor_copy(table[t][k][:], tf[:, t, k:k + 1]))
            dve.sem_inc(ready, 1)
            step(dve.scalar_tensor_tensor(bb[:], bb[:], float(CAP), place[:], ALU.mult, ALU.add))
            step(dve.tensor_tensor(bb[:], bb[:], fixed[:, 0], ALU.mult))
            for t in range(NT):
                for k in range(2):
                    step(dve.tensor_copy(row_of[t][k][:], bb[:, t, k:k + 1]))


def experts(nc, io, keep):
    BLOCKS = NE + OVERFLOW + 2
    UNROLL = 2
    with ExitStack() as c:
        sb = lambda n, s, d=F32: c.enter_context(nc.sbuf_tensor("f_" + n, s, d))
        sem = lambda n: c.enter_context(nc.semaphore("f_" + n))
        ps = lambda n: c.enter_context(nc.psum_tensor("f_" + n, [P, 512], F32))
        ident = sb("ident", [P, P])
        tokens = sb("tokens", [P, BLOCKS], I32)
        index = [sb(f"index{j}", [P, 1], I32) for j in range(2)]
        xg = [sb(f"xg{j}", [P, D]) for j in range(2)]
        xT = [sb(f"xT{j}", [P, DC, P]) for j in range(2)]
        wgu = [sb(f"wgu{j}", [P, DC, 2 * FF]) for j in range(2)]
        wd = [sb(f"wd{j}", [P, 2, D]) for j in range(2)]
        sg = sb("sg", [P, FF])
        mid = sb("mid", [P, FF])
        midT = sb("midT", [P, 2, P])
        y = [sb(f"y{j}", [P, D]) for j in range(2)]
        turned = [ps("turned0"), ps("turned1")]
        hidden = [ps("hidden0"), ps("hidden1")]
        midps = ps("midps")
        down = [ps("down0"), ps("down1")]
        plan = keep["plan"]
        pool_on = sem("pool_on")
        names = ("const_in tokens_in index_set x_in0 x_in1 up_in0 up_in1 down_in0 down_in1 turn_done turn_dve turn_act up_done sig_done mid_ready "
                 "midT_done midT_copied down_done y_dve y_act y_stored dve_step").split()
        s = {n: sem(n) for n in names}
        o = {n: sem("o_" + n) for n in names}
        block = c.enter_context(nc.Block())

        def gather(pool, s, n, b, blk):
            pool.wait_ge(s["turn_done"], n)
            pool.tensor_copy(index[b][:], tokens[:, bass.ds(blk, 1)]).then_inc(s["index_set"], 1)
            pool.wait_ge(s["index_set"], n + 1)
            goes_on(pool, pool_on)
            pool.indirect_dma_start(xg[b][:], None, io["h2_d"].rearrange("t p n -> (t p) n"),
                                    bass.IndirectOffsetOnAxis(ap=index[b][:, 0:1], axis=0)).then_inc(s["x_in" + str(b)], 16)

        def turn(pe, s, n, b, m):
            pe.wait_ge(s["x_in" + str(b)], 16 * (m + 1))
            pe.wait_ge(s["turn_dve"], n)
            pe.wait_ge(s["turn_act"], n)
            for k in range(DC):
                mm = pe.transpose(turned[k // 4][:, k % 4 * P:(k % 4 + 1) * P], xg[b][:, k * P:(k + 1) * P], ident[:])
            mm.then_inc(s["turn_done"], 1)

        def up(pe, s, n, b, m):
            pe.wait_ge(s["turn_dve"], n + 1)
            pe.wait_ge(s["turn_act"], n + 1)
            pe.wait_ge(s["up_in" + str(b)], 16 * (m + 1))
            pe.wait_ge(s["mid_ready"], n)
            for k in range(DC):
                mm = pe.matmul(hidden[b][:], xT[b][:, k, :], wgu[b][:, k, :], start=(k == 0), stop=(k == DC - 1))
            mm.then_inc(s["up_done"], 1)

        def turn_mid(pe, s, n, b):
            pe.wait_ge(s["mid_ready"], n + 1)
            for k in range(2):
                mm = pe.transpose(midps[:, k * P:(k + 1) * P], mid[:, k * P:(k + 1) * P], ident[:])
            mm.then_inc(s["midT_done"], 1)

        def project(pe, s, n, b, m):
            pe.wait_ge(s["midT_copied"], n + 1)
            pe.wait_ge(s["down_in" + str(b)], 16 * (m + 1))
            pe.wait_ge(s["y_dve"], n)
            pe.wait_ge(s["y_act"], n)
            for h in range(2):
                for k in range(2):
                    mm = pe.matmul(down[h][:], midT[:, k, :], wd[b][:, k, 512 * h:512 * h + 512], start=(k == 0), stop=(k == 1))
            mm.then_inc(s["down_done"], 1)

        def copy_turned(eng, copy, s, n, b, half, flag):
            eng.wait_ge(s["turn_done"], n + 1)
            eng.wait_ge(s["up_done"], n)
            copy(xT[b][:, 4 * half:4 * half + 4, :], turned[half][:].rearrange("p (a b) -> p a b", b=P)).then_inc(s[flag], 1)

        def middle_dve(dve, step, s, n, b):
            dve.wait_ge(s["sig_done"], n + 1)
            dve.wait_ge(s["midT_done"], n)
            step(dve.tensor_tensor(mid[:], hidden[b][:, 0:FF], sg[:], ALU.mult))
            step.lap()
            dve.tensor_tensor(mid[:], mid[:], hidden[b][:, FF:], ALU.mult).then_inc(s["mid_ready"], 1)

        def copy_mid(dve, s, n):
            dve.wait_ge(s["midT_done"], n + 1)
            dve.wait_ge(s["down_done"], n)
            dve.tensor_copy(midT[:], midps[:, 0:2 * P].rearrange("p (a b) -> p a b", b=P)).then_inc(s["midT_copied"], 1)

        def copy_y(eng, copy, s, n, b, half, flag):
            eng.wait_ge(s["down_done"], n + 1)
            copy(y[b][:, 512 * half:512 * half + 512], down[half][:]).then_inc(s[flag], 1)

        def sigmoid(act, s, n, b):
            act.wait_ge(s["up_done"], n + 1)
            act.wait_ge(s["mid_ready"], n)
            act.activation(sg[:], hidden[b][:, 0:FF], ACT.Sigmoid).then_inc(s["sig_done"], 1)

        def overflow(eng, work):
            used = eng.value_load(plan[0:1, OVERFLOW:OVERFLOW + 1], min_val=0, max_val=OVERFLOW)
            with eng.Fori(0, OVERFLOW) as n:
                with eng.If(n < used):
                    work(n)
                with eng.Else():
                    eng.nop()

        @block.sync
        def _(sp):
            sp.dma_start(ident[:], io["ident"]).then_inc(s["const_in"], 16)
            sp.dma_start(tokens[:], io["table_d"].rearrange("(p n) o -> p (n o)", p=P)).then_inc(s["tokens_in"], 16)
            with sp.Fori(0, NE // UNROLL) as u:
                for j in range(UNROLL):
                    e = u * UNROLL + j
                    sp.wait_ge(s["up_done"], u * UNROLL)
                    sp.dma_start(wgu[j][:], at(io["w_gate_up"], e)).then_inc(s["up_in" + str(j)], 16)
                    sp.wait_ge(s["down_done"], u * UNROLL)
                    sp.dma_start(wd[j][:], at(io["w_down"], e)).then_inc(s["down_in" + str(j)], 16)
            sp.wait_ge(s["down_done"], NE)

            def work(n):
                e = sp.value_load(plan[0:1, bass.ds(n, 1)], min_val=0, max_val=NE - 1)
                sp.wait_ge(o["down_done"], n)
                sp.dma_start(wgu[0][:], at(io["w_gate_up"], e)).then_inc(o["up_in0"], 16)
                sp.dma_start(wd[0][:], at(io["w_down"], e)).then_inc(o["down_in0"], 16)

            overflow(sp, work)

        @block.gpsimd
        def _(pool):
            pool.wait_ge(s["tokens_in"], 16)

            def store(s, n, b, blk):
                pool.wait_ge(s["y_dve"], n + 1)
                pool.wait_ge(s["y_act"], n + 1)
                goes_on(pool, pool_on)
                pool.dma_start(at(io["y_d"], blk), y[b][:]).then_inc(s["y_stored"], 16)

            gather(pool, s, 0, 0, 0)
            with pool.Fori(0, NE // UNROLL) as u:
                for j in range(UNROLL):
                    e = u * UNROLL + j
                    if j == 0:
                        gather(pool, s, e + 1, 1, e + 1)
                    else:
                        gather(pool, s, e + 1, 0, e + 1)
                    store(s, e, j, e)
            pool.wait_ge(s["y_stored"], 16 * NE)
            pool.wait_ge(s["x_in0"], 16 * (NE // 2 + 1))

            def work(n):
                gather(pool, o, n, 0, n + NE)
                store(o, n, 0, n + NE)
                pool.wait_ge(o["y_stored"], 16 * (n + 1))

            overflow(pool, work)

        @block.vector
        def _(dve):
            step = InOrder(dve, s["dve_step"])
            copy_turned(dve, dve.tensor_copy, s, 0, 0, 1, "turn_dve")
            with dve.Fori(0, NE // UNROLL) as u:
                for j in range(UNROLL):
                    e = u * UNROLL + j
                    middle_dve(dve, step, s, e, j)
                    copy_turned(dve, dve.tensor_copy, s, e + 1, 1 - j, 1, "turn_dve")
                    copy_mid(dve, s, e)
                    dve.wait_ge(s["y_stored"], 16 * e)
                    copy_y(dve, dve.tensor_copy, s, e, j, 1, "y_dve")

            def work(n):
                copy_turned(dve, dve.tensor_copy, o, n, 0, 1, "turn_dve")
                middle_dve(dve, step, o, n, 0)
                copy_mid(dve, o, n)
                dve.wait_ge(o["y_stored"], 16 * n)
                copy_y(dve, dve.tensor_copy, o, n, 0, 1, "y_dve")

            overflow(dve, work)

        @block.scalar
        def _(act):
            copy = lambda dst, src: act.activation(dst, src, ACT.Copy)
            copy_turned(act, copy, s, 0, 0, 0, "turn_act")
            with act.Fori(0, NE // UNROLL) as u:
                for j in range(UNROLL):
                    e = u * UNROLL + j
                    sigmoid(act, s, e, j)
                    copy_turned(act, copy, s, e + 1, 1 - j, 0, "turn_act")
                    act.wait_ge(s["y_stored"], 16 * e)
                    copy_y(act, copy, s, e, j, 0, "y_act")

            def work(n):
                copy_turned(act, copy, o, n, 0, 0, "turn_act")
                sigmoid(act, o, n, 0)
                act.wait_ge(o["y_stored"], 16 * n)
                copy_y(act, copy, o, n, 0, 0, "y_act")

            overflow(act, work)

        @block.tensor
        def _(pe):
            pe.wait_ge(s["const_in"], 16)
            turn(pe, s, 0, 0, 0)
            with pe.Fori(0, NE // UNROLL) as u:
                for j in range(UNROLL):
                    e = u * UNROLL + j
                    up(pe, s, e, j, u)
                    turn(pe, s, e + 1, 1 - j, u + j)
                    turn_mid(pe, s, e, j)
                    project(pe, s, e, j, u)

            def work(n):
                turn(pe, o, n, 0, n)
                up(pe, o, n, 0, n)
                turn_mid(pe, o, n, 0)
                project(pe, o, n, 0, n)

            overflow(pe, work)


def combine(nc, io, keep):
    with ExitStack() as c:
        sb = lambda n, s, d=F32: c.enter_context(nc.sbuf_tensor("g_" + n, s, d))
        sem = lambda n: c.enter_context(nc.semaphore("g_" + n))
        x = [sb(f"x{i}", [P, D]) for i in range(3)]
        ys = [[sb(f"y{i}_{k}", [P, D]) for k in range(2)] for i in range(3)]
        x_in = [sem(f"x_in{i}") for i in range(3)]
        y_in = [sem(f"y_in{i}") for i in range(3)]
        first_added, x_ready, stored = sem("first_added"), sem("x_ready"), sem("stored")
        route, row_of = keep["route"], keep["row_of"]
        y_rows = io["y_d"].rearrange("b p n -> (b p) n")
        block = c.enter_context(nc.Block())

        @block.sync
        def _(sp):
            for t in range(NT):
                if t >= 3:
                    sp.wait_ge(stored, 16 * (t - 2))
                sp.dma_start(x[t % 3][:], io["x2_d"][t]).then_inc(x_in[t % 3], 16)

        @block.gpsimd
        def _(pool):
            for t in range(NT):
                if t >= 3:
                    pool.wait_ge(x_ready, t - 2)
                for k in range(2):
                    pool.indirect_dma_start(ys[t % 3][k][:], None, y_rows,
                                            bass.IndirectOffsetOnAxis(ap=row_of[t][k][:, 0:1], axis=0)).then_inc(y_in[t % 3], 16)

        @block.vector
        def _(dve):
            for t in range(NT):
                dve.wait_ge(x_in[t % 3], 16 * (t // 3 + 1))
                dve.wait_ge(y_in[t % 3], 32 * (t // 3 + 1))
                w = route[:, t, 2 * NE + 4:]
                xt = x[t % 3]
                dve.scalar_tensor_tensor(xt[:], ys[t % 3][0][:], w[:, 0:1], xt[:], ALU.mult, ALU.add).then_inc(first_added, 1)
                dve.wait_ge(first_added, t + 1)
                dve.scalar_tensor_tensor(xt[:], ys[t % 3][1][:], w[:, 1:2], xt[:], ALU.mult, ALU.add).then_inc(x_ready, 1)

        @block.scalar
        def _(act):
            for t in range(NT):
                act.wait_ge(x_ready, t + 1)
                if t >= 1:
                    act.wait_ge(stored, 16 * t)
                act.dma_start(io["out"][t], x[t % 3][:]).then_inc(stored, 16)
            act.wait_ge(stored, 16 * NT)


def layer(nc, io):
    with ExitStack() as c:
        sb = lambda n, s, d=F32: c.enter_context(nc.sbuf_tensor(n, s, d))
        io["hold"] = c
        latents(nc, io)
        mixing(nc, io)
        attention(nc, io)
        keep = dict(
            run=sb("run", [P, NE]),
            route=sb("route", [P, NT, 2 * NE + 6]),
            row_of=[[sb(f"row_of{t}_{k}", [P, 1], I32) for k in range(2)] for t in range(NT)],
            plan=sb("plan", [P, OVERFLOW + 1], I32),
        )
        merge(nc, io, keep)
        slots(nc, io, keep)
        experts(nc, io, keep)
        combine(nc, io, keep)


def lay_out(inputs):
    import numpy as np
    i = {k: np.ascontiguousarray(v) for k, v in inputs.items()}
    x = np.zeros(((NT + 1) * P, D), np.float32)
    x[0:SEQ] = i["x_prompt"][0]
    x[SEQ:SEQ + DEC] = i["x_sample"][0]
    xT = np.ascontiguousarray(x.reshape(NT + 1, P, DC, P).transpose(0, 3, 2, 1))
    chunks = lambda w: np.ascontiguousarray(w.reshape(w.shape[0] // P, P, -1).transpose(1, 0, 2))
    w_in = i["w_in"][0]
    pos = np.concatenate([np.arange(SEQ), PAST + np.arange(P), np.arange(P)]).astype(np.float32)
    inv = (1.0 / (np.float32(10000.0) ** (np.arange(HALF, dtype=np.float32) * np.float32(2.0 / ROPE)))).astype(np.float32)
    ang = (pos[:, None] * inv[None, :]).astype(np.float32)
    trig = np.concatenate([np.cos(ang), np.sin(ang)], axis=1).astype(np.float32).reshape(NT + 1, P, ROPE)
    r, f = np.arange(P)[:, None], np.arange(P)[None, :]
    cols = lambda a: np.ascontiguousarray(a.reshape(-1, P).T)
    levels = np.zeros((6, P, P // 2), np.float32)
    for n in range(6):
        b = 2 << n
        of = 2 * b * (np.arange(P // 2) // b)
        levels[n] = (r // b * b == of[None, :] + b)
    state = i["state_wkv"][0, 0].reshape(PAIRS, 2, RH, RH)
    wkv0 = np.zeros((P, PAIRS, P), np.float32)
    for j in range(2):
        wkv0[RH * j:RH * j + RH, :, RH * j:RH * j + RH] = state[:, j].transpose(2, 0, 1)
    fixed = np.zeros((P, 2, NT, 2), np.float32)
    fixed[:, 0] = 1.0
    fixed[DEC:, 0, NT - 1] = 0.0
    for k in range(2):
        fixed[DEC:, 1, NT - 1, k] = np.arange(DEC, P) * (NE + OVERFLOW + 2) + NE + OVERFLOW + k
    experts_in = lambda w: np.ascontiguousarray(w.reshape(NE, w.shape[1] // P, P, w.shape[2]).transpose(0, 2, 1, 3))
    return dict(
        xT=xT, x=x[:NT * P].reshape(NT, P, D), trig=trig, ident=np.eye(P, dtype=np.float32),
        w_mla=chunks(np.ascontiguousarray(w_in[:, :MLA])),
        w_uq=chunks(i["w_uq"][0].reshape(QL, -1)), w_ukv=i["w_ukv"][0].reshape(KL, -1),
        norm_mix_g=np.ascontiguousarray(i["norm_mix_g"][0].reshape(DC, P).T),
        q_norm_g=i["q_norm_g"][0], kv_norm_g=i["kv_norm_g"][0],
        q_head_norm_g=i["q_head_norm_g"][0], k_head_norm_g=i["k_head_norm_g"][0],
        w_z=chunks(np.ascontiguousarray(w_in[:, MLA:MLA + ZC])),
        wa2=np.concatenate([i["rwkv_w2"][0], i["rwkv_a2"][0]], axis=0), g2=i["rwkv_g2"][0],
        vecs=np.ascontiguousarray(np.concatenate([cols(i[n][0]) for n in (
            "rwkv_mu", "rwkv_w0", "rwkv_a0", "rwkv_k_k", "rwkv_k_a", "rwkv_r_k")], axis=1)),
        rwkv_lnx_g=i["rwkv_lnx_g"][0], rwkv_lnx_b=i["rwkv_lnx_b"][0],
        same_head=(f // RH == r // RH).astype(np.float32),
        causal=np.concatenate([r < f, r <= f], axis=1).astype(np.float32),
        first=np.stack([(r == f + 1) & (f % 2 == 0), (f == r + 1) & (r % 2 == 0)], axis=1).astype(np.float32),
        merge_mask=np.ascontiguousarray(levels.transpose(1, 0, 2)),
        w_gates=chunks(np.ascontiguousarray(w_in[:, MLA + ZC:])), w_out=chunks(i["w_out"][0].reshape(2 * RD, D)),
        w_router=chunks(np.ascontiguousarray(np.concatenate(
            [i["w_router_group"][0], i["w_router_expert"][0].reshape(D, NE)], axis=1))),
        b_router=np.concatenate([i["b_router_group"][0], i["b_router_expert"][0].reshape(-1)]),
        norm_ffn_g=i["norm_ffn_g"][0], count_up=np.arange(NE, dtype=np.float32),
        real=(r < DEC).astype(np.float32), fixed=fixed,
        token=np.ascontiguousarray(np.arange(NT * P, dtype=np.int32).reshape(NT, P).T),
        w_gate_up=experts_in(np.concatenate([i["w_expert_gate"][0], i["w_expert_up"][0]], axis=2)),
        w_down=experts_in(i["w_expert_down"][0]),
        shift0=cols(i["state_shift"][0, 0]), wkv0=wkv0,
        past_lat=i["cache_kv_latent"][0, 0], past_kpe=i["cache_k_rope"][0, 0],
    )


OUTPUTS = dict(out=(NT, P, D), shift=(2, P, ZT), wkv=(2, P, PAIRS, P), lat=(NT, P, KL), kpe=(NT, P, ROPE))
SCRATCH = dict(x2_d=(NT, P, D), h2_d=(NT, P, D), y_d=(NE + OVERFLOW, P, D), oa_d=(NT, P, H, VD), ob_d=(NT, P, H, RH), hT_d=(NT + 1, P, DC, P), v_d=(NT + 1, P, H, VD), qT_d=(NT + 1, QK, H, P), kT_d=(NT + 1, QK, H, P))


def kernel(**inputs):
    import numpy as np
    import concourse.bacc as bacc
    from concourse.bass_utils import run_bass_kernel_spmd as run

    nc = bacc.Bacc("TRN2", target_bir_lowering=False, num_devices=1)
    arrays = lay_out(inputs)
    io = {n: nc.dram_tensor(n, a.shape, mybir.dt.from_np(a.dtype), kind="ExternalInput").ap() for n, a in arrays.items()}
    for n, s in OUTPUTS.items():
        io[n] = nc.dram_tensor(n, s, F32, kind="ExternalOutput").ap()
    for n, s in SCRATCH.items():
        io[n] = nc.dram_tensor(n, s, F32, kind="Internal").ap()
    io["table_d"] = nc.dram_tensor("table_d", (P * (NE + OVERFLOW + 2), 1), I32, kind="Internal").ap()
    layer(nc, io)
    got = run(nc, [arrays], core_ids=[0]).results[0]
    rows = {n: np.asarray(got[n]).reshape(NT * P, -1) for n in ("out", "lat", "kpe")}
    prompt, sample = slice(0, SEQ), slice(SEQ, SEQ + DEC)

    def state(g):
        s = np.asarray(got["wkv"])[g]
        heads = [s[RH * (h % 2):RH * (h % 2) + RH, h // 2, RH * (h % 2):RH * (h % 2) + RH].T for h in range(H)]
        return np.ascontiguousarray(np.stack(heads)[None, None])

    shift = lambda g: np.ascontiguousarray(np.asarray(got["shift"])[g].T).reshape(1, 1, 1, ZC)
    out = []
    for g, part in enumerate((prompt, sample)):
        out.append((rows["lat"][part][None, None], rows["kpe"][part][None, None], state(g), shift(g)))
    return (rows["out"][prompt][None], rows["out"][sample][None], *out[0], *out[1])
```

```python
import math
from contextlib import ExitStack

import concourse.bass as bass
from concourse import mybir

F32 = mybir.dt.float32
I32 = mybir.dt.int32
U32 = mybir.dt.uint32
ALU = mybir.AluOpType
ACT = mybir.ActivationFunctionType
AX = mybir.AxisListType.X

P = 128
D = 1024
DC = D // P
SEQ, DEC, PAST = 1024, 32, 128
NPT = SEQ // P
NT = NPT + 1
PAST_TILE = NT
EPS = 1e-6
H, NOPE, ROPE, VD = 8, 64, 32, 64
HALF = ROPE // 2
QK = NOPE + ROPE
QL, KL = 256, 128
MLA = QL + KL + ROPE
NEG = -1e30
HB = H // 2
RD, RH = 512, 64
ZC = 1792
ZT = ZC // P
W_LORA = 64
PAIRS = RD // P
KAPPA = 0.6065306597126334
CENTRE = 38.0
GN_EPS = 64e-5
NG, EPG, NE, FF = 4, 8, 32, 256
RT = NG + NE
CAP = P
OVERFLOW = 2 * (SEQ + DEC) // CAP
SLOTS = (NE + OVERFLOW) * CAP
DUMMY = 2 * P
BIG = 3.0e38


WB = 4


START = 1


class InOrder:

    def __init__(self, eng, sem):
        self.eng, self.sem, self.n = eng, sem, 0

    def __call__(self, ins):
        self.n += 1
        ins.then_inc(self.sem, 1)
        self.eng.wait_ge(self.sem, self.n)

    def lap(self):
        self.eng.sem_clear(self.sem)
        self.n = 0


def at(x, t):
    s = x[bass.ds(t, 1)]
    names = "bcdef"[:len(s.shape) - 2]
    return s.rearrange("o a " + " ".join(names) + " -> (o a) " + " ".join(names))


def goes_on(eng, sem):
    eng.sem_inc(sem, 1)


def prime(nc, sems):
    with nc.Block() as block:
        @block.sync
        def _(sp):
            for s in sems:
                sp.sem_inc(s, START)


def give_back(nc, sems):
    with nc.Block() as block:
        @block.sync
        def _(sp):
            for s in sems:
                sp.sem_clear(s)


def spread(ap, shape):
    return ap.broadcast_to(shape)


def tiles(eng, body, first, last):
    with eng.Fori(0, first) as t:
        body(t, False)
    for t in range(first, last):
        body(t, True)


def latents(nc, io):
    with ExitStack() as c:
        sb = lambda n, s: c.enter_context(nc.sbuf_tensor("a_" + n, s, F32))
        sems = []

        def sem(n):
            sems.append(c.enter_context(nc.semaphore("a_" + n)))
            return sems[-1]

        banks = [c.enter_context(nc.psum_tensor(f"a_ps{i}", [P, 512], F32)) for i in range(8)]
        w = sb("w", [P, DC, MLA])
        wq = sb("wq", [P, 2, H * QK])
        wkv = sb("wkv", [P, H * P])
        ident = sb("ident", [P, P])
        ones = sb("ones", [P, P])
        g_mix = sb("g_mix", [P, DC])
        g_lat = sb("g_lat", [P, QL + KL])
        g_head = sb("g_head", [P, 2, QK])
        xT = sb("xT", [P, DC, P])
        sq = sb("sq", [P, DC, P])
        hT = sb("hT", [P, DC, P])
        rb = sb("rb", [P, P])
        trigs = sb("trigs", [P, NT + 1, ROPE])
        trig = sb("trig", [P, ROPE])
        p1 = sb("p1", [P, MLA])
        p1sq = sb("p1sq", [P, QL])
        ms = sb("ms", [P, 2])
        cn = sb("cn", [P, QL + KL])
        kpe = sb("kpe", [P, ROPE])
        rt = sb("rt", [P, 4, H, HALF])
        rk = sb("rk", [P, 4, HALF])
        cT = sb("cT", [P, 3, P])
        qk = sb("qk", [P, 2 * H, QK])
        qksq = sb("qksq", [P, 2 * H, QK])
        hms = sb("hms", [P, 2 * H])
        v = sb("v", [P, H, VD])
        qkT = sb("qkT", [QK, 2 * H, P])
        consts_in, x_in, past_in = sem("consts_in"), sem("x_in"), sem("past_in")
        ones_set, dve_step, act_step = sem("ones_set"), sem("dve_step"), sem("act_step")
        sq_ready, ssq_done, ms_ready, rms_root, xg_done, h_ready = (sem(n) for n in (
            "sq_ready", "ssq_done", "ms_ready", "rms_root", "xg_done", "h_ready"))
        p1_done, p1_copied, lat_ss, lat_ms, lat_root, c_ready = (sem(n) for n in (
            "p1_done", "p1_copied", "lat_ss", "lat_ms", "lat_root", "c_ready"))
        cT_done, cT_copied, qkv_done, qkv_copied, head_ms, head_root, qk_ready = (sem(n) for n in (
            "cT_done", "cT_copied", "qkv_done", "qkv_copied", "head_ms", "head_root", "qk_ready"))
        qkT_done, qkT_copied = sem("qkT_done"), sem("qkT_copied")
        h_stored, lat_stored, v_stored, qk_stored = sem("h_stored"), sem("lat_stored"), sem("v_stored"), sem("qk_stored")
        NTILE = NT + 1
        c.callback(give_back, nc, sems)
        prime(nc, [s for s in sems if not s.name.endswith("_step")])
        block = c.enter_context(nc.Block())

        @block.sync
        def _(sp):
            for dst, src in ((w[:], io["w_mla"]), (wq[:], io["w_uq"]), (wkv[:], io["w_ukv"]),
                             (ident[:], io["ident"]), (g_mix[:], io["norm_mix_g"]),
                             (trigs[:], io["trig"].rearrange("t p n -> p t n")),
                             (g_lat[:, 0:QL], io["q_norm_g"].partition_broadcast(P)),
                             (g_lat[:, QL:], io["kv_norm_g"].partition_broadcast(P)),
                             (g_head[:, 0, :], io["q_head_norm_g"].partition_broadcast(P)),
                             (g_head[:, 1, :], io["k_head_norm_g"].partition_broadcast(P))):
                sp.dma_start(dst, src).then_inc(consts_in, 16)
            sp.dma_start(xT[:], io["xT"][0]).then_inc(x_in, 16)

            def body(t, last):
                sp.wait_ge(h_ready, t + 1 + START)
                sp.dma_start(at(io["hT_d"], t), hT[:]).then_inc(h_stored, 16)
                if not (last and t == PAST_TILE):
                    sp.wait_ge(xg_done, t + 1 + START)
                    sp.dma_start(xT[:], at(io["xT"], t + 1)).then_inc(x_in, 16)
                    sp.wait_ge(c_ready, t + 1 + START)
                    sp.dma_start(at(io["lat"], t), cn[:, QL:]).then_inc(lat_stored, 16)
                    sp.dma_start(at(io["kpe"], t), kpe[:]).then_inc(lat_stored, 16)
                else:
                    sp.wait_ge(cT_done, t + START)
                    sp.wait_ge(lat_stored, 32 * t + START)
                    sp.wait_ge(qk_ready, t + START)
                    sp.dma_start(cn[:, QL:], io["past_lat"]).then_inc(past_in, 16)
                    sp.dma_start(kpe[:], io["past_kpe"]).then_inc(past_in, 16)
                sp.wait_ge(qkv_copied, t + 1 + START)
                sp.dma_start(at(io["v_d"], t), v[:]).then_inc(v_stored, 16)
                sp.wait_ge(qkT_copied, 4 * (t + 1) + START)
                sp.dma_start(at(io["qT_d"], t), qkT[:, 0:H, :]).then_inc(qk_stored, 16)
                sp.dma_start(at(io["kT_d"], t), qkT[:, H:, :]).then_inc(qk_stored, 16)

            tiles(sp, body, NPT, NTILE)
            sp.wait_ge(h_stored, 16 * NTILE + START)
            sp.wait_ge(lat_stored, 32 * NT + START)
            sp.wait_ge(v_stored, 16 * NTILE + START)
            sp.wait_ge(qk_stored, 32 * NTILE + START)

        @block.gpsimd
        def _(pool):
            pool.memset(ones[:], 1.0).then_inc(ones_set, 1)

        @block.vector
        def _(dve):
            step = InOrder(dve, dve_step)
            dve.wait_ge(consts_in, 16 * 10 + START)
            dve.wait_ge(ones_set, 1 + START)
            step(dve.tensor_scalar(g_head[:, 0, :], g_head[:, 0, :], QK ** -0.5, None, ALU.mult))
            step.lap()

            def front(t):
                dve.wait_ge(x_in, 16 * (t + 1) + START)
                dve.wait_ge(ssq_done, t + START)
                dve.tensor_tensor(sq[:], xT[:], xT[:], ALU.mult).then_inc(sq_ready, 1)
                dve.wait_ge(p1_done, t + START)
                dve.wait_ge(h_stored, 16 * t + START)
                dve.tensor_tensor(hT[:], xT[:], spread(g_mix[:].unsqueeze(2), [P, DC, P]),
                                  ALU.mult).then_inc(xg_done, 1)
                dve.wait_ge(ssq_done, t + 1 + START)
                dve.tensor_scalar(rb[:], banks[0][:, 0:P], 1.0 / D, EPS, ALU.mult, ALU.add).then_inc(ms_ready, 1)
                dve.wait_ge(rms_root, t + 1 + START)
                step(dve.reciprocal(rb[:], rb[:]))
                dve.wait_ge(xg_done, t + 1 + START)
                dve.tensor_tensor(hT[:], hT[:], spread(rb[:].unsqueeze(1), [P, DC, P]),
                                  ALU.mult).then_inc(h_ready, 1)

            def latent_squares(t):
                dve.wait_ge(lat_ss, 2 * (t + 1) + START)
                step(dve.tensor_scalar(ms[:, 0:1], ms[:, 0:1], 1.0 / QL, EPS, ALU.mult, ALU.add))
                dve.tensor_scalar(ms[:, 1:2], ms[:, 1:2], 1.0 / KL, EPS, ALU.mult, ALU.add).then_inc(lat_ms, 1)

            def body(t, last):
                past = last and t == PAST_TILE
                step.lap()
                dve.wait_ge(lat_root, t + 1 + START)
                step(dve.reciprocal(ms[:], ms[:]))
                step(dve.tensor_copy(trig[:], trigs[:, bass.ds(t, 1), :].rearrange("p o n -> p (o n)")))
                dve.wait_ge(cT_done, t + START)
                cos, sin = trig[:, 0:HALF], trig[:, HALF:]
                if past:
                    dve.wait_ge(past_in, 32 + START)
                    dve.scalar_tensor_tensor(cn[:, 0:QL], p1[:, 0:QL], ms[:, 0:1], g_lat[:, 0:QL], ALU.mult, ALU.mult).then_inc(c_ready, 1)
                else:
                    dve.wait_ge(lat_stored, 32 * t + START)
                    dve.scalar_tensor_tensor(cn[:, 0:QL], p1[:, 0:QL], ms[:, 0:1], g_lat[:, 0:QL], ALU.mult, ALU.mult)
                    step(dve.scalar_tensor_tensor(cn[:, QL:], p1[:, QL:QL + KL], ms[:, 1:2], g_lat[:, QL:], ALU.mult, ALU.mult))
                    x1, x2 = p1[:, QL + KL:QL + KL + HALF], p1[:, QL + KL + HALF:]
                    for n, (a, b) in enumerate(((x1, cos), (x2, sin), (x1, sin), (x2, cos))):
                        ins = dve.tensor_tensor(rk[:, n, :], a, b, ALU.mult)
                    step(ins)
                    dve.tensor_tensor(kpe[:, 0:HALF], rk[:, 0, :], rk[:, 1, :], ALU.subtract)
                    dve.tensor_tensor(kpe[:, HALF:], rk[:, 2, :], rk[:, 3, :], ALU.add).then_inc(c_ready, 1)
                if not past:
                    front(t + 1)
                dve.wait_ge(c_ready, t + 1 + START)
                dve.wait_ge(qkv_copied, t + 1 + START)
                dve.tensor_copy(qk[:, H:, NOPE:], spread(kpe[:].unsqueeze(1), [P, H, ROPE]))
                cos8, sin8 = (spread(a.unsqueeze(1), [P, H, HALF]) for a in (cos, sin))
                x1, x2 = qk[:, 0:H, NOPE:NOPE + HALF], qk[:, 0:H, NOPE + HALF:]
                for n, (a, b) in enumerate(((x1, cos8), (x2, sin8), (x1, sin8), (x2, cos8))):
                    ins = dve.tensor_tensor(rt[:, n], a, b, ALU.mult)
                step(ins)
                dve.tensor_tensor(x1, rt[:, 0], rt[:, 1], ALU.subtract)
                step(dve.tensor_tensor(x2, rt[:, 2], rt[:, 3], ALU.add))
                step(dve.tensor_tensor(qksq[:], qk[:], qk[:], ALU.mult))
                step(dve.tensor_reduce(hms[:], qksq[:], AX, ALU.add))
                dve.tensor_scalar(hms[:], hms[:], 1.0 / QK, EPS, ALU.mult, ALU.add).then_inc(head_ms, 1)
                dve.wait_ge(head_root, t + 1 + START)
                step(dve.reciprocal(hms[:], hms[:]))
                step(dve.tensor_tensor(qksq[:], qk[:], spread(hms[:].unsqueeze(2), [P, 2 * H, QK]), ALU.mult))
                dve.tensor_tensor(qk[:, 0:H], qksq[:, 0:H], spread(g_head[:, 0:1], [P, H, QK]), ALU.mult)
                dve.tensor_tensor(qk[:, H:], qksq[:, H:], spread(g_head[:, 1:2], [P, H, QK]),
                                  ALU.mult).then_inc(qk_ready, 1)
                if not past:
                    latent_squares(t + 1)

            front(0)
            latent_squares(0)
            tiles(dve, body, NPT, NTILE)

        @block.scalar
        def _(act):
            def root(t):
                act.wait_ge(ms_ready, t + 1 + START)
                act.activation(rb[:], rb[:], ACT.Sqrt).then_inc(rms_root, 1)

            def latents_out(t):
                act.wait_ge(p1_done, t + 1 + START)
                act.wait_ge(c_ready, t + START)
                act.activation(p1[:], banks[1][:, 0:MLA], ACT.Copy).then_inc(p1_copied, 1)
                act.wait_ge(p1_copied, t + 1 + START)
                act.wait_ge(lat_ss, 2 * t + START)
                act.activation(p1sq[:], p1[:, 0:QL], ACT.Square, accum_out=ms[:, 0:1]).then_inc(lat_ss, 1)
                act.wait_ge(lat_ss, 2 * t + 1 + START)
                act.activation(p1sq[:, 0:KL], p1[:, QL:QL + KL], ACT.Square, accum_out=ms[:, 1:2]).then_inc(lat_ss, 1)

            def latent_root(t):
                act.wait_ge(lat_ms, t + 1 + START)
                act.activation(ms[:], ms[:], ACT.Sqrt).then_inc(lat_root, 1)

            def body(t, last):
                past = last and t == PAST_TILE
                act.wait_ge(cT_done, t + 1 + START)
                act.activation(cT[:], banks[2][:, 0:3 * P], ACT.Copy).then_inc(cT_copied, 1)
                if not past:
                    root(t + 1)
                act.wait_ge(qkv_done, t + 1 + START)
                act.wait_ge(qkT_done, 4 * t + START)
                act.wait_ge(v_stored, 16 * t + START)
                for n in range(2):
                    heads = slice(HB * n, HB * n + HB)
                    act.activation(qk[:, heads, :], banks[3 + n][:, 0:HB * QK], ACT.Copy)
                    kv = banks[5 + n][:].rearrange("p (h d) -> p h d", h=HB)
                    act.activation(qk[:, H + HB * n:H + HB * n + HB, 0:NOPE], kv[:, :, 0:NOPE], ACT.Copy)
                    ins = act.activation(v[:, heads, :], kv[:, :, NOPE:], ACT.Copy)
                ins.then_inc(qkv_copied, 1)
                if not past:
                    latents_out(t + 1)
                act.wait_ge(head_ms, t + 1 + START)
                act.activation(hms[:], hms[:], ACT.Sqrt).then_inc(head_root, 1)
                act.wait_ge(qk_stored, 32 * t + START)
                for n, b in enumerate((7, 2, 3, 4)):
                    act.wait_ge(qkT_done, 4 * t + n + 1 + START)
                    act.activation(qkT[:, 4 * n:4 * n + 4, :], banks[b][0:QK, :], ACT.Copy).then_inc(qkT_copied, 1)
                if not past:
                    latent_root(t + 1)

            root(0)
            latents_out(0)
            latent_root(0)
            tiles(act, body, NPT, NTILE)

        @block.tensor
        def _(pe):
            pe.wait_ge(consts_in, 16 * 10 + START)
            pe.wait_ge(ones_set, 1 + START)

            def squares(t):
                pe.wait_ge(sq_ready, t + 1 + START)
                pe.wait_ge(ms_ready, t + START)
                for k in range(DC):
                    mm = pe.matmul(banks[0][:, 0:P], ones[:], sq[:, k, :], start=(k == 0), stop=(k == DC - 1))
                mm.then_inc(ssq_done, 1)

            def project(t):
                pe.wait_ge(h_ready, t + 1 + START)
                pe.wait_ge(p1_copied, t + START)
                for k in range(DC):
                    mm = pe.matmul(banks[1][:, 0:MLA], hT[:, k, :], w[:, k, :], start=(k == 0), stop=(k == DC - 1))
                mm.then_inc(p1_done, 1)

            def body(t, last):
                past = last and t == PAST_TILE
                pe.wait_ge(c_ready, t + 1 + START)
                pe.wait_ge(qkT_copied, 4 * t + START)
                for n in range(3):
                    mm = pe.transpose(banks[2][:, n * P:(n + 1) * P], cn[:, n * P:(n + 1) * P], ident[:])
                mm.then_inc(cT_done, 1)
                if not past:
                    squares(t + 1)
                pe.wait_ge(cT_copied, t + 1 + START)
                pe.wait_ge(qkv_copied, t + START)
                for n in range(2):
                    for k in range(2):
                        pe.matmul(banks[3 + n][:, 0:HB * QK], cT[:, k, :], wq[:, k, n * HB * QK:(n + 1) * HB * QK],
                                  start=(k == 0), stop=(k == 1))
                    mm = pe.matmul(banks[5 + n][:], cT[:, 2, :], wkv[:, n * 512:(n + 1) * 512], start=True, stop=True)
                mm.then_inc(qkv_done, 1)
                if not past:
                    project(t + 1)
                pe.wait_ge(qk_ready, t + 1 + START)
                for n, b in enumerate((7, 2, 3, 4)):
                    for j in range(4):
                        mm = pe.transpose(banks[b][0:QK, j * P:(j + 1) * P], qk[:, 4 * n + j, :], ident[:])
                    mm.then_inc(qkT_done, 1)

            squares(0)
            project(0)
            tiles(pe, body, NPT, NTILE)


def mixing(nc, io):
    LEVELS = (2, 4, 8, 16, 32, 64)
    NL = len(LEVELS)
    GROUPS = -(-ZT // 4)
    with ExitStack() as c:
        sb = lambda n, s: c.enter_context(nc.sbuf_tensor("b_" + n, s, F32))
        sems = []

        def sem(n):
            sems.append(c.enter_context(nc.semaphore("b_" + n)))
            return sems[-1]

        banks = [c.enter_context(nc.psum_tensor(f"b_ps{i}", [P, 512], F32)) for i in range(8)]
        paired = lambda i: banks[i][:].rearrange("p (a b) -> p a b", a=PAIRS)
        wz = sb("wz", [P, DC, ZC])
        wa2 = sb("wa2", [P, RD])
        g2 = sb("g2", [P, RD])
        ident = sb("ident", [P, P])
        vecs = sb("vecs", [P, ZT + 5 * PAIRS])
        mu = vecs[:, 0:ZT]
        w0, a0, k_k, k_a, r_k = (vecs[:, ZT + PAIRS * n:ZT + PAIRS * (n + 1)] for n in range(5))
        ln = sb("ln", [P, 2, RD])
        same_head = sb("same_head", [P, P])
        causal = sb("causal", [P, 2 * P])
        first = sb("first", [P, 2, P])
        merge_mask = sb("merge_mask", [P, NL, P // 2])
        hT = sb("hT", [P, DC, P])
        z = sb("z", [P, ZT, P + 1])
        zlast = sb("zlast", [P, 2, ZT])
        shift_in = sb("shift_in", [P, ZT])
        zm = sb("zm", [P, ZT, P])
        la = sb("la", [P, P])
        sg = sb("sg", [P, P])
        kk = sb("kk", [P, PAIRS, P])
        kn = sb("kn", [P, PAIRS, P])
        sig = sb("sig", [P, PAIRS, P])
        av = sb("av", [P, PAIRS, P])
        cs = sb("cs", [P, PAIRS, P])
        csm = sig
        one = sb("one", [P, P])
        bias = sb("bias", [P, 2])
        eW = sb("eW", [P, PAIRS, P])
        wc = sb("wc", [P, PAIRS])
        k2 = sb("k2", [P, PAIRS, P])
        art = [sb(f"art{j}", [P, PAIRS, 2 * P]) for j in range(2)]
        bt = sb("bt", [P, PAIRS, P])
        kt = sb("kt", [P, PAIRS, P])
        rkk = kn
        tok = [sb(f"tok{j}", [P, 3, RD]) for j in range(2)]
        bon = [sb(f"bon{j}", [P, H]) for j in range(2)]
        gs = [sb(f"gs{j}", [P, RD]) for j in range(2)]
        M = sb("M", [P, H, 2, 2 * P])
        T = sb("T", [P, H, P])
        U = sb("U", [P, H, P])
        L = [sb(f"L{n}", [P, H, P]) for n in range(NL)]
        X = sb("X", [P, RD])
        W = sb("W", [P, RD])
        S = sb("S", [P, PAIRS, P])
        state_given = sb("state_given", [P, PAIRS, P])
        grown = sb("grown", [P, PAIRS, P])
        y = sb("y", [P, H, RH])
        normed = sb("normed", [P, RD])
        st = sb("st", [P, 2, H])
        (consts_in, h_in, set_done, carry_set, z_done, z_copied, zm_ready, lora_in, kk_sq, lora_done, gate_done, gate_copied,
         w_sum, w_sig, a_sum, a_sig, nn_ready, nn_root, cs_ready, e_ready, e_used, feats_ready, tok_done, tok_copied, wc_ready,
         gram_done, gram_copied, T_ready, low_done, low_copied, merge_done, merged, x_done, x_copied, w_done, w_copied,
         y_done, y_copied, d_done, s_ready, v_ready, v_root, out_ready, ob_stored, state_out, state_stored, dve_step) = (
            sem(n) for n in (
                "consts_in h_in set_done carry_set z_done z_copied zm_ready lora_in kk_sq lora_done gate_done gate_copied "
                "w_sum w_sig a_sum a_sig nn_ready nn_root cs_ready e_ready e_used feats_ready tok_done tok_copied wc_ready "
                "gram_done gram_copied T_ready low_done low_copied merge_done merged x_done x_copied w_done w_copied "
                "y_done y_copied d_done s_ready v_ready v_root out_ready ob_stored state_out state_stored dve_step").split())
        c.callback(give_back, nc, sems)
        prime(nc, [s for s in sems if not s.name.endswith("_step")])
        block = c.enter_context(nc.Block())
        CONSTS = 13

        EARLY = 3

        def chunks(eng, body):
            with eng.Fori(0, (NT - 3) // 2) as u:
                for j in range(2):
                    body(u * 2 + j, j)
            for t in range(NT - 3, NT):
                body(t, t % 2)

        there = lambda t, ahead: not isinstance(t, int) or t + ahead < NT

        @block.sync
        def _(sp):
            loads = ((wz[:], io["w_z"]), (wa2[:], io["wa2"]), (g2[:], io["g2"]), (ident[:], io["ident"]),
                     (vecs[:], io["vecs"]), (ln[:, 0, :], io["rwkv_lnx_g"].partition_broadcast(P)),
                     (ln[:, 1, :], io["rwkv_lnx_b"].partition_broadcast(P)), (same_head[:], io["same_head"]),
                     (causal[:], io["causal"]), (first[:], io["first"]), (merge_mask[:], io["merge_mask"]),
                     (shift_in[:], io["shift0"]), (state_given[:], io["wkv0"]))
            for dst, src in loads:
                sp.dma_start(dst, src).then_inc(consts_in, 16)

            def load(t):
                sp.wait_ge(z_done, GROUPS * t + START)
                sp.dma_start(hT[:], at(io["hT_d"], t)).then_inc(h_in, 16)

            def body(t, b):
                if there(t, 3):
                    load(t + 3)
                if not there(t, 1):
                    sp.wait_ge(state_out, 1 + START)
                    sp.dma_start(io["shift"][0], zlast[:, 0, :]).then_inc(state_stored, 16)
                    sp.dma_start(io["wkv"][0], grown[:]).then_inc(state_stored, 16)
                sp.wait_ge(out_ready, t + 1 + START)
                sp.dma_start(at(io["ob_d"], t), y[:]).then_inc(ob_stored, 16)

            load(0)
            load(1)
            load(2)
            chunks(sp, body)
            sp.wait_ge(state_out, 2 + START)
            sp.dma_start(io["shift"][1], zlast[:, 1, :]).then_inc(state_stored, 16)
            sp.dma_start(io["wkv"][1], grown[:]).then_inc(state_stored, 16)
            sp.wait_ge(state_stored, 64 + START)
            sp.wait_ge(ob_stored, 16 * NT + START)

        @block.gpsimd
        def _(pool):
            for n in range(NL):
                pool.memset(L[n][:], 0.0)
            pool.memset(one[:], 1.0)
            pool.memset(bias[:, 0:1], CENTRE)
            pool.memset(bias[:, 1:2], -CENTRE)
            pool.memset(z[:, :, 0:1], 0.0)
            pool.memset(S[:], 0.0).then_inc(set_done, 1)

        @block.vector
        def _(dve):
            step = InOrder(dve, dve_step)
            dve.wait_ge(consts_in, 16 * CONSTS + START)
            dve.wait_ge(set_done, 1 + START)
            col = lambda a, n: spread(a.unsqueeze(2), [P, n, P])
            r, k = zm[:, 0:PAIRS], zm[:, PAIRS:2 * PAIRS]

            def shift_a(n):
                dve.wait_ge(z_copied, GROUPS * (n + 1) + START)
                step(dve.tensor_tensor(zm[:], z[:, :, 0:P], z[:, :, 1:], ALU.subtract))

            def shift_b(n):
                step(dve.tensor_tensor(zm[:], zm[:], col(mu, ZT), ALU.mult))

            def shift_c(n, carry):
                dve.tensor_tensor(zm[:], zm[:], z[:, :, 1:], ALU.add).then_inc(zm_ready, 1)
                dve.wait_ge(zm_ready, n + 1 + START)
                if carry == "rows":
                    dve.tensor_copy(z[:, :, 0:1], z[:, :, P:]).then_inc(carry_set, 1)
                elif carry == "sample":
                    dve.tensor_copy(zlast[:, 0, :], z[:, :, P])
                    dve.tensor_copy(z[:, :, 0], shift_in[:]).then_inc(carry_set, 1)
                else:
                    dve.tensor_copy(zlast[:, 1, :], z[:, :, DEC])

            def keys_squared(n):
                step(dve.tensor_tensor(kk[:], k, col(k_k, PAIRS), ALU.mult))
                dve.tensor_tensor(kn[:], kk[:], kk[:], ALU.mult).then_inc(kk_sq, 1)

            def sums(n):
                dve.wait_ge(lora_done, n + 1 + START)
                dve.tensor_tensor(sig[:], paired(3), col(w0, PAIRS), ALU.add).then_inc(w_sum, 1)
                dve.tensor_tensor(av[:], paired(4), col(a0, PAIRS), ALU.add).then_inc(a_sum, 1)
                dve.tensor_scalar(kn[:], paired(5), 1e-24, None, ALU.max).then_inc(nn_ready, 1)

            def decays(n):
                dve.wait_ge(w_sig, n + 1 + START)
                for p in range(PAIRS):
                    ins = dve.tensor_tensor_scan(cs[:, p, :], one[:], sig[:, p, :], 0.0, ALU.mult, ALU.add)
                step(ins)
                dve.tensor_tensor(csm[:], cs[:], sig[:], ALU.subtract).then_inc(cs_ready, 1)

            def keys(n):
                dve.wait_ge(nn_root, n + 1 + START)
                step(dve.reciprocal(kn[:], kn[:]))
                step(dve.tensor_tensor(kk[:], kk[:], kn[:], ALU.mult))

            def keys_mixed(n):
                dve.wait_ge(a_sig, n + 1 + START)
                step(dve.scalar_tensor_tensor(k2[:], av[:], 1.0, col(k_a, PAIRS), ALU.subtract, ALU.mult))
                step(dve.scalar_tensor_tensor(k2[:], k2[:], 1.0, k, ALU.add, ALU.mult))

            def scaled_inverse(n):
                step(dve.tensor_tensor(av[:], kk[:], av[:], ALU.mult))
                dve.wait_ge(e_ready, 3 * n + 1 + START)
                dve.tensor_tensor(bt[:], av[:], eW[:], ALU.mult)
                dve.tensor_tensor(kt[:], k2[:], eW[:], ALU.mult).then_inc(e_used, 1)
                step(dve.tensor_tensor(rkk[:], r, k2[:], ALU.mult))
                step(dve.tensor_tensor(rkk[:], rkk[:], col(r_k, PAIRS), ALU.mult))

            def scaled_a(n, b):
                dve.wait_ge(e_ready, 3 * n + 2 + START)
                dve.scalar_tensor_tensor(art[b][:, :, 0:P], kk[:], -1.0, eW[:], ALU.mult, ALU.mult).then_inc(e_used, 1)

            def scaled_r(n, b):
                dve.wait_ge(e_ready, 3 * n + 3 + START)
                dve.wait_ge(e_used, 3 * n + 2 + START)
                dve.tensor_tensor(art[b][:, :, P:], r, eW[:], ALU.mult).then_inc(e_used, 1)
                dve.wait_ge(e_used, 3 * n + 3 + START)
                dve.sem_inc(feats_ready, 1)

            def products(n):
                for p in range(PAIRS):
                    dve.wait_ge(gram_done, PAIRS * n + p + 1 + START)
                    for j in range(2):
                        bank = banks[((3, 4), (5, 0))[p % 2][j]]
                        ins = dve.tensor_tensor(M[:, 2 * p + j], bank[:].rearrange("p (a b) -> p a b", a=2),
                                                spread(causal[:].unsqueeze(1), [P, 2, 2 * P]), ALU.mult)
                    ins.then_inc(gram_copied, 1)
                for j in range(2):
                    step(dve.tensor_tensor(T[:, j:H:2, :], paired(6 + j), spread(first[:, 0:1, :], [P, PAIRS, P]), ALU.mult))
                dve.wait_ge(gram_copied, PAIRS * (n + 1) + START)
                dve.tensor_tensor(T[:], T[:], spread(ident[:].unsqueeze(1), [P, H, P]), ALU.add).then_inc(T_ready, 1)
                step(dve.tensor_tensor(U[:], M[:, :, 0, 0:P], spread(first[:, 1:2, :], [P, H, P]), ALU.mult))
                dve.tensor_tensor(U[:], U[:], spread(ident[:].unsqueeze(1), [P, H, P]), ALU.add).then_inc(T_ready, 1)

            def next_state(t):
                dve.wait_ge(d_done, t + 1 + START)
                if not there(t, 1):
                    dve.wait_ge(state_stored, 32 + START)
                step(dve.tensor_tensor(grown[:], paired(2), spread(same_head[:].unsqueeze(1), [P, PAIRS, P]), ALU.mult))
                step(dve.tensor_tensor(grown[:], grown[:], S[:], ALU.add))
                dve.wait_ge(wc_ready, t + 1 + START)
                ins = dve.tensor_tensor(S[:], grown[:], col(wc[:], PAIRS), ALU.mult)
                if there(t, 1) and not there(t, 2):
                    step(ins)
                    dve.tensor_scalar(grown[:], S[:], float(math.exp(CENTRE)), None, ALU.mult).then_inc(state_out, 1)
                    dve.wait_ge(state_out, 1 + START)
                    ins = dve.tensor_scalar(S[:], state_given[:], float(math.exp(-CENTRE)), None, ALU.mult)
                ins.then_inc(s_ready, 1)

            def finish(t, b):
                dve.wait_ge(y_copied, t + 1 + START)
                heads = lambda a: spread(a.unsqueeze(2), [P, H, RH])
                xh = normed[:].rearrange("p (h d) -> p h d", h=H)
                step(dve.tensor_reduce(st[:, 0], y[:], AX, ALU.add))
                step(dve.tensor_scalar(st[:, 0], st[:, 0], 1.0 / RH, None, ALU.mult))
                step(dve.tensor_tensor(y[:], y[:], heads(st[:, 0]), ALU.subtract))
                step(dve.tensor_tensor(xh, y[:], y[:], ALU.mult))
                step(dve.tensor_reduce(st[:, 1], xh, AX, ALU.add))
                dve.tensor_scalar(st[:, 1], st[:, 1], 1.0 / RH, GN_EPS, ALU.mult, ALU.add).then_inc(v_ready, 1)
                vt = tok[b][:, 2, :].rearrange("p (h d) -> p h d", h=H)
                step(dve.tensor_tensor(xh, vt, heads(bon[b][:]), ALU.mult))
                step(dve.tensor_tensor(normed[:], normed[:], ln[:, 1, :], ALU.add))
                dve.wait_ge(v_root, t + 1 + START)
                step(dve.reciprocal(st[:, 1], st[:, 1]))
                step(dve.tensor_tensor(y[:], y[:], heads(st[:, 1]), ALU.mult))
                yf = y[:].rearrange("p h d -> p (h d)")
                step(dve.tensor_tensor(yf, yf, ln[:, 0, :], ALU.mult))
                step(dve.tensor_tensor(yf, yf, normed[:], ALU.add))
                dve.tensor_tensor(yf, yf, gs[b][:], ALU.mult).then_inc(out_ready, 1)

            def body(t, b):
                step.lap()
                n, nb = t + 1, 1 - b
                feats = there(t, 1)
                carry = "rows" if there(t, 3) else "sample" if there(t, 2) else "end"
                dve.wait_ge(T_ready, 2 * (t + 1) + START)
                between = {
                    (0, 0): lambda: shift_a(n), (0, 1): lambda: shift_b(n), (1, 0): lambda: shift_c(n, carry),
                    (1, 1): lambda: keys_squared(n), (2, 1): lambda: sums(n), (3, 0): lambda: decays(n),
                    (3, 1): lambda: keys(n), (4, 0): lambda: keys_mixed(n), (4, 1): lambda: scaled_inverse(n),
                    (5, 0): lambda: scaled_a(n, nb), (5, 1): lambda: scaled_r(n, nb),
                } if feats else {}
                for i, w in enumerate(LEVELS):
                    halves = lambda a: a[:].rearrange("p h (j e i) -> p h j e i", e=2, i=w)
                    flat = lambda q: banks[q][:].rearrange("p (h j i) -> p h j i", h=H, i=w)
                    dve.wait_ge(low_done, NL * t + i + 1 + START)
                    mask = merge_mask[:, i, :].rearrange("p (j i) -> p j i", i=w).unsqueeze(1)
                    dve.tensor_tensor(halves(L[i])[:, :, :, 0, :], flat(0), spread(mask, [P, H, P // (2 * w), w]),
                                      ALU.mult).then_inc(low_copied, 1)
                    between.get((i, 0), lambda: None)()
                    dve.wait_ge(merge_done, NL * t + i + 1 + START)
                    if i < NL - 1:
                        dve.tensor_tensor(halves(T)[:, :, :, 0, :], halves(T)[:, :, :, 0, :], flat(1), ALU.add)
                    dve.tensor_tensor(halves(U)[:, :, :, 1, :], halves(U)[:, :, :, 1, :], flat(2), ALU.add).then_inc(merged, 1)
                    dve.wait_ge(merged, NL * t + i + 1 + START)
                    between.get((i, 1), lambda: None)()
                next_state(t)
                if feats:
                    products(n)
                finish(t, b)

            dve.sem_inc(carry_set, 1)
            shift_a(0)
            shift_b(0)
            shift_c(0, "rows")
            keys_squared(0)
            sums(0)
            decays(0)
            keys(0)
            keys_mixed(0)
            scaled_inverse(0)
            scaled_a(0, 0)
            scaled_r(0, 0)
            products(0)
            chunks(dve, body)
            dve.wait_ge(s_ready, NT + START)
            dve.tensor_scalar(grown[:], S[:], float(math.exp(CENTRE)), None, ALU.mult).then_inc(state_out, 1)

        @block.scalar
        def _(act):
            act.wait_ge(set_done, 1 + START)

            def copy_z(n, g):
                k = min(4, ZT - 4 * g)
                act.wait_ge(carry_set, n + 1 + START)
                act.wait_ge(z_done, GROUPS * n + g + 1 + START)
                act.activation(z[:, 4 * g:4 * g + k, 1:], banks[6 + g % 2][:, 0:k * P].rearrange("p (a b) -> p a b", a=k),
                               ACT.Copy).then_inc(z_copied, 1)

            def lora(n):
                act.wait_ge(zm_ready, n + 1 + START)
                act.activation(la[0:W_LORA, :], zm[0:W_LORA, 12, :], ACT.Tanh)
                act.activation(sg[:], zm[:, 13, :], ACT.Sigmoid).then_inc(lora_in, 1)

            def sigmoids(n):
                act.wait_ge(w_sum, n + 1 + START)
                act.activation(sig[:], sig[:], ACT.Sigmoid).then_inc(w_sig, 1)
                act.wait_ge(a_sum, n + 1 + START)
                act.activation(av[:], av[:], ACT.Sigmoid).then_inc(a_sig, 1)

            def key_root(n):
                act.wait_ge(nn_ready, n + 1 + START)
                act.activation(kn[:], kn[:], ACT.Sqrt).then_inc(nn_root, 1)

            def decay(n, m):
                src, b, sign = ((cs, 1, 1.0), (csm, 0, -1.0), (cs, 0, -1.0))[m]
                act.wait_ge(cs_ready, n + 1 + START)
                act.wait_ge(e_used, 3 * n + m + START)
                act.activation(eW[:], src[:], ACT.Exp, bias=bias[:, b:b + 1], scale=sign * KAPPA).then_inc(e_ready, 1)

            def chunk_decay(n, rows):
                act.wait_ge(cs_ready, n + 1 + START)
                act.wait_ge(s_ready, n + START)
                act.activation(wc[:], cs[:, :, rows - 1], ACT.Exp, scale=-KAPPA).then_inc(wc_ready, 1)

            def by_rows(n, b):
                act.wait_ge(gate_done, n + 1 + START)
                act.activation(gs[b][:], banks[3][:], ACT.Copy).then_inc(gate_copied, 1)
                act.wait_ge(tok_done, n + 1 + START)
                for q, bank in enumerate((4, 5, 7)):
                    act.activation(tok[b][:, q, :], banks[bank][:], ACT.Copy)
                act.activation(bon[b][:], banks[6][:, 0:H], ACT.Copy).then_inc(tok_copied, 1)

            def copy_x(n):
                act.wait_ge(x_done, n + 1 + START)
                act.activation(X[:], banks[3][:], ACT.Copy).then_inc(x_copied, 1)

            def body(t, b):
                n = t + 1
                feats, proj = there(t, 1), there(t, 2)
                if feats:
                    lora(n)
                if proj:
                    copy_z(n + 1, 0)
                if feats:
                    sigmoids(n)
                    key_root(n)
                if proj:
                    copy_z(n + 1, 1)
                if feats:
                    decay(n, 0)
                if proj:
                    copy_z(n + 1, 2)
                if feats:
                    decay(n, 1)
                if proj:
                    copy_z(n + 1, 3)
                if feats:
                    decay(n, 2)
                act.wait_ge(w_done, t + 1 + START)
                act.activation(W[:], banks[0][:], ACT.Copy).then_inc(w_copied, 1)
                if feats:
                    act.wait_ge(out_ready, t + START)
                    by_rows(n, 1 - b)
                act.wait_ge(y_done, t + 1 + START)
                act.wait_ge(ob_stored, 16 * t + START)
                act.activation(y[:], banks[1][:].rearrange("p (h d) -> p h d", h=H), ACT.Copy).then_inc(y_copied, 1)
                if feats:
                    chunk_decay(n, P if proj else DEC)
                    copy_x(n)
                act.wait_ge(v_ready, t + 1 + START)
                act.activation(st[:, 1], st[:, 1], ACT.Sqrt).then_inc(v_root, 1)

            for g in range(GROUPS):
                copy_z(0, g)
            lora(0)
            copy_z(1, 0)
            copy_z(1, 1)
            copy_z(1, 2)
            copy_z(1, 3)
            sigmoids(0)
            key_root(0)
            for m in range(3):
                decay(0, m)
            chunk_decay(0, P)
            by_rows(0, 0)
            copy_x(0)
            chunks(act, body)

        @block.tensor
        def _(pe):
            pe.wait_ge(consts_in, 16 * CONSTS + START)
            pe.wait_ge(set_done, 1 + START)

            def project(n, k):
                g = k // 4
                if k == 0:
                    pe.wait_ge(h_in, 16 * (n + 1) + START)
                    pe.wait_ge(z_copied, GROUPS * n + START)
                    if not isinstance(n, int) or n > 1:
                        pe.wait_ge(T_ready, 2 * (n - 2) + 1 + START)
                if k % 4 == 0 and g >= 2:
                    pe.wait_ge(z_copied, GROUPS * n + g - 1 + START)
                for i in range(DC):
                    mm = pe.matmul(banks[6 + g % 2][:, k % 4 * P:(k % 4 + 1) * P], wz[:, i, k * P:(k + 1) * P], hT[:, i, :],
                                   start=(i == 0), stop=(i == DC - 1))
                if k % 4 == 3 or k == ZT - 1:
                    mm.then_inc(z_done, 1)

            def lora(n):
                pe.wait_ge(lora_in, n + 1 + START)
                pe.wait_ge(x_copied, n + START)
                for p in range(PAIRS):
                    cols = slice(p * P, (p + 1) * P)
                    pe.matmul(banks[3][:, cols], wa2[0:W_LORA, cols], la[0:W_LORA, :], start=True, stop=True)
                    pe.matmul(banks[4][:, cols], wa2[W_LORA:, cols], zm[W_LORA:, 12, :], start=True, stop=True)
                pe.wait_ge(kk_sq, n + 1 + START)
                for p in range(PAIRS):
                    mm = pe.matmul(banks[5][:, p * P:(p + 1) * P], same_head[:], kn[:, p, :], start=True, stop=True)
                mm.then_inc(lora_done, 1)

            def gates(n):
                pe.wait_ge(w_sum, n + 1 + START)
                pe.matmul(banks[3][:], sg[:], g2[:], start=True, stop=True).then_inc(gate_done, 1)

            def by_rows(n, last_z):
                pe.wait_ge(feats_ready, n + 1 + START)
                pe.wait_ge(z_copied, last_z + START)
                for p in range(PAIRS):
                    cols = slice(p * P, (p + 1) * P)
                    pe.transpose(banks[4][:, cols], kt[:, p, :], ident[:])
                    pe.transpose(banks[5][:, cols], bt[:, p, :], ident[:])
                    pe.transpose(banks[7][:, cols], zm[:, 2 * PAIRS + p, :], ident[:])
                    mm = pe.matmul(banks[6][:, 2 * p:2 * p + 2], rkk[:, p, :], same_head[:, 0:P:RH], start=True, stop=True)
                mm.then_inc(tok_done, 1)

            def products(n, b):
                pe.wait_ge(gate_copied, n + 1 + START)
                pe.wait_ge(tok_copied, n + 1 + START)
                pe.wait_ge(w_copied, n + START)
                for p in range(PAIRS):
                    if p >= 2:
                        pe.wait_ge(gram_copied, PAIRS * n + p - 1 + START)
                    for j in range(2):
                        bank = banks[((3, 4), (5, 0))[p % 2][j]]
                        f = slice(RH * j, RH * j + RH)
                        pe.matmul(bank[:, 0:2 * P], bt[f, p, :], art[b][f, p, :], start=True, stop=True)
                        pe.matmul(bank[:, 2 * P:], kt[f, p, :], art[b][f, p, :], start=True, stop=True)
                        mm = pe.matmul(banks[6 + j][:, p * P:(p + 1) * P], art[b][f, p, 0:P], bt[f, p, :], start=True, stop=True)
                    mm.then_inc(gram_done, 1)

            def right_side(n, b):
                pe.wait_ge(gram_copied, PAIRS * (n + 1) + START)
                pe.wait_ge(s_ready, n + START)
                for p in range(PAIRS):
                    pe.matmul(banks[3][:, p * P:(p + 1) * P], art[b][:, p, 0:P], S[:, p, :], start=True, stop=False)
                    for h in (2 * p, 2 * p + 1):
                        cols = slice(h * RH, (h + 1) * RH)
                        mm = pe.matmul(banks[3][:, cols], M[:, h, 1, 0:P], tok[b][:, 2, cols], start=False, stop=(h % 2 == 1))
                mm.then_inc(x_done, 1)

            def begin(n, b):
                products(n, b)
                if there(n, 2):
                    project(n + 2, 0)
                right_side(n, b)
                for k in range(1, EARLY):
                    if there(n, 2):
                        project(n + 2, k)

            def body(t, b):
                n, nb = t + 1, 1 - b
                feats = there(t, 1)
                rows = P if feats else DEC
                tile = iter(range(EARLY, ZT if there(t, 2) else EARLY))

                def fill():
                    k = next(tile, None)
                    if k is not None:
                        project(t + 2, k)

                pe.wait_ge(T_ready, 2 * (t + 1) + START)
                pe.wait_ge(y_copied, t + START)
                pe.wait_ge(s_ready, t + START)
                for i, w in enumerate(LEVELS):
                    halves = lambda a, h: a[:, h, :].rearrange("p (j e i) -> p j e i", e=2, i=w)
                    if i > 0:
                        pe.wait_ge(merged, NL * t + i + START)
                    for h in range(H):
                        mm = pe.matmul(banks[0][:, h * RH:(h + 1) * RH], M[:, h, 0, 0:P], halves(T, h)[:, :, 0, :],
                                       start=True, stop=True)
                    mm.then_inc(low_done, 1)
                    fill()
                    if i == 2 and feats:
                        lora(n)
                    pe.wait_ge(low_copied, NL * t + i + 1 + START)
                    for h in range(H):
                        cols = slice(h * RH, (h + 1) * RH)
                        if i < NL - 1:
                            pe.matmul(banks[1][:, cols], U[:, h, :], halves(L[i], h)[:, :, 0, :], start=True, stop=True)
                        mm = pe.matmul(banks[2][:, cols], L[i][:, h, :], halves(U, h)[:, :, 1, :], start=True, stop=True)
                    mm.then_inc(merge_done, 1)
                    fill()
                pe.wait_ge(merged, NL * (t + 1) + START)
                for h in range(H):
                    cols = slice(h * RH, (h + 1) * RH)
                    mm = pe.matmul(banks[0][:, cols], U[:, h, :], X[:, cols], start=True, stop=True)
                mm.then_inc(w_done, 1)
                if feats:
                    gates(n)
                    by_rows(n, GROUPS * (t + 3) if there(t, 2) else GROUPS * NT)
                pe.wait_ge(w_copied, t + 1 + START)
                for p in range(PAIRS):
                    pe.matmul(banks[1][:, p * P:(p + 1) * P], art[b][:, p, P:], S[:, p, :], start=True, stop=False)
                    for h in (2 * p, 2 * p + 1):
                        cols = slice(h * RH, (h + 1) * RH)
                        pe.matmul(banks[1][:, cols], M[:, h, 0, P:], W[:, cols], start=False, stop=False)
                        mm = pe.matmul(banks[1][:, cols], M[:, h, 1, P:], tok[b][:, 2, cols], start=False, stop=(h % 2 == 1))
                mm.then_inc(y_done, 1)
                for p in range(PAIRS):
                    cols = slice(p * P, (p + 1) * P)
                    pe.matmul(banks[2][:, cols], tok[b][0:rows, 1, cols], W[0:rows, cols], start=True, stop=False)
                    mm = pe.matmul(banks[2][:, cols], tok[b][0:rows, 0, cols], tok[b][0:rows, 2, cols], start=False, stop=True)
                mm.then_inc(d_done, 1)
                if feats:
                    begin(n, nb)

            for k in range(ZT):
                project(0, k)
            pe.wait_ge(h_in, 32 + START)
            for k in range(ZT):
                project(1, k)
            lora(0)
            gates(0)
            by_rows(0, GROUPS * 2)
            begin(0, 0)
            chunks(pe, body)


def attention(nc, io):
    STEPS = NT
    with ExitStack() as c:
        sb = lambda n, s: c.enter_context(nc.sbuf_tensor("c_" + n, s, F32))
        sems = []

        def sem(n):
            sems.append(c.enter_context(nc.semaphore("c_" + n)))
            return sems[-1]

        ps = lambda n, s: c.enter_context(nc.psum_tensor("c_" + n, s, F32))
        score = [ps(f"score{i}", [P, 2, 512]) for i in range(2)]
        turned = [ps(f"turned{i}", [P, 512]) for i in range(2)]
        acc = ps("acc", [P, 512])
        ident = sb("ident", [P, P])
        qT = [sb(f"qT{j}", [QK, NT, P]) for j in range(2)]
        kT = [sb(f"kT{j}", [QK, NT + 1, P]) for j in range(2)]
        v = [sb(f"v{j}", [P, NT + 1, VD]) for j in range(2)]
        probs = [sb(f"probs{i}", [P, NPT * P]) for i in range(2)]
        probsT = sb("probsT", [P, NPT, P])
        top = sb("top", [P, 2])
        total = sb("total", [P, 2])
        inv = sb("inv", [P, 1])
        out = [sb(f"out{j}", [P, NT, VD]) for j in range(2)]
        (const_in, score_done, score_free, top_ready, exp_done, turn_done, turn_dve, turn_act, probs_free, pv_done, acc_copied,
         total_free, nothing_set, overflow_filled, dve_step) = (sem(n) for n in (
             "const_in score_done score_free top_ready exp_done turn_done turn_dve turn_act probs_free pv_done acc_copied "
             "total_free nothing_set overflow_filled dve_step").split())
        head_in = [sem("head_in0"), sem("head_in1")]
        out_stored = [sem("out_stored0"), sem("out_stored1")]
        nothing = sb("nothing", [P, D])
        prime(nc, [s for s in sems if not s.name.endswith("_step")])
        block = c.enter_context(nc.Block())
        keys = [[(k, P) for k in range(i + 1)] for i in range(NPT)] + [[(PAST_TILE, P), (NPT, DEC)]]
        width = [sum(n for _, n in ks) for ks in keys]
        ROUND = 2 * STEPS
        ROUNDS = H // 2

        head_of = lambda p: p // STEPS % 2
        tile_of = lambda p: p % STEPS

        WIDE = sum(len(ks) > 4 for ks in keys)
        wide_before = lambda u, p: 2 * WIDE * u + WIDE * (p // STEPS) + sum(len(keys[n]) > 4 for n in range(tile_of(p)))

        def rounds(eng, body):
            with eng.Fori(0, ROUNDS - 1) as u:
                body(u, ROUND)
            body(ROUNDS - 1, 0)

        @block.sync
        def _(sp):
            def load(u, j):
                h = u * 2 + j
                head = lambda x: x[:, :, bass.ds(h, 1), :]
                sp.dma_start(qT[j][:], head(io["qT_d"][0:NT]).rearrange("t d o n -> d t (o n)")).then_inc(head_in[j], 16)
                sp.dma_start(kT[j][:], head(io["kT_d"]).rearrange("t d o n -> d t (o n)")).then_inc(head_in[j], 16)
                sp.dma_start(v[j][:], head(io["v_d"]).rearrange("t p o n -> p t (o n)")).then_inc(head_in[j], 16)

            def body(u, ahead):
                for j in range(2):
                    sp.wait_ge(acc_copied, ROUND * u + STEPS * (j + 1) + START)
                    sp.dma_start(io["oa_d"][:, :, bass.ds(u * 2 + j, 1), :].rearrange("t p o n -> p t (o n)"),
                                 out[j][:]).then_inc(out_stored[j], 16)
                    if ahead:
                        load(u + 1, j)

            sp.dma_start(ident[:], io["ident"]).then_inc(const_in, 16)
            load(0, 0)
            load(0, 1)
            sp.wait_ge(nothing_set, 1 + START)
            with sp.Fori(0, OVERFLOW) as n:
                sp.dma_start(at(io["y_d"], n + NE), nothing[:]).then_inc(overflow_filled, 16)
            rounds(sp, body)
            sp.wait_ge(overflow_filled, 16 * OVERFLOW + START)
            for j in range(2):
                sp.wait_ge(out_stored[j], 16 * ROUNDS + START)

        @block.gpsimd
        def _(pool):
            pool.memset(nothing[:], 0.0).then_inc(nothing_set, 1)

        @block.vector
        def _(dve):
            step = InOrder(dve, dve_step)

            def maximum(u, p):
                b, s = p % 2, tile_of(p)
                sc = score[b][:].rearrange("p a n -> p (a n)")
                dve.wait_ge(score_done, ROUND * u + p + 1 + START)
                if s < NPT:
                    step(dve.memset(sc[0:64, width[s] - 64:width[s]], NEG))
                dve.tensor_reduce(top[:, b:b + 1], sc[:, 0:width[s]], AX, ALU.max, negate=True).then_inc(top_ready, 1)

            def body(u, ahead):
                step.lap()
                for p in range(ROUND):
                    b, s, j = p % 2, tile_of(p), head_of(p)
                    n = min(4, len(keys[s]))
                    G = ROUND * u + p
                    dve.wait_ge(turn_done, 2 * G + 1 + START)
                    dve.wait_ge(pv_done, G + START)
                    if s < NPT:
                        dve.tensor_copy(probsT[:, 0:n, :], turned[0][:, 0:n * P].rearrange("p (a b) -> p a b", b=P)).then_inc(turn_dve, 1)
                    else:
                        step(dve.tensor_copy(probsT[:, 0, :], turned[0][:, 0:P]))
                        dve.tensor_copy(probsT[0:DEC, 1, :], turned[0][0:DEC, P:2 * P]).then_inc(turn_dve, 1)
                    if p + 2 < ROUND + ahead:
                        maximum(u, p + 2)
                    dve.wait_ge(exp_done, G + 1 + START)
                    dve.wait_ge(acc_copied, G + START)
                    step(dve.reciprocal(inv[:], total[:, b:b + 1]))
                    dve.sem_inc(total_free, 1)
                    if s == 0:
                        dve.wait_ge(out_stored[j], 16 * u + START)
                    dve.wait_ge(pv_done, G + 1 + START)
                    dve.tensor_scalar(out[j][:, s, :], acc[:, 0:VD], inv[:, 0:1], None, ALU.mult).then_inc(acc_copied, 1)

            maximum(0, 0)
            maximum(0, 1)
            rounds(dve, body)

        @block.scalar
        def _(act):
            act.sem_inc(score_free, 2)
            act.sem_inc(probs_free, 1)
            act.sem_inc(total_free, 1)

            def exponential(u, p):
                b, s = p % 2, tile_of(p)
                G = ROUND * u + p
                act.wait_ge(top_ready, G + 1 + START)
                act.wait_ge(probs_free, G + START)
                act.wait_ge(total_free, G + START)
                act.activation(probs[b][:, 0:width[s]], score[b][:].rearrange("p a n -> p (a n)")[:, 0:width[s]],
                               ACT.Exp, bias=top[:, b:b + 1], accum_out=total[:, b:b + 1]).then_inc(exp_done, 1)
                act.wait_ge(exp_done, G + 1 + START)
                act.sem_inc(score_free, 1)

            def body(u, ahead):
                for p in range(ROUND):
                    if p + 1 < ROUND + ahead:
                        exponential(u, p + 1)
                    n = len(keys[tile_of(p)])
                    G = ROUND * u + p
                    if n > 4:
                        act.wait_ge(turn_done, 2 * G + 2 + START)
                        act.wait_ge(pv_done, G + START)
                        act.activation(probsT[:, 4:n, :], turned[1][:, 0:(n - 4) * P], ACT.Copy).then_inc(turn_act, 1)

            exponential(0, 0)
            rounds(act, body)

        @block.tensor
        def _(pe):
            pe.wait_ge(const_in, 16 + START)

            def scores(u, p):
                b, s, j = p % 2, tile_of(p), head_of(p)
                if s == 0:
                    pe.wait_ge(head_in[j], 48 * (u + p // ROUND + 1) + START)
                pe.wait_ge(score_free, ROUND * u + p + 1 + START)
                if s < NPT:
                    for n in range(0, width[s], 512):
                        m = min(512, width[s] - n)
                        mm = pe.matmul(score[b][:, n // 512, 0:m], qT[j][:, s, :], kT[j][:, n // P:(n + m) // P, :],
                                       start=True, stop=True)
                else:
                    pe.matmul(score[b][:, 0, 0:P], qT[j][:, s, :], kT[j][:, PAST_TILE, :], start=True, stop=True)
                    mm = pe.matmul(score[b][:, 0, P:P + DEC], qT[j][:, s, :], kT[j][:, NPT, 0:DEC], start=True, stop=True)
                mm.then_inc(score_done, 1)

            def body(u, ahead):
                for p in range(ROUND):
                    b, s, j = p % 2, tile_of(p), head_of(p)
                    G = ROUND * u + p
                    wide = len(keys[s]) > 4
                    pe.wait_ge(exp_done, G + 1 + START)
                    pe.wait_ge(turn_dve, G + START)
                    if wide:
                        pe.wait_ge(turn_act, wide_before(u, p) + START)
                    for n, (_, m) in enumerate(keys[s]):
                        mm = pe.transpose(turned[n // 4][0:m, n % 4 * P:(n % 4 + 1) * P], probs[b][:, n * P:n * P + m], ident[:])
                        if n == 3 and wide:
                            mm.then_inc(turn_done, 1)
                    mm.then_inc(turn_done, 1 if wide else 2)
                    if p + 2 < ROUND + ahead:
                        scores(u, p + 2)
                    pe.wait_ge(turn_dve, G + 1 + START)
                    if wide:
                        pe.wait_ge(turn_act, wide_before(u, p) + 1 + START)
                    pe.sem_inc(probs_free, 1)
                    pe.wait_ge(acc_copied, G + START)
                    for n, (k, m) in enumerate(keys[s]):
                        mm = pe.matmul(acc[:, 0:VD], probsT[0:m, n, :], v[j][0:m, k, :], start=(n == 0), stop=(n == len(keys[s]) - 1))
                    mm.then_inc(pv_done, 1)

            scores(0, 0)
            scores(0, 1)
            rounds(pe, body)


def merge(nc, io, keep):
    UNITS = 4
    with ExitStack() as c:
        sb = lambda n, s, d=F32: c.enter_context(nc.sbuf_tensor("d_" + n, s, d))
        sems = []

        def sem(n):
            sems.append(c.enter_context(nc.semaphore("d_" + n)))
            return sems[-1]

        banks = [c.enter_context(nc.psum_tensor(f"d_ps{i}", [P, 512], F32)) for i in range(8)]
        wg = sb("wg", [P, DC, 2 * D])
        wo = sb("wo", [P, 2 * HB, D])
        wr = sb("wr", [P, DC, RT])
        br = sb("br", [P, RT])
        ident = sb("ident", [P, P])
        before = sb("before", [P, P])
        ones = sb("ones", [P, P])
        g_ffn = sb("g_ffn", [P, D])
        count_up = sb("count_up", [P, NE])
        real = sb("real", [P, 1])
        hT = sb("hT", [P, DC, P])
        o = sb("o", [P, 2, H * VD])
        x = sb("x", [P, D])
        oT = sb("oT", [P, 2 * HB, P])
        gate = sb("gate", [P, UNITS, 512])
        mixed = sb("mixed", [P, 512])
        junk = sb("junk", [P, D])
        ms = sb("ms", [P, 1])
        h2 = sb("h2", [P, D])
        h2T = sb("h2T", [P, DC, P])
        lg = sb("lg", [P, RT])
        gpad = sb("gpad", [P, 8])
        gtop = sb("gtop", [P, 8])
        gidx = sb("gidx", [P, 8], U32)
        etop = sb("etop", [P, 8])
        eidx = sb("eidx", [P, 8], U32)
        small = sb("small", [P, 8])
        gexp = sb("gexp", [P, NG])
        pen = sb("pen", [P, NG])
        el = sb("el", [P, NE])
        rec = sb("rec", [P, 2 * NE + 6])
        both = sb("both", [P, NE])
        pos = sb("pos", [P, NE])
        prod = sb("prod", [P, 2, NE])
        hot = rec[:, 0:2 * NE].rearrange("p (k e) -> p k e", k=2)
        run, route = keep["run"], keep["route"]
        (consts_in, set_done, h_in, o_in, x_in, oT_done, oT_copied, gates_done, sig_done, proj_done, mixed_done, x_done, x_sq,
         ms_ready, rms_root, h2_ready, h2T_done, h2T_copied, lg_done, neg_top, g_sum, d_ready, d_sig, both_ready, count_done,
         counted, x_stored, h2_stored, dve_step) = (sem(n) for n in (
             "consts_in set_done h_in o_in x_in oT_done oT_copied gates_done sig_done proj_done mixed_done x_done x_sq "
             "ms_ready rms_root h2_ready h2T_done h2T_copied lg_done neg_top g_sum d_ready d_sig both_ready count_done "
             "counted x_stored h2_stored dve_step").split())
        prime(nc, [s for s in sems if not s.name.endswith("_step")])
        block = c.enter_context(nc.Block())
        CONSTS = 9
        branch = lambda u: u % 2
        half = lambda u: slice(u // 2 * 512, u // 2 * 512 + 512)

        @block.sync
        def _(sp):
            consts = ((wg[:], io["w_gates"]), (wo[:], io["w_out"]), (wr[:], io["w_router"]),
                      (br[:], io["b_router"].partition_broadcast(P)), (ident[:], io["ident"]),
                      (before[:], io["causal"][:, 0:P]), (g_ffn[:], io["norm_ffn_g"].partition_broadcast(P)),
                      (count_up[:], io["count_up"].partition_broadcast(P)), (real[:], io["real"]))

            def load_o(t):
                sp.dma_start(o[:, 0, :], at(io["oa_d"], t).rearrange("p h d -> p (h d)")).then_inc(o_in, 16)
                sp.dma_start(o[:, 1, :], at(io["ob_d"], t).rearrange("p h d -> p (h d)")).then_inc(o_in, 16)

            def load_h(t):
                sp.dma_start(hT[:], at(io["hT_d"], t)).then_inc(h_in, 16)

            def load_x(t):
                sp.dma_start(x[:], at(io["x"], t)).then_inc(x_in, 16)

            def store_x(n):
                sp.wait_ge(x_done, n + 1 + START)
                sp.dma_start(at(io["x2_d"], n), x[:]).then_inc(x_stored, 16)

            def store_h2(n):
                sp.wait_ge(h2_ready, n + 1 + START)
                sp.dma_start(at(io["h2_d"], n), h2[:]).then_inc(h2_stored, 16)

            def body(n, more):
                store_x(n)
                if more:
                    sp.wait_ge(oT_done, n + 2 + START)
                    load_o(n + 2)
                store_h2(n)
                sp.wait_ge(x_stored, 16 * (n + 1) + START)
                load_x(n + 1)
                if more:
                    sp.wait_ge(gates_done, UNITS * (n + 2) + START)
                    load_h(n + 2)

            for dst, src in consts:
                sp.dma_start(dst, src).then_inc(consts_in, 16)
            load_o(0)
            load_h(0)
            load_x(0)
            sp.wait_ge(oT_done, 1 + START)
            load_o(1)
            sp.wait_ge(gates_done, UNITS + START)
            load_h(1)
            with sp.Fori(0, NT - 2) as n:
                body(n, True)
            body(NT - 2, False)
            store_x(NT - 1)
            store_h2(NT - 1)
            sp.wait_ge(x_stored, 16 * NT + START)
            sp.wait_ge(h2_stored, 16 * NT + START)

        @block.gpsimd
        def _(pool):
            pool.memset(ones[:], 1.0)
            pool.memset(gpad[:], -BIG)
            pool.memset(run[:], 0.0).then_inc(set_done, 1)

        @block.vector
        def _(dve):
            step = InOrder(dve, dve_step)
            dve.wait_ge(consts_in, 16 * CONSTS + START)
            dve.wait_ge(set_done, 1 + START)

            def copy_oT(t):
                dve.wait_ge(oT_done, t + 1 + START)
                dve.wait_ge(proj_done, UNITS * t + START)
                dve.tensor_copy(oT[:, HB:, :], banks[1][:].rearrange("p (a b) -> p a b", b=P)).then_inc(oT_copied, 1)

            def unit(t, u):
                if u == 0:
                    dve.wait_ge(x_in, 16 * (t + 1) + START)
                dve.wait_ge(sig_done, UNITS * t + u + 1 + START)
                dve.wait_ge(proj_done, UNITS * t + u + 1 + START)
                dve.tensor_tensor(mixed[:], gate[:, u, :], banks[4 + u % 2][:], ALU.mult).then_inc(mixed_done, 1)
                dve.wait_ge(mixed_done, UNITS * t + u + 1 + START)
                ins = dve.tensor_tensor(x[:, half(u)], x[:, half(u)], mixed[:], ALU.add)
                if u == UNITS - 1:
                    ins.then_inc(x_done, 1)
                else:
                    step(ins)

            def norm(n):
                dve.wait_ge(x_sq, n + 1 + START)
                dve.tensor_scalar(ms[:], ms[:], 1.0 / D, EPS, ALU.mult, ALU.add).then_inc(ms_ready, 1)
                dve.wait_ge(rms_root, n + 1 + START)
                step(dve.reciprocal(ms[:], ms[:]))
                dve.wait_ge(h2_stored, 16 * n + START)
                dve.wait_ge(h2T_done, n + START)
                dve.scalar_tensor_tensor(h2[:], x[:], ms[:, 0:1], g_ffn[:], ALU.mult, ALU.mult).then_inc(h2_ready, 1)

            def copy_h2T(n):
                dve.wait_ge(h2T_done, n + 1 + START)
                dve.tensor_copy(h2T[:, 4:, :], banks[7][:].rearrange("p (a b) -> p a b", b=P)).then_inc(h2T_copied, 1)

            def choose(n, last):
                dve.wait_ge(lg_done, n + 1 + START)
                step(dve.tensor_tensor(lg[:], banks[6][:, 0:RT], br[:], ALU.add))
                step(dve.tensor_copy(gpad[:, 0:NG], lg[:, 0:NG]))
                step(dve.max(gtop[:], gpad[:]))
                dve.tensor_scalar(small[:, 0:1], gtop[:, 0:1], -1.0, None, ALU.mult).then_inc(neg_top, 1)
                step(dve.max_index(gidx[:], gtop[:], gpad[:]))
                step(dve.tensor_copy(small[:, 2:3], gidx[:, 0:1]))
                step(dve.tensor_scalar(pen[:], count_up[:, 0:NG], small[:, 2:3], None, ALU.is_equal))
                step(dve.tensor_scalar(pen[:], pen[:], BIG, -BIG, ALU.mult, ALU.add))
                step(dve.tensor_tensor(el[:].rearrange("p (g e) -> p g e", g=NG), lg[:, NG:].rearrange("p (g e) -> p g e", g=NG),
                                       spread(pen[:].unsqueeze(2), [P, NG, EPG]), ALU.add))
                step(dve.max(etop[:], el[:]))
                step(dve.max_index(eidx[:], etop[:], el[:]))
                step(dve.tensor_tensor(small[:, 4:5], etop[:, 0:1], etop[:, 1:2], ALU.subtract))
                dve.tensor_scalar(small[:, 5:6], small[:, 4:5], -1.0, None, ALU.mult).then_inc(d_ready, 1)
                step(dve.tensor_copy(rec[:, 2 * NE:2 * NE + 2], eidx[:, 0:2]))
                for k in range(2):
                    step(dve.tensor_scalar(hot[:, k, :], count_up[:], rec[:, 2 * NE + k:2 * NE + k + 1], None, ALU.is_equal))
                    if last:
                        step(dve.tensor_scalar(hot[:, k, :], hot[:, k, :], real[:, 0:1], None, ALU.mult))
                dve.tensor_tensor(both[:], hot[:, 0, :], hot[:, 1, :], ALU.add).then_inc(both_ready, 1)

            def record(n):
                dve.wait_ge(g_sum, n + 1 + START)
                step(dve.reciprocal(small[:, 3:4], small[:, 1:2]))
                dve.wait_ge(d_sig, n + 1 + START)
                step(dve.tensor_scalar(rec[:, 2 * NE + 4:], small[:, 6:8], small[:, 3:4], None, ALU.mult))
                dve.wait_ge(count_done, n + 1 + START)
                step(dve.tensor_tensor(pos[:], banks[7][:, 0:NE], run[:], ALU.add))
                dve.tensor_tensor(run[:], banks[7][:, NE:2 * NE], run[:], ALU.add).then_inc(counted, 1)
                step(dve.tensor_tensor(prod[:], hot, spread(pos[:].unsqueeze(1), [P, 2, NE]), ALU.mult))
                step(dve.tensor_reduce(rec[:, 2 * NE + 2:2 * NE + 4], prod[:], AX, ALU.add))
                dve.wait_ge(counted, n + 1 + START)
                step(dve.tensor_copy(route[:, bass.ds(n, 1), :].rearrange("p o n -> p (o n)"), rec[:]))

            copy_oT(0)
            for u in range(UNITS):
                unit(0, u)
            with dve.Fori(0, NT - 1) as n:
                step.lap()
                copy_oT(n + 1)
                norm(n)
                copy_h2T(n)
                unit(n + 1, 0)
                choose(n, False)
                unit(n + 1, 1)
                record(n)
                unit(n + 1, 2)
                unit(n + 1, 3)
            norm(NT - 1)
            copy_h2T(NT - 1)
            choose(NT - 1, True)
            record(NT - 1)

        @block.scalar
        def _(act):
            def copy_oT(t):
                act.wait_ge(oT_done, t + 1 + START)
                act.wait_ge(proj_done, UNITS * t + START)
                act.activation(oT[:, 0:HB, :], banks[0][:].rearrange("p (a b) -> p a b", b=P), ACT.Copy).then_inc(oT_copied, 1)

            def sigmoid(t, u):
                act.wait_ge(gates_done, UNITS * t + u + 1 + START)
                act.wait_ge(x_done, t + START)
                act.activation(gate[:, u, :], banks[2 + u % 2][:], ACT.Sigmoid).then_inc(sig_done, 1)

            def square(n):
                act.wait_ge(x_done, n + 1 + START)
                act.wait_ge(h2_ready, n + START)
                act.activation(junk[:], x[:], ACT.Square, accum_out=ms[:]).then_inc(x_sq, 1)

            def root(n):
                act.wait_ge(ms_ready, n + 1 + START)
                act.activation(ms[:], ms[:], ACT.Sqrt).then_inc(rms_root, 1)

            def copy_h2T(n):
                act.wait_ge(h2T_done, n + 1 + START)
                act.activation(h2T[:, 0:4, :], banks[6][:].rearrange("p (a b) -> p a b", b=P), ACT.Copy).then_inc(h2T_copied, 1)

            def weights(n):
                act.wait_ge(d_ready, n + 1 + START)
                act.activation(small[:, 6:8], small[:, 4:6], ACT.Sigmoid).then_inc(d_sig, 1)
                act.wait_ge(neg_top, n + 1 + START)
                act.wait_ge(g_sum, n + START)
                act.activation(gexp[:], lg[:, 0:NG], ACT.Exp, bias=small[:, 0:1], accum_out=small[:, 1:2]).then_inc(g_sum, 1)

            copy_oT(0)
            for u in range(UNITS):
                sigmoid(0, u)
            with act.Fori(0, NT - 1) as n:
                square(n)
                copy_oT(n + 1)
                root(n)
                sigmoid(n + 1, 0)
                copy_h2T(n)
                sigmoid(n + 1, 1)
                weights(n)
                sigmoid(n + 1, 2)
                sigmoid(n + 1, 3)
            square(NT - 1)
            root(NT - 1)
            copy_h2T(NT - 1)
            weights(NT - 1)

        @block.tensor
        def _(pe):
            pe.wait_ge(consts_in, 16 * CONSTS + START)
            pe.wait_ge(set_done, 1 + START)

            def turn_o(t):
                pe.wait_ge(o_in, 32 * (t + 1) + START)
                pe.wait_ge(oT_copied, 2 * t + START)
                for b in range(2):
                    for k in range(HB):
                        mm = pe.transpose(banks[b][:, k * P:(k + 1) * P], o[:, b, k * P:(k + 1) * P], ident[:])
                mm.then_inc(oT_done, 1)

            def gates(t, u):
                if u == 0:
                    pe.wait_ge(h_in, 16 * (t + 1) + START)
                pe.wait_ge(sig_done, UNITS * t + (u - 1 if u >= 2 else 0) + START)
                for k in range(DC):
                    mm = pe.matmul(banks[2 + u % 2][:], hT[:, k, :], wg[:, k, branch(u) * D + u // 2 * 512:][:, 0:512],
                                   start=(k == 0), stop=(k == DC - 1))
                mm.then_inc(gates_done, 1)

            def project(t, u):
                pe.wait_ge(oT_copied, 2 * (t + 1) + START)
                pe.wait_ge(mixed_done, UNITS * t + (u - 1 if u >= 2 else 0) + START)
                for k in range(HB):
                    mm = pe.matmul(banks[4 + u % 2][:], oT[:, HB * branch(u) + k, :], wo[:, HB * branch(u) + k, half(u)],
                                   start=(k == 0), stop=(k == HB - 1))
                mm.then_inc(proj_done, 1)

            def turn_h2(n):
                pe.wait_ge(h2_ready, n + 1 + START)
                pe.wait_ge(counted, n + START)
                for k in range(DC):
                    mm = pe.transpose(banks[6 + k // 4][:, k % 4 * P:(k % 4 + 1) * P], h2[:, k * P:(k + 1) * P], ident[:])
                mm.then_inc(h2T_done, 1)

            def router(n):
                pe.wait_ge(h2T_copied, 2 * (n + 1) + START)
                for k in range(DC):
                    mm = pe.matmul(banks[6][:, 0:RT], h2T[:, k, :], wr[:, k, :], start=(k == 0), stop=(k == DC - 1))
                mm.then_inc(lg_done, 1)

            def count(n):
                pe.wait_ge(both_ready, n + 1 + START)
                pe.matmul(banks[7][:, 0:NE], before[:], both[:], start=True, stop=True)
                pe.matmul(banks[7][:, NE:2 * NE], ones[:], both[:], start=True, stop=True).then_inc(count_done, 1)

            turn_o(0)
            for u in range(UNITS):
                gates(0, u)
                project(0, u)
            with pe.Fori(0, NT - 1) as n:
                t = n + 1
                turn_o(t)
                gates(t, 0)
                turn_h2(n)
                project(t, 0)
                gates(t, 1)
                router(n)
                project(t, 1)
                gates(t, 2)
                gates(t, 3)
                count(n)
                project(t, 2)
                project(t, 3)
            turn_h2(NT - 1)
            router(NT - 1)
            count(NT - 1)


def slots(nc, io, keep):
    BLOCKS = NE + OVERFLOW + 2
    NBMAX = -(-(SEQ + DEC) // CAP)
    with ExitStack() as c:
        sb = lambda n, s, d=F32: c.enter_context(nc.sbuf_tensor("e_" + n, s, d))
        sems = []

        def sem(n):
            sems.append(c.enter_context(nc.semaphore("e_" + n)))
            return sems[-1]

        more = sb("more", [P, NE])
        gt = sb("gt", [P, NE])
        upto = sb("upto", [P, NE])
        one = sb("one", [P, NE])
        base = sb("base", [P, NE])
        count_up = sb("count_up", [P, NE])
        owned = sb("owned", [P, OVERFLOW, NE])
        q = sb("q", [P, NT, 2])
        ge = sb("ge", [P, NT, 2])
        hb = sb("hb", [P, NT, 2, NE])
        bb = sb("bb", [P, NT, 2])
        over = sb("over", [P, NT, 2])
        place = sb("place", [P, NT, 2])
        fixed = sb("fixed", [P, 2, NT, 2])
        zeros = sb("zeros", [P, BLOCKS], I32)
        token = sb("token", [P, NT], I32)
        table = [[sb(f"table{t}_{k}", [P, 1], I32) for k in range(2)] for t in range(NT)]
        tf = sb("tf", [P, NT, 2])
        run, route, row_of, plan = keep["run"], keep["route"], keep["row_of"], keep["plan"]
        planf = sb("planf", [P, OVERFLOW + 1])
        consts_in, set_done, dve_step, ready = (sem(n) for n in ("consts_in", "set_done", "dve_step", "ready"))
        table_set, scattered = keep["gathered"]["table_set"], keep["gathered"]["scattered"]
        prime(nc, [s for s in sems if not s.name.endswith("_step")] + list(keep["weights_in"].values()))
        block = c.enter_context(nc.Block())

        @block.sync
        def _(sp):
            sp.dma_start(count_up[:], io["count_up"].partition_broadcast(P)).then_inc(consts_in, 16)
            sp.dma_start(fixed[:], io["fixed"]).then_inc(consts_in, 16)
            sp.dma_start(token[:], io["token"]).then_inc(consts_in, 16)
            for e in range(WB):
                sp.dma_start(keep["wgu"][e][:], io["w_gate_up"][e]).then_inc(keep["weights_in"][f"up_in{e}"], 16)
                sp.dma_start(keep["wd"][e][:], io["w_down"][e]).then_inc(keep["weights_in"][f"down_in{e}"], 16)

        @block.gpsimd
        def _(pool):
            pool.memset(one[:], 1.0).then_inc(set_done, 1)
            pool.memset(zeros[:], 0).then_inc(set_done, 1)
            pool.wait_ge(set_done, 2 + START)
            pool.dma_start(io["table_d"].rearrange("(p n) o -> p (n o)", p=P), zeros[:]).then_inc(table_set, 16)
            pool.wait_ge(table_set, 16)
            pool.wait_ge(consts_in, 48 + START)
            pool.wait_ge(ready, 1 + START)
            for t in range(NT):
                for k in range(2):
                    pool.indirect_dma_start(io["table_d"], bass.IndirectOffsetOnAxis(ap=table[t][k][:, 0:1], axis=0),
                                            token[:, t:t + 1], None).then_inc(scattered, 16)
            pool.wait_ge(scattered, 32 * NT)

        @block.vector
        def _(dve):
            step = InOrder(dve, dve_step)
            dve.wait_ge(consts_in, 48 + START)
            dve.wait_ge(set_done, 2 + START)
            step(dve.tensor_scalar(more[:], run[:], float(CAP), None, ALU.is_gt))
            for n in range(2, NBMAX):
                step(dve.tensor_scalar(gt[:], run[:], float(CAP * n), None, ALU.is_gt))
                step(dve.tensor_tensor(more[:], more[:], gt[:], ALU.add))
            step(dve.tensor_tensor_scan(upto[:], one[:], more[:], 0.0, ALU.mult, ALU.add))
            step(dve.tensor_tensor(base[:], upto[:], more[:], ALU.subtract))
            for n in range(OVERFLOW):
                step(dve.tensor_scalar(owned[:, n, :], upto[:], float(n), None, ALU.is_le))
            step(dve.tensor_reduce(planf[:, 0:OVERFLOW], owned[:], AX, ALU.add))
            step(dve.tensor_scalar(planf[:, 0:OVERFLOW], planf[:, 0:OVERFLOW], float(NE - 1), None, ALU.min))
            step(dve.tensor_copy(planf[:, OVERFLOW:], upto[:, NE - 1:]))
            step(dve.tensor_copy(plan[:], planf[:]))
            pos, ex = route[:, :, 2 * NE + 2:2 * NE + 4], route[:, :, 2 * NE:2 * NE + 2]
            step(dve.tensor_scalar(q[:], pos, float(CAP), None, ALU.is_ge))
            for n in range(2, NBMAX):
                step(dve.tensor_scalar(ge[:], pos, float(CAP * n), None, ALU.is_ge))
                step(dve.tensor_tensor(q[:], q[:], ge[:], ALU.add))
            step(dve.scalar_tensor_tensor(place[:], q[:], -float(CAP), pos, ALU.mult, ALU.add))
            for k in range(2):
                step(dve.tensor_tensor(hb[:, :, k, :], route[:, :, NE * k:NE * k + NE],
                                       spread(base[:].unsqueeze(1), [P, NT, NE]), ALU.mult))
                step(dve.tensor_reduce(bb[:, :, k], hb[:, :, k, :], AX, ALU.add))
            step(dve.tensor_scalar(over[:], q[:], 1.0, None, ALU.min))
            step(dve.scalar_tensor_tensor(bb[:], q[:], float(NE - 1), bb[:], ALU.add, ALU.add))
            step(dve.tensor_tensor(bb[:], bb[:], ex, ALU.subtract))
            step(dve.tensor_tensor(bb[:], bb[:], over[:], ALU.mult))
            step(dve.tensor_tensor(bb[:], bb[:], ex, ALU.add))
            step(dve.scalar_tensor_tensor(tf[:], place[:], float(BLOCKS), bb[:], ALU.mult, ALU.add))
            step(dve.tensor_tensor(tf[:], tf[:], fixed[:, 0], ALU.mult))
            step(dve.tensor_tensor(tf[:], tf[:], fixed[:, 1], ALU.add))
            for t in range(NT):
                for k in range(2):
                    step(dve.tensor_copy(table[t][k][:], tf[:, t, k:k + 1]))
            dve.sem_inc(ready, 1)
            step(dve.scalar_tensor_tensor(bb[:], bb[:], float(CAP), place[:], ALU.mult, ALU.add))
            step(dve.tensor_tensor(bb[:], bb[:], fixed[:, 0], ALU.mult))
            for t in range(NT):
                for k in range(2):
                    step(dve.tensor_copy(row_of[t][k][:], bb[:, t, k:k + 1]))


def experts(nc, io, keep):
    BLOCKS = NE + OVERFLOW + 2
    with ExitStack() as c:
        sb = lambda n, s, d=F32: c.enter_context(nc.sbuf_tensor("f_" + n, s, d))
        sems = []

        def sem(n):
            sems.append(c.enter_context(nc.semaphore("f_" + n)))
            return sems[-1]

        ps = lambda n: c.enter_context(nc.psum_tensor("f_" + n, [P, 512], F32))
        ident = sb("ident", [P, P])
        tokens = sb("tokens", [P, BLOCKS], I32)
        index = [sb(f"index{j}", [P, 1], I32) for j in range(2)]
        xg = [sb(f"xg{j}", [P, D]) for j in range(2)]
        xT = [sb(f"xT{j}", [P, DC, P]) for j in range(2)]
        wgu, wd = keep["wgu"], keep["wd"]
        sg = sb("sg", [P, FF])
        mid = sb("mid", [P, FF])
        midT = sb("midT", [P, 2, P])
        y = [sb(f"y{j}", [P, D]) for j in range(2)]
        turned = [ps("turned0"), ps("turned1")]
        hidden = [ps("hidden0"), ps("hidden1")]
        midps = ps("midps")
        down = [ps("down0"), ps("down1")]
        plan = keep["plan"]
        names = ("index_set index_seen store_seen turn_done turn_dve turn_act up_done sig_done mid_ready midT_done midT_copied down_done "
                 "y_dve y_act y_stored0 y_stored1 dve_step").split()
        const_in, tokens_in = sem("const_in"), sem("tokens_in")
        s = {n: sem(n) for n in names}
        o = {n: sem("o_" + n) for n in names + ["up_in0", "down_in0"]}
        s.update(keep["weights_in"])
        s.update({n: keep["gathered"][n] for n in ("x_in0", "x_in1")})
        o["x_in0"] = keep["gathered"]["o_x_in0"]
        prime(nc, [s for s in sems if not s.name.endswith("_step")])
        block = c.enter_context(nc.Block())

        def gather(pool, s, n, b, free, blk):
            if free is not None:
                pool.wait_ge(s["turn_done"], free + START)
            pool.tensor_copy(index[b][:], tokens[:, bass.ds(blk, 1)]).then_inc(s["index_set"], 1)
            pool.wait_ge(s["index_set"], n + 1 + START)
            goes_on(pool, s["index_seen"])
            pool.indirect_dma_start(xg[b][:], None, io["h2_d"].rearrange("t p n -> (t p) n"),
                                    bass.IndirectOffsetOnAxis(ap=index[b][:, 0:1], axis=0)).then_inc(s["x_in" + str(b)], 16)

        def turn(pe, s, n, b, m):
            pe.wait_ge(s["x_in" + str(b)], 16 * (m + 1))
            pe.wait_ge(s["turn_dve"], n + START)
            pe.wait_ge(s["turn_act"], n + START)
            for k in range(DC):
                mm = pe.transpose(turned[k // 4][:, k % 4 * P:(k % 4 + 1) * P], xg[b][:, k * P:(k + 1) * P], ident[:])
            mm.then_inc(s["turn_done"], 1)

        def up(pe, s, n, b, wb, m, free):
            pe.wait_ge(s["turn_dve"], n + 1 + START)
            pe.wait_ge(s["turn_act"], n + 1 + START)
            pe.wait_ge(s["up_in" + str(wb)], 16 * (m + 1) + START)
            if free is not None:
                pe.wait_ge(s["mid_ready"], free + START)
            for k in range(DC):
                mm = pe.matmul(hidden[b][:], xT[b][:, k, :], wgu[wb][:, k, :], start=(k == 0), stop=(k == DC - 1))
            mm.then_inc(s["up_done"], 1)

        def turn_mid(pe, s, n):
            pe.wait_ge(s["mid_ready"], n + 1 + START)
            pe.wait_ge(s["midT_copied"], n + START)
            for k in range(2):
                mm = pe.transpose(midps[:, k * P:(k + 1) * P], mid[:, k * P:(k + 1) * P], ident[:])
            mm.then_inc(s["midT_done"], 1)

        def project(pe, s, n, wb, m):
            pe.wait_ge(s["midT_copied"], n + 1 + START)
            pe.wait_ge(s["down_in" + str(wb)], 16 * (m + 1) + START)
            pe.wait_ge(s["y_dve"], n + START)
            pe.wait_ge(s["y_act"], n + START)
            for h in range(2):
                for k in range(2):
                    mm = pe.matmul(down[h][:], midT[:, k, :], wd[wb][:, k, 512 * h:512 * h + 512], start=(k == 0), stop=(k == 1))
            mm.then_inc(s["down_done"], 1)

        def copy_turned(eng, copy, s, n, b, free, half, flag):
            eng.wait_ge(s["turn_done"], n + 1 + START)
            if free is not None:
                eng.wait_ge(s["up_done"], free + START)
            copy(xT[b][:, 4 * half:4 * half + 4, :], turned[half][:].rearrange("p (a b) -> p a b", b=P)).then_inc(s[flag], 1)

        def middle(dve, step, s, n, b):
            step.lap()
            dve.wait_ge(s["sig_done"], n + 1 + START)
            dve.wait_ge(s["midT_done"], n + START)
            step(dve.tensor_tensor(mid[:], hidden[b][:, 0:FF], sg[:], ALU.mult))
            dve.tensor_tensor(mid[:], mid[:], hidden[b][:, FF:], ALU.mult).then_inc(s["mid_ready"], 1)

        def copy_mid(dve, s, n):
            dve.wait_ge(s["midT_done"], n + 1 + START)
            dve.wait_ge(s["down_done"], n + START)
            dve.tensor_copy(midT[:], midps[:, 0:2 * P].rearrange("p (a b) -> p a b", b=P)).then_inc(s["midT_copied"], 1)

        def copy_y(eng, copy, s, n, b, m, half, flag):
            eng.wait_ge(s["down_done"], n + 1 + START)
            eng.wait_ge(s["y_stored" + str(b)], 16 * m + START)
            copy(y[b][:, 512 * half:512 * half + 512], down[half][:]).then_inc(s[flag], 1)

        def sigmoid(act, s, n, b):
            act.wait_ge(s["up_done"], n + 1 + START)
            act.wait_ge(s["mid_ready"], n + START)
            act.activation(sg[:], hidden[b][:, 0:FF], ACT.Sigmoid).then_inc(s["sig_done"], 1)

        def store(sp, s, n, b, blk):
            sp.wait_ge(s["y_dve"], n + 1 + START)
            sp.wait_ge(s["y_act"], n + 1 + START)
            sp.dma_start(at(io["y_d"], blk), y[b][:]).then_inc(s["y_stored" + str(b)], 16)

        def through(eng, body):
            with eng.Fori(0, NE // WB - 1) as u:
                for j in range(WB):
                    body(u, j, WB)
            for j in range(WB):
                body(NE // WB - 1, j, 0)

        def overflow(eng, work):
            for b in range(2):
                eng.wait_ge(s["y_stored" + str(b)], 16 * (NE // 2) + START)
            used = eng.value_load(plan[0:1, OVERFLOW:OVERFLOW + 1], min_val=0, max_val=OVERFLOW)
            with eng.Fori(0, OVERFLOW) as n:
                with eng.If(n < used):
                    work(n)
                with eng.Else():
                    eng.nop()

        @block.sync
        def _(sp):
            def body(u, j, ahead):
                e = u * WB + j
                if ahead:
                    sp.wait_ge(s["up_done"], e + 1 + START)
                    sp.dma_start(wgu[j][:], at(io["w_gate_up"], e + WB)).then_inc(s["up_in" + str(j)], 16)
                    sp.wait_ge(s["down_done"], e + 1 + START)
                    sp.dma_start(wd[j][:], at(io["w_down"], e + WB)).then_inc(s["down_in" + str(j)], 16)
                store(sp, s, e, j % 2, e)

            def work(n):
                e = sp.value_load(plan[0:1, bass.ds(n, 1)], min_val=0, max_val=NE - 1)
                sp.wait_ge(o["down_done"], n + START)
                sp.dma_start(wgu[0][:], at(io["w_gate_up"], e)).then_inc(o["up_in0"], 16)
                sp.dma_start(wd[0][:], at(io["w_down"], e)).then_inc(o["down_in0"], 16)
                store(sp, o, n, 0, n + NE)
                sp.wait_ge(o["y_stored0"], 16 * (n + 1) + START)
                goes_on(sp, o["store_seen"])

            sp.dma_start(ident[:], io["ident"]).then_inc(const_in, 16)
            sp.dma_start(tokens[:], io["table_d"].rearrange("(p n) o -> p (n o)", p=P)).then_inc(tokens_in, 16)
            through(sp, body)
            overflow(sp, work)

        @block.gpsimd
        def _(pool):
            def body(u, j, ahead):
                if j + 2 < WB + ahead:
                    gather(pool, s, u * WB + j + 2, j % 2, u * WB + j + 1, u * WB + j + 2)

            pool.wait_ge(tokens_in, 16 + START)
            gather(pool, s, 0, 0, None, 0)
            gather(pool, s, 1, 1, None, 1)
            through(pool, body)
            overflow(pool, lambda n: gather(pool, o, n, 0, n, n + NE))

        @block.vector
        def _(dve):
            step = InOrder(dve, s["dve_step"])

            def body(u, j, ahead):
                e = u * WB + j
                middle(dve, step, s, e, j % 2)
                copy_mid(dve, s, e)
                if j + 2 < WB + ahead:
                    copy_turned(dve, dve.tensor_copy, s, e + 2, j % 2, e + 1, 1, "turn_dve")
                copy_y(dve, dve.tensor_copy, s, e, j % 2, (WB // 2) * u + j // 2, 1, "y_dve")

            def work(n):
                copy_turned(dve, dve.tensor_copy, o, n, 0, n, 1, "turn_dve")
                middle(dve, step, o, n, 0)
                copy_mid(dve, o, n)
                copy_y(dve, dve.tensor_copy, o, n, 0, n, 1, "y_dve")

            copy_turned(dve, dve.tensor_copy, s, 0, 0, None, 1, "turn_dve")
            copy_turned(dve, dve.tensor_copy, s, 1, 1, None, 1, "turn_dve")
            through(dve, body)
            overflow(dve, work)

        @block.scalar
        def _(act):
            copy = lambda dst, src: act.activation(dst, src, ACT.Copy)

            def body(u, j, ahead):
                e = u * WB + j
                sigmoid(act, s, e, j % 2)
                if j + 2 < WB + ahead:
                    copy_turned(act, copy, s, e + 2, j % 2, e + 1, 0, "turn_act")
                copy_y(act, copy, s, e, j % 2, (WB // 2) * u + j // 2, 0, "y_act")

            def work(n):
                copy_turned(act, copy, o, n, 0, n, 0, "turn_act")
                sigmoid(act, o, n, 0)
                copy_y(act, copy, o, n, 0, n, 0, "y_act")

            copy_turned(act, copy, s, 0, 0, None, 0, "turn_act")
            copy_turned(act, copy, s, 1, 1, None, 0, "turn_act")
            through(act, body)
            overflow(act, work)

        @block.tensor
        def _(pe):
            def body(u, j, ahead):
                e = u * WB + j
                if j + 1 < WB + ahead:
                    up(pe, s, e + 1, (j + 1) % 2, (j + 1) % WB, u + (j + 1) // WB, e)
                turn_mid(pe, s, e)
                if j + 2 < WB + ahead:
                    turn(pe, s, e + 2, j % 2, (WB // 2) * u + j // 2 + 1)
                project(pe, s, e, j, u)

            def work(n):
                turn(pe, o, n, 0, n)
                up(pe, o, n, 0, 0, n, n)
                turn_mid(pe, o, n)
                project(pe, o, n, 0, n)

            pe.wait_ge(const_in, 16 + START)
            turn(pe, s, 0, 0, 0)
            turn(pe, s, 1, 1, 0)
            up(pe, s, 0, 0, 0, 0, None)
            through(pe, body)
            overflow(pe, work)


def combine(nc, io, keep):
    with ExitStack() as c:
        sb = lambda n, s, d=F32: c.enter_context(nc.sbuf_tensor("g_" + n, s, d))
        sems = []

        def sem(n):
            sems.append(c.enter_context(nc.semaphore("g_" + n)))
            return sems[-1]

        x = [sb(f"x{i}", [P, D]) for i in range(3)]
        ys = [[sb(f"y{i}_{k}", [P, D]) for k in range(2)] for i in range(3)]
        x_in = [sem(f"x_in{i}") for i in range(3)]
        y_in = [keep["gathered"][f"y_in{i}"] for i in range(3)]
        first_added, x_ready, stored = sem("first_added"), sem("x_ready"), sem("stored")
        route, row_of = keep["route"], keep["row_of"]
        y_rows = io["y_d"].rearrange("b p n -> (b p) n")
        prime(nc, [s for s in sems if not s.name.endswith("_step")])
        block = c.enter_context(nc.Block())

        @block.sync
        def _(sp):
            for t in range(NT):
                if t >= 3:
                    sp.wait_ge(stored, 16 * (t - 2) + START)
                sp.dma_start(x[t % 3][:], io["x2_d"][t]).then_inc(x_in[t % 3], 16)

        @block.gpsimd
        def _(pool):
            for t in range(NT):
                if t >= 3:
                    pool.wait_ge(x_ready, t - 2 + START)
                for k in range(2):
                    pool.indirect_dma_start(ys[t % 3][k][:], None, y_rows,
                                            bass.IndirectOffsetOnAxis(ap=row_of[t][k][:, 0:1], axis=0)).then_inc(y_in[t % 3], 16)

        @block.vector
        def _(dve):
            for t in range(NT):
                dve.wait_ge(x_in[t % 3], 16 * (t // 3 + 1) + START)
                dve.wait_ge(y_in[t % 3], 32 * (t // 3 + 1))
                w = route[:, t, 2 * NE + 4:]
                xt = x[t % 3]
                dve.scalar_tensor_tensor(xt[:], ys[t % 3][0][:], w[:, 0:1], xt[:], ALU.mult, ALU.add).then_inc(first_added, 1)
                dve.wait_ge(first_added, t + 1 + START)
                dve.scalar_tensor_tensor(xt[:], ys[t % 3][1][:], w[:, 1:2], xt[:], ALU.mult, ALU.add).then_inc(x_ready, 1)

        @block.scalar
        def _(act):
            for t in range(NT):
                act.wait_ge(x_ready, t + 1 + START)
                if t >= 1:
                    act.wait_ge(stored, 16 * t + START)
                act.dma_start(io["out"][t], x[t % 3][:]).then_inc(stored, 16)
            act.wait_ge(stored, 16 * NT + START)


def layer(nc, io):
    with ExitStack() as c:
        sb = lambda n, s, d=F32: c.enter_context(nc.sbuf_tensor(n, s, d))
        gathered = {n: c.enter_context(nc.semaphore(n)) for n in (
            "table_set", "scattered", "x_in0", "x_in1", "o_x_in0", "y_in0", "y_in1", "y_in2")}
        latents(nc, io)
        mixing(nc, io)
        attention(nc, io)
        keep = dict(
            run=sb("run", [P, NE]),
            route=sb("route", [P, NT, 2 * NE + 6]),
            row_of=[[sb(f"row_of{t}_{k}", [P, 1], I32) for k in range(2)] for t in range(NT)],
            plan=sb("plan", [P, OVERFLOW + 1], I32),
        )
        merge(nc, io, keep)
        keep.update(
            wgu=[sb(f"wgu{j}", [P, DC, 2 * FF]) for j in range(WB)],
            wd=[sb(f"wd{j}", [P, 2, D]) for j in range(WB)],
            weights_in={f"{w}_in{j}": c.enter_context(nc.semaphore(f"{w}_in{j}")) for w in ("up", "down") for j in range(WB)},
            gathered=gathered,
        )
        slots(nc, io, keep)
        experts(nc, io, keep)
        combine(nc, io, keep)


def lay_out(inputs):
    import numpy as np
    i = {k: np.ascontiguousarray(v) for k, v in inputs.items()}
    x = np.zeros(((NT + 1) * P, D), np.float32)
    x[0:SEQ] = i["x_prompt"][0]
    x[SEQ:SEQ + DEC] = i["x_sample"][0]
    xT = np.ascontiguousarray(x.reshape(NT + 1, P, DC, P).transpose(0, 3, 2, 1))
    chunks = lambda w: np.ascontiguousarray(w.reshape(w.shape[0] // P, P, -1).transpose(1, 0, 2))
    w_in = i["w_in"][0]
    pos = np.concatenate([np.arange(SEQ), PAST + np.arange(P), np.arange(P)]).astype(np.float32)
    inv = (1.0 / (np.float32(10000.0) ** (np.arange(HALF, dtype=np.float32) * np.float32(2.0 / ROPE)))).astype(np.float32)
    ang = (pos[:, None] * inv[None, :]).astype(np.float32)
    trig = np.concatenate([np.cos(ang), np.sin(ang)], axis=1).astype(np.float32).reshape(NT + 1, P, ROPE)
    r, f = np.arange(P)[:, None], np.arange(P)[None, :]
    cols = lambda a: np.ascontiguousarray(a.reshape(-1, P).T)
    levels = np.zeros((6, P, P // 2), np.float32)
    for n in range(6):
        b = 2 << n
        of = 2 * b * (np.arange(P // 2) // b)
        levels[n] = (r // b * b == of[None, :] + b)
    state = i["state_wkv"][0, 0].reshape(PAIRS, 2, RH, RH)
    wkv0 = np.zeros((P, PAIRS, P), np.float32)
    for j in range(2):
        wkv0[RH * j:RH * j + RH, :, RH * j:RH * j + RH] = state[:, j].transpose(2, 0, 1)
    fixed = np.zeros((P, 2, NT, 2), np.float32)
    fixed[:, 0] = 1.0
    fixed[DEC:, 0, NT - 1] = 0.0
    for k in range(2):
        fixed[DEC:, 1, NT - 1, k] = np.arange(DEC, P) * (NE + OVERFLOW + 2) + NE + OVERFLOW + k
    experts_in = lambda w: np.ascontiguousarray(w.reshape(NE, w.shape[1] // P, P, w.shape[2]).transpose(0, 2, 1, 3))
    return dict(
        xT=xT, x=x[:NT * P].reshape(NT, P, D), trig=trig, ident=np.eye(P, dtype=np.float32),
        w_mla=chunks(np.ascontiguousarray(w_in[:, :MLA])),
        w_uq=chunks(i["w_uq"][0].reshape(QL, -1)), w_ukv=i["w_ukv"][0].reshape(KL, -1),
        norm_mix_g=np.ascontiguousarray(i["norm_mix_g"][0].reshape(DC, P).T),
        q_norm_g=i["q_norm_g"][0], kv_norm_g=i["kv_norm_g"][0],
        q_head_norm_g=i["q_head_norm_g"][0], k_head_norm_g=i["k_head_norm_g"][0],
        w_z=chunks(np.ascontiguousarray(w_in[:, MLA:MLA + ZC])),
        wa2=np.concatenate([i["rwkv_w2"][0], i["rwkv_a2"][0]], axis=0), g2=i["rwkv_g2"][0],
        vecs=np.ascontiguousarray(np.concatenate([cols(i[n][0]) for n in (
            "rwkv_mu", "rwkv_w0", "rwkv_a0", "rwkv_k_k", "rwkv_k_a", "rwkv_r_k")], axis=1)),
        rwkv_lnx_g=i["rwkv_lnx_g"][0], rwkv_lnx_b=i["rwkv_lnx_b"][0],
        same_head=(f // RH == r // RH).astype(np.float32),
        causal=np.concatenate([r < f, r <= f], axis=1).astype(np.float32),
        first=np.stack([(r == f + 1) & (f % 2 == 0), (f == r + 1) & (r % 2 == 0)], axis=1).astype(np.float32),
        merge_mask=np.ascontiguousarray(levels.transpose(1, 0, 2)),
        w_gates=chunks(np.ascontiguousarray(w_in[:, MLA + ZC:])), w_out=chunks(i["w_out"][0].reshape(2 * RD, D)),
        w_router=chunks(np.ascontiguousarray(np.concatenate(
            [i["w_router_group"][0], i["w_router_expert"][0].reshape(D, NE)], axis=1))),
        b_router=np.concatenate([i["b_router_group"][0], i["b_router_expert"][0].reshape(-1)]),
        norm_ffn_g=i["norm_ffn_g"][0], count_up=np.arange(NE, dtype=np.float32),
        real=(r < DEC).astype(np.float32), fixed=fixed,
        token=np.ascontiguousarray(np.arange(NT * P, dtype=np.int32).reshape(NT, P).T),
        w_gate_up=experts_in(np.concatenate([i["w_expert_gate"][0], i["w_expert_up"][0]], axis=2)),
        w_down=experts_in(i["w_expert_down"][0]),
        shift0=cols(i["state_shift"][0, 0]), wkv0=wkv0,
        past_lat=i["cache_kv_latent"][0, 0], past_kpe=i["cache_k_rope"][0, 0],
    )


OUTPUTS = dict(out=(NT, P, D), shift=(2, P, ZT), wkv=(2, P, PAIRS, P), lat=(NT, P, KL), kpe=(NT, P, ROPE))
SCRATCH = dict(x2_d=(NT, P, D), h2_d=(NT, P, D), y_d=(NE + OVERFLOW, P, D), oa_d=(NT, P, H, VD), ob_d=(NT, P, H, RH), hT_d=(NT + 1, P, DC, P), v_d=(NT + 1, P, H, VD), qT_d=(NT + 1, QK, H, P), kT_d=(NT + 1, QK, H, P))


def kernel(**inputs):
    import numpy as np
    import concourse.bacc as bacc
    from concourse.bass_utils import run_bass_kernel_spmd as run

    nc = bacc.Bacc("TRN2", target_bir_lowering=False, num_devices=1)
    arrays = lay_out(inputs)
    io = {n: nc.dram_tensor(n, a.shape, mybir.dt.from_np(a.dtype), kind="ExternalInput").ap() for n, a in arrays.items()}
    for n, s in OUTPUTS.items():
        io[n] = nc.dram_tensor(n, s, F32, kind="ExternalOutput").ap()
    for n, s in SCRATCH.items():
        io[n] = nc.dram_tensor(n, s, F32, kind="Internal").ap()
    io["table_d"] = nc.dram_tensor("table_d", (P * (NE + OVERFLOW + 2), 1), I32, kind="Internal").ap()
    layer(nc, io)
    got = run(nc, [arrays], core_ids=[0]).results[0]
    rows = {n: np.asarray(got[n]).reshape(NT * P, -1) for n in ("out", "lat", "kpe")}
    prompt, sample = slice(0, SEQ), slice(SEQ, SEQ + DEC)

    def state(g):
        s = np.asarray(got["wkv"])[g]
        heads = [s[RH * (h % 2):RH * (h % 2) + RH, h // 2, RH * (h % 2):RH * (h % 2) + RH].T for h in range(H)]
        return np.ascontiguousarray(np.stack(heads)[None, None])

    shift = lambda g: np.ascontiguousarray(np.asarray(got["shift"])[g].T).reshape(1, 1, 1, ZC)
    out = []
    for g, part in enumerate((prompt, sample)):
        out.append((rows["lat"][part][None, None], rows["kpe"][part][None, None], state(g), shift(g)))
    return (rows["out"][prompt][None], rows["out"][sample][None], *out[0], *out[1])
```
